# Optimizing a Trainium2 kernel written in Bass

```python
import jax, jax.numpy as jnp
from jax import lax
import numpy as np

D_MODEL = 1024
BATCH = 1
SEQ = 512
DEPTH = 1

HEAD_DIM = 64
GRID_W = 64
NA_HEADS = 8
NA_WIN_ROWS = 8
NA_WIN_COLS = 16
DIL_GROUPS = ((128, 1), (512, 4), (2048, 16))
DIL_HEADS_PER_GROUP = 4
N_DIL_GROUPS = len(DIL_GROUPS)
NA_WIDTH = NA_HEADS * HEAD_DIM
DIL_WIDTH = N_DIL_GROUPS * DIL_HEADS_PER_GROUP * HEAD_DIM
DIL_OUT_WIDTH = DIL_HEADS_PER_GROUP * HEAD_DIM
N_BRANCHES = 2
IN_COLS = 3 * (NA_WIDTH + DIL_WIDTH) + N_BRANCHES * D_MODEL
N_EXPERTS = 64
TOP_K = 8
N_EXPERT_GROUPS = 8
TOP_GROUPS = 4
EXPERT_DIM = 256
ROUTED_SCALE = 2.5
EXPERT_BLOCK = 256
ALIBI_MAX = 8.0
EPS = 1e-6
NEG_INF = -1e30

kernel_name = 'hybrid_natten_dilated_moe_encoder'

def rmsnorm(x, g):
    xf = x.astype(jnp.float32)
    xf = xf * lax.rsqrt(jnp.mean(xf * xf, axis=-1, keepdims=True) + EPS)
    return (xf * g.astype(jnp.float32)).astype(x.dtype)

def swiglu(x, wg, wu, wd):
    return (jax.nn.silu(x @ wg) * (x @ wu)) @ wd

def alibi_slopes(n):
    return jnp.exp2(-ALIBI_MAX * jnp.arange(1, n + 1, dtype=jnp.float32) / n)

def neighbourhood_attention(q, k, v, rpb):
    B, H, S, hd = q.shape
    rows = S // GRID_W
    kr = min(NA_WIN_ROWS, rows)
    qg = q.reshape(B, H, rows, GRID_W, hd)
    kg = k.reshape(B, H, rows, GRID_W, hd)
    vg = v.reshape(B, H, rows, GRID_W, hd)
    cols = jnp.arange(GRID_W)
    col_start = jnp.clip(cols - NA_WIN_COLS // 2, 0, GRID_W - NA_WIN_COLS)
    col_mask = (cols[None, :] >= col_start[:, None]) & (cols[None, :] < col_start[:, None] + NA_WIN_COLS)
    dc = jnp.clip(cols[None, :] - cols[:, None], -(NA_WIN_COLS - 1), NA_WIN_COLS - 1) + NA_WIN_COLS - 1
    rpb_cols = rpb[:, :, dc].astype(jnp.float32)
    scale = hd ** -0.5

    def row_step(r):
        rs = jnp.clip(r - kr // 2, 0, rows - kr)
        q_r = lax.dynamic_index_in_dim(qg, r, axis=2, keepdims=False)
        k_w = lax.dynamic_slice_in_dim(kg, rs, kr, axis=2)
        v_w = lax.dynamic_slice_in_dim(vg, rs, kr, axis=2)
        dr = rs + jnp.arange(kr) - r + NA_WIN_ROWS - 1
        bias = jnp.take(rpb_cols, dr, axis=1).transpose(0, 2, 1, 3)
        s = jnp.einsum('bhcd,bhwkd->bhcwk', q_r, k_w).astype(jnp.float32) * scale + bias
        s = jnp.where(col_mask[:, None, :], s, NEG_INF)
        p = jax.nn.softmax(s.reshape(B, H, GRID_W, kr * GRID_W), axis=-1)
        p = p.reshape(B, H, GRID_W, kr, GRID_W).astype(v.dtype)
        return jnp.einsum('bhcwk,bhwkd->bhcd', p, v_w)

    out = lax.map(row_step, jnp.arange(rows))
    return out.transpose(1, 2, 0, 3, 4).reshape(B, H, S, hd)

def dilated_window_attention(q, k, v, window, dilation, slopes):
    B, H, S, hd = q.shape
    radius = window // (2 * dilation)
    blk = radius
    L = S // dilation
    nb = -(-L // blk)
    Lp = nb * blk

    def to_residue(a):
        return a.reshape(B, H, L, dilation, hd).transpose(0, 1, 3, 2, 4)

    qr = jnp.pad(to_residue(q), ((0, 0), (0, 0), (0, 0), (0, Lp - L), (0, 0)))
    kpad = jnp.pad(to_residue(k), ((0, 0), (0, 0), (0, 0), (blk, Lp - L + blk), (0, 0)))
    vpad = jnp.pad(to_residue(v), ((0, 0), (0, 0), (0, 0), (blk, Lp - L + blk), (0, 0)))
    qb = qr.reshape(B, H, dilation, nb, blk, hd)

    def band(a):
        ab = a.reshape(B, H, dilation, nb + 2, blk, hd)
        return jnp.concatenate([ab[:, :, :, :-2], ab[:, :, :, 1:-1], ab[:, :, :, 2:]], axis=4)

    kw, vw = band(kpad), band(vpad)
    qi = jnp.arange(blk)
    kj = jnp.arange(3 * blk)
    rel = kj[None, :] - blk - qi[:, None]
    key_pos = jnp.arange(nb)[:, None] * blk - blk + kj[None, :]
    valid = (jnp.abs(rel) <= radius)[None] & ((key_pos >= 0) & (key_pos < L))[:, None, :]
    dist = (dilation * jnp.abs(rel)).astype(jnp.float32)
    s = jnp.einsum('bhrnqd,bhrnkd->bhrnqk', qb, kw).astype(jnp.float32) * (hd ** -0.5)
    s = s - slopes.astype(jnp.float32)[None, :, None, None, None, None] * dist
    s = jnp.where(valid, s, NEG_INF)
    m = jnp.max(s, axis=-1, keepdims=True)
    p = jnp.exp(s - m)
    z = jnp.sum(p, axis=-1)
    o = jnp.einsum('bhrnqk,bhrnkd->bhrnqd', p.astype(v.dtype), vw).astype(jnp.float32) / z[..., None]
    lse = m[..., 0] + jnp.log(z)
    o = o.reshape(B, H, dilation, Lp, hd)[:, :, :, :L].transpose(0, 1, 3, 2, 4).reshape(B, H, S, hd)
    lse = lse.reshape(B, H, dilation, Lp)[..., :L].transpose(0, 1, 3, 2).reshape(B, H, S)
    return o.astype(q.dtype), lse

def token_mixer(h, w_in, b_gate, rpb, w_pa, w_pb, w_o, slopes):
    B, S, _ = h.shape
    proj = h @ w_in
    na_end = 3 * NA_WIDTH
    dil_end = na_end + 3 * DIL_WIDTH
    qkv_a = proj[..., :na_end].reshape(B, S, 3, NA_HEADS, HEAD_DIM).transpose(2, 0, 3, 1, 4)
    o_a = neighbourhood_attention(qkv_a[0], qkv_a[1], qkv_a[2], rpb)
    qkv_b = proj[..., na_end:dil_end].reshape(B, S, 3, N_DIL_GROUPS, DIL_HEADS_PER_GROUP, HEAD_DIM)
    qkv_b = qkv_b.transpose(2, 3, 0, 4, 1, 5)
    outs, lses = [], []
    for g, (window, dilation) in enumerate(DIL_GROUPS):
        o_g, lse_g = dilated_window_attention(qkv_b[0, g], qkv_b[1, g], qkv_b[2, g], window, dilation, slopes[g])
        outs.append(o_g)
        lses.append(lse_g)
    o_stack = jnp.stack(outs).astype(jnp.float32)
    w_den = jax.nn.softmax(jnp.stack(lses), axis=0)
    o_b = jnp.sum(w_den[..., None] * o_stack, axis=0).astype(h.dtype)
    gates = jax.nn.sigmoid((proj[..., dil_end:] + b_gate).astype(jnp.float32)).astype(h.dtype)
    g_a, g_b = jnp.split(gates, N_BRANCHES, axis=-1)
    y_a = o_a.transpose(0, 2, 1, 3).reshape(B, S, NA_WIDTH) @ w_pa
    y_b = o_b.transpose(0, 2, 1, 3).reshape(B, S, DIL_OUT_WIDTH) @ w_pb
    return (g_a * y_a + g_b * y_b) @ w_o

def route(h, w_router, e_bias):
    N = h.shape[0]
    scores = jax.nn.sigmoid((h @ w_router).astype(jnp.float32))
    biased = scores + e_bias.astype(jnp.float32)
    per_group = N_EXPERTS // N_EXPERT_GROUPS
    grp_score = lax.top_k(biased.reshape(N, N_EXPERT_GROUPS, per_group), 2)[0].sum(-1)
    _, top_grp = lax.top_k(grp_score, TOP_GROUPS)
    grp_mask = jnp.any(top_grp[:, :, None] == jnp.arange(N_EXPERT_GROUPS)[None, None, :], axis=1)
    expert_mask = jnp.repeat(grp_mask, per_group, axis=1)
    _, eidx = lax.top_k(jnp.where(expert_mask, biased, NEG_INF), TOP_K)
    w = jnp.take_along_axis(scores, eidx, axis=1)
    w = w / jnp.sum(w, axis=-1, keepdims=True) * ROUTED_SCALE
    return eidx, w

def routed_experts(h, eidx, ew, we_gate, we_up, we_down):
    N, D = h.shape
    NK = N * TOP_K
    flat_e = eidx.reshape(NK)
    flat_tok = jnp.arange(NK, dtype=jnp.int32) // TOP_K
    flat_w = ew.reshape(NK).astype(h.dtype)
    order = jnp.argsort(flat_e)
    e_sorted = flat_e[order]
    counts = jnp.bincount(flat_e, length=N_EXPERTS)
    starts = jnp.cumsum(counts) - counts
    padded = (counts + EXPERT_BLOCK - 1) // EXPERT_BLOCK * EXPERT_BLOCK
    pad_ends = jnp.cumsum(padded)
    pad_starts = pad_ends - padded
    dest = pad_starts[e_sorted] + jnp.arange(NK) - starts[e_sorted]
    n_blocks = -(-(NK + N_EXPERTS * (EXPERT_BLOCK - 1)) // EXPERT_BLOCK)
    P = n_blocks * EXPERT_BLOCK
    row_tok = jnp.zeros((P,), jnp.int32).at[dest].set(flat_tok[order])
    row_w = jnp.zeros((P,), h.dtype).at[dest].set(flat_w[order])
    block_e = jnp.minimum(jnp.searchsorted(pad_ends, jnp.arange(n_blocks) * EXPERT_BLOCK, side='right'),
                          N_EXPERTS - 1)

    def step(acc, blk):
        tok, wts, e = blk
        y = swiglu(h[tok], we_gate[e], we_up[e], we_down[e]) * wts[:, None]
        return acc.at[tok].add(y), None

    acc, _ = lax.scan(step, jnp.zeros_like(h),
                      (row_tok.reshape(n_blocks, EXPERT_BLOCK), row_w.reshape(n_blocks, EXPERT_BLOCK), block_e))
    return acc

def moe_ffn(h, w_router, e_bias, we_gate, we_up, we_down, ws_gate, ws_up, ws_down):
    eidx, ew = route(h, w_router, e_bias)
    return swiglu(h, ws_gate, ws_up, ws_down) + routed_experts(h, eidx, ew, we_gate, we_up, we_down)

def setup_inputs(seed: int = 0) -> dict:
    key = jax.random.key(seed)
    ks = jax.random.split(key, 24)
    D = D_MODEL
    F = EXPERT_DIM
    f32 = jnp.float32

    def nrm(k, shape, fan_in, gain=1.0):
        return jax.random.normal(k, shape, f32) * (gain * fan_in ** -0.5)

    def small(k, shape, s):
        return jax.random.normal(k, shape, f32) * s

    return {
        'x': jax.random.normal(ks[0], (BATCH, SEQ, D), f32),
        'c': jax.random.normal(ks[1], (BATCH, D), f32),
        'w_ada': nrm(ks[2], (DEPTH, D, 6 * D), D, 0.5),
        'b_ada': small(ks[3], (DEPTH, 6 * D), 0.02),
        'g_mix': 1.0 + small(ks[4], (DEPTH, D), 0.05),
        'w_in': nrm(ks[5], (DEPTH, D, IN_COLS), D),
        'b_gate': small(ks[6], (DEPTH, N_BRANCHES * D), 0.02),
        'rpb': small(ks[7], (DEPTH, NA_HEADS, 2 * NA_WIN_ROWS - 1, 2 * NA_WIN_COLS - 1), 0.05),
        'w_pa': nrm(ks[8], (DEPTH, NA_WIDTH, D), NA_WIDTH),
        'w_pb': nrm(ks[9], (DEPTH, DIL_OUT_WIDTH, D), DIL_OUT_WIDTH),
        'w_o': nrm(ks[10], (DEPTH, D, D), D),
        'g_ffn': 1.0 + small(ks[11], (DEPTH, D), 0.05),
        'w_router': nrm(ks[12], (DEPTH, D, N_EXPERTS), D),
        'e_bias': small(ks[13], (DEPTH, N_EXPERTS), 0.01),
        'we_gate': nrm(ks[14], (DEPTH, N_EXPERTS, D, F), D),
        'we_up': nrm(ks[15], (DEPTH, N_EXPERTS, D, F), D),
        'we_down': nrm(ks[16], (DEPTH, N_EXPERTS, F, D), F),
        'ws_gate': nrm(ks[17], (DEPTH, D, F), D),
        'ws_up': nrm(ks[18], (DEPTH, D, F), D),
        'ws_down': nrm(ks[19], (DEPTH, F, D), F),
        'g_final': 1.0 + small(ks[20], (D,), 0.05),
    }

def reference(x, c, w_ada, b_ada, g_mix, w_in, b_gate, rpb, w_pa, w_pb, w_o, g_ffn, w_router, e_bias,
              we_gate, we_up, we_down, ws_gate, ws_up, ws_down, g_final):
    B, S, D = x.shape
    slopes = alibi_slopes(N_DIL_GROUPS * DIL_HEADS_PER_GROUP).reshape(N_DIL_GROUPS, DIL_HEADS_PER_GROUP)
    c_act = jax.nn.silu(c)
    for l in range(DEPTH):
        mod = c_act @ w_ada[l] + b_ada[l]
        sh1, sc1, gt1, sh2, sc2, gt2 = [m[:, None, :] for m in jnp.split(mod, 6, axis=-1)]
        h = rmsnorm(x, g_mix[l]) * (1.0 + sc1) + sh1
        x = x + gt1 * token_mixer(h, w_in[l], b_gate[l], rpb[l], w_pa[l], w_pb[l], w_o[l], slopes)
        h = rmsnorm(x, g_ffn[l]) * (1.0 + sc2) + sh2
        y = moe_ffn(h.reshape(B * S, D), w_router[l], e_bias[l], we_gate[l], we_up[l], we_down[l],
                    ws_gate[l], ws_up[l], ws_down[l])
        x = x + gt2 * y.reshape(B, S, D)
    return rmsnorm(x, g_final)


_drawn_inputs = setup_inputs


def setup_inputs(seed=0):
    import zlib

    import numpy as np

    out = dict(_drawn_inputs(seed))
    spreads = {}
    factors = {'g_mix': 3.042, 'b_gate': 7.776, 'rpb': 8.0}
    for name, (base, spread) in spreads.items():
        noise = np.random.default_rng([zlib.crc32(name.encode()), seed]).standard_normal(out[name].shape)
        drawn = base * np.exp(spread * noise) if base else spread * noise
        out[name] = __import__('jax').numpy.asarray(drawn.astype(out[name].dtype))
    for name, factor in factors.items():
        out[name] = (out[name] * factor).astype(out[name].dtype)
    return out
```

```python
from contextlib import ExitStack

import concourse.bass as bass
from concourse import mybir

F32 = mybir.dt.float32
BF16 = mybir.dt.bfloat16
I32 = mybir.dt.int32
U32 = mybir.dt.uint32
ALU = mybir.AluOpType
ACT = mybir.ActivationFunctionType
AX = mybir.AxisListType

P = 128
D = 1024
S = 512
NT = S // P
KD = D // P
HD = 64
GRID = 64
ROWS = S // GRID
NAH, WR, WC = 8, 8, 16
NG, GH = 3, 4
RADIUS = 64
DIL = (1, 4, 16)
NE, TOPK, NGRP, TOPG, FE = 64, 8, 8, 4, 256
ROUTED = 2.5
EPS = 1e-6
BIG = 1e30
SCALE = HD ** -0.5
SLOPES = [2.0 ** (-8.0 * (i + 1) / (NG * GH)) for i in range(NG * GH)]
RPBH = (2 * WR - 1) * (2 * WC - 1)
RPBW = 2 * WC - 1
BT = (NAH - 1) * RPBH + (ROWS - 1) * RPBW + 48
RPAD = WC
CW = 256

DIL0 = 3 * NAH * HD
GATE0 = DIL0 + 3 * NG * GH * HD
CHUNKS = ([0, 256, 512, 768] + [DIL0 + CW * i for i in range(6)] + [1024, 1280]
          + [DIL0 + 1536 + CW * i for i in range(3)] + [GATE0 + CW * i for i in range(8)])
N_QK, N_V, N_GATE = 10, 5, 8
QK_UNITS, V_UNITS, GATE_UNITS = 2 * N_QK, 2 * N_V, 2 * N_GATE
VSTAGE = 4
UNITS = QK_UNITS + V_UNITS
WSLOTS = 3
ADA_CHUNKS = 2 * KD

NEAR = [[0, 1], [0, 1, 2], [1, 2, 3], [2, 3]]


def jobs():
    out = [("group", g, h, None) for g in (2, 1) for h in range(GH)]
    out += [("band", 0, h, t) for h in range(GH) for t in range(NT)]
    out += [("na", 0, h, t) for h in range(NAH) for t in range(NT)]
    return out


JOBS = jobs()
HEAD_OF = []
BIAS_OF = []
_h = _b = -1
for _kind, _g, _hh, _t in JOBS:
    if _t in (None, 0):
        _h += 1
    if _kind != "band" or _t == 0:
        _b += 1
    HEAD_OF.append(_h)
    BIAS_OF.append(_b)
N_HEADS, N_BIAS = _h + 1, _b + 1


def last_of(table, value):
    return max(i for i, x in enumerate(table) if x == value)


A_QKT, A_V, A_HT, A_W, A_BT, A_JOB, A_GATE, A_O = 0, 10240, 15360, 19456, 25600, 29120, 33344, 41536
A_END = 46752
B_WPA, B_OAT, B_OGN, B_TMP, B_WO, B_X = 0, 6144, 10240, 12352, 19456, 27648
SLOT = [0, 12288, 18432, 6144]
SLOT_WORDS = 6144
C_XS, C_H2T, C_YSH, C_WR = 33344, 37440, 41536, 45632
C_Y, C_OH, C_AT, C_ACT, C_XG, C_HTS = 24576, 26624, 27136, 31744, 33344, 35392
XT_BANK = [2, 3, 4, 5, 6, 7, 1, 0]
BT_UNIT = 4
AHEAD = 4
FILL = 2


def build(nc, x, c, w_ada, b_ada, g_mix, w_in, b_gate, rpb, w_pa, w_pb, w_o, g_ffn, w_router, e_bias,
          we_gate, we_up, we_down, ws_gate, ws_up, ws_down, g_final, out):
    rpb_pad = nc.dram_tensor("rpb_pad", [2 * RPAD + NAH * RPBH], F32, kind="Internal").ap()
    dil_dram = nc.dram_tensor("dil_dram", [2, S, 264], F32, kind="Internal").ap()
    xn_dram = nc.dram_tensor("xn_dram", [S, D], F32, kind="Internal").ap()
    pair_dram = nc.dram_tensor("pair_dram", [S * TOPK, D], F32, kind="Internal").ap()

    with ExitStack() as ctx:
        def sb(name, shape, dt=F32):
            return ctx.enter_context(nc.sbuf_tensor(name, shape, dt))

        def sem(name):
            return ctx.enter_context(nc.semaphore(name))

        arena = sb("arena", [P, A_END])

        def at(off, n):
            return arena[:, off:off + n]

        ada_first = [at(2048 * k, 2048) for k in range(7)] + [at(A_GATE + 4096, 2048)]
        ada_ring = [at(A_GATE + 4096, 2048), at(A_GATE + 6144, 2048)]
        x_first = at(A_GATE, 4096).rearrange("p (n d) -> p n d", n=NT)
        acc = at(A_JOB, 2048)
        bt_rev = at(A_O, BT)
        qkt = at(A_QKT, 10240).rearrange("p (m t) -> p m t", m=20)
        vbuf = at(A_V, 5120).rearrange("p (n f) -> p n f", n=NT)
        hT = at(A_HT, 4096).rearrange("p (k t) -> p k t", k=KD)
        vT = [at(A_GATE + 512 * i, 512) for i in range(VSTAGE)]
        wbuf = [at(A_W + 2048 * i, 2048).rearrange("p (k f) -> p k f", k=KD) for i in range(WSLOTS)]
        bt8 = at(A_BT, BT)
        bias = [at(A_JOB + 384 * i, 384) for i in range(3)]
        sneg = [at(A_JOB + 1152 + 512 * i, 512) for i in range(2)]
        prob = [at(A_JOB + 2176 + 512 * i, 512) for i in range(2)]
        pT = [at(A_JOB + 3200 + 512 * i, 512) for i in range(2)]
        gates = at(A_GATE, 8192).rearrange("p (m t) -> p m t", m=16)
        o_na = at(A_O, 2048).rearrange("p (n f) -> p n f", n=NT)
        og = [at(A_O + 2048 + 1056 * g, 1056).rearrange("p (n f) -> p n f", n=NT) for g in range(NG)]
        wpa = at(B_WPA, 4096).rearrange("p (k f) -> p k f", k=4)
        wpb = at(B_WPA + 4096, 2048).rearrange("p (k f) -> p k f", k=2)
        oaT = at(B_OAT, 2048).rearrange("p (k t) -> p k t", k=4)
        obT = at(B_OAT + 2048, 1024).rearrange("p (k t) -> p k t", k=2)
        ogn = [og[0]] + [at(B_OGN + 1056 * i, 1056).rearrange("p (n f) -> p n f", n=NT) for i in range(2)]
        prod = [at(B_TMP + 1024 * i, 1024).rearrange("p (n f) -> p n f", n=NT) for i in range(2)]
        merged = at(A_HT, 4096).rearrange("p (k t) -> p k t", k=KD)
        wo = at(B_WO, 8192).rearrange("p (k f) -> p k f", k=KD)
        x2 = at(B_X, 4096).rearrange("p (n d) -> p n d", n=NT)
        xs = at(C_XS, 4096).rearrange("p (n d) -> p n d", n=NT)
        ytmp = [at(B_OGN + 512 * i, 512) for i in range(4)]
        h2T = at(C_H2T, 4096).rearrange("p (k t) -> p k t", k=KD)
        ysh = at(C_YSH, 4096).rearrange("p (n d) -> p n d", n=NT)
        wgu = [at(SLOT[i], 4096).rearrange("p (a k f) -> p a k f", a=2, k=KD) for i in range(4)]
        wd = [at(SLOT[i] + 4096, 2048).rearrange("p (k f) -> p k f", k=2) for i in range(4)]
        sh_act = at(C_Y, 1024).rearrange("p (m t) -> p m t", m=2)
        sh_tmp = at(C_Y + 1024, 1024).rearrange("p (m t) -> p m t", m=2)
        ysb = [at((C_Y if i < 2 else C_H2T) + 1024 * i, 1024) for i in range(4)]
        onehot = [at(C_OH + 256 * i, 256).bitcast(BF16).rearrange("p (n s) -> p n s", n=NT) for i in range(2)]
        aT = [at(C_AT + 256 * i, 256).rearrange("p (k s) -> p k s", k=2) for i in range(2)]
        th = [at(C_ACT + 768 * i, 256) for i in range(2)]
        gth = [at(C_ACT + 768 * i + 256, 256) for i in range(2)]
        act_t = [at(C_ACT + 768 * i + 512, 256) for i in range(2)]
        xg = [at(C_XG + 1024 * i if i < 2 else C_H2T + 1024 * (i - 2), 1024) for i in range(4)]
        hTs = [at(C_HTS + 1024 * i, 1024).rearrange("p (k s) -> p k s", k=KD) for i in range(2)]
        pairs = [at(8192 * i, 8192).rearrange("p (q d) -> p q d", q=TOPK) for i in range(2)]
        fin = at(C_XG, 4096).rearrange("p (n d) -> p n d", n=NT)

        gt1 = sb("gt1", [P, D])
        gt2 = sb("gt2", [P, D])
        gfin = gt1
        ident = sb("ident", [P, P])
        flip = sb("flip", [P, P])
        ones = sb("ones", [P, P])
        zero16 = sb("zero16", [1, RPAD])
        c_col = sb("c_col", [P, KD])
        c_th = sb("c_th", [P, KD])
        c_act = sb("c_act", [P, KD])
        bada = sb("bada", [P, 6, KD])
        gmix = sb("gmix", [P, KD])
        gffn = sb("gffn", [P, KD])
        modc = sb("modc", [P, 6, KD])
        a1 = sb("a1", [P, KD])
        a2 = sb("a2", [P, KD])
        bg_rows = sb("bg_rows", [16, P])
        bg_half = sb("bg_half", [P, 16])
        ss = sb("ss", [P, NT])
        rs = sb("rs", [P, NT])
        var = sb("var", [P, NT])
        rt = sb("rt", [P, NT])
        nm_na = sb("nm_na", [P, NAH, NT])
        z_na = sb("z_na", [P, NAH, NT])
        rz_na = sb("rz_na", [P, NAH, NT])
        part_i = sb("part_i", [P, 2], I32)
        cl = sb("cl", [P, 2])
        win = sb("win", [P, NT, 2])
        shared = sb("shared", [P, 1152])
        col_i = shared[:, 0:384].bitcast(I32)
        col_f = shared[:, 384:768]
        nmask = sb("nmask", [P, NT, 48])
        mtmp = shared[:, 768:1152]
        dist = [sb(f"dist{g}", [P, 384 if g == 0 else P]) for g in range(NG)]
        lse = sb("lse", [P, 8, NT, GH])
        wr = at(C_WR, 512).rearrange("p (k e) -> p k e", k=KD)
        ebias = sb("ebias", [P, NE])
        score = at(C_ACT, 256).rearrange("p (n e) -> p n e", n=NT)
        biased = at(C_ACT + 256, 256).rearrange("p (n e) -> p n e", n=NT)
        grp8 = at(C_ACT + 512, 256).rearrange("p (n e) -> p n e", e=8)
        grp = sb("grp", [P, NT, NGRP])
        cmp = at(C_ACT + 768, 256).rearrange("p (n g h) -> p n g h", n=NT, g=NGRP)
        cmq = at(C_ACT + 1024, 256).rearrange("p (n g h) -> p n g h", n=NT, g=NGRP)
        before = sb("before", [P, NGRP, NGRP])
        gsel = sb("gsel", [P, NT, NGRP])
        gpen = sb("gpen", [P, NT, NGRP])
        top8 = sb("top8", [P, NT, 8])
        sel = at(C_OH, 256).rearrange("p (n e) -> p n e", n=NT)
        selb = at(C_AT, 128).bitcast(BF16).rearrange("p (n e) -> p n e", n=NT)
        wt = at(C_ACT + 1280, 256).rearrange("p (n e) -> p n e", n=NT)
        wsum = sb("wsum", [P, NT])
        kth = at(C_OH + 256, 256).rearrange("p (n e) -> p n e", n=NT)
        posm = sb("posm", [P, NT, NE])
        rhs9 = shared[:, :].bitcast(BF16).rearrange("p (n e c a) -> p n e c a", n=NT, e=NE, c=3)
        tri = sb("tri", [P, P], BF16)
        onesb = sb("onesb", [P, P], BF16)
        slot_id = at(C_WR + 512, 512).rearrange("p (b s) -> p b s", b=4)
        info = sb("info", [P, NE + 1, 3])
        idx_t = sb("idx_t", [P, 4, 1], U32)
        idx_r = sb("idx_r", [P, 4, 1], U32)
        cnt_e = sb("cnt_e", [NE, 1])
        eval_ = sb("eval_", [NE, 4])
        ovf = sb("ovf", [NE, 3])
        ovfb = sb("ovfb", [NE, 3], BF16)
        ovr = sb("ovr", [NE, 3])
        ov1h = sb("ov1h", [NE, 3, 32])
        ovlist = sb("ovlist", [1, 96], U32)

        bank = [ctx.enter_context(nc.psum_tensor(f"bank{i}", [P, 512], F32)) for i in range(8)]
        ps_proj, ps_s, ps_t, ps_o = bank[0:2], bank[2:4], bank[4:6], bank[6:8]

        s_small = sem("s_small")
        s_rows = sem("s_rows")
        s_bg = sem("s_bg")
        s_x = sem("s_x")
        s_ada0 = [sem(f"s_ada0_{k}") for k in range(KD)]
        s_adar = [sem(f"s_adar_{k}") for k in range(2)]
        s_pad = sem("s_pad")
        s_btr = sem("s_btr")
        s_w = [sem(f"s_w_{i}") for i in range(WSLOTS)]
        s_dil = sem("s_dil")
        s_ogn = sem("s_ogn")
        s_wp = sem("s_wp")
        s_wo = sem("s_wo")
        s_xr = sem("s_xr")
        s_wsh = sem("s_wsh")
        s_wr = sem("s_wr")
        s_gfin = sem("s_gfin")
        s_wgu = [sem(f"s_wgu_{i}") for i in range(4)]
        s_wd = [sem(f"s_wd_{i}") for i in range(4)]
        s_xn = sem("s_xn")
        s_gather = [sem(f"s_gather_{i}") for i in range(4)]
        s_scatter = [sem(f"s_scatter_{i}") for i in range(4)]
        s_pair = [sem(f"s_pair_{i}") for i in range(2)]
        s_out = sem("s_out")
        pool_c = sem("pool_c")
        pool_seq = sem("pool_seq")
        pool_bias = sem("pool_bias")
        dve_c = sem("dve_c")
        act_c = sem("act_c")
        dve_one = sem("dve_one")
        dve_tab = sem("dve_tab")
        dve_ada = sem("dve_ada")
        dve_rs = sem("dve_rs")
        dve_var = sem("dve_var")
        act_ss = sem("act_ss")
        act_sd = sem("act_sd")
        act_cth = sem("act_cth")
        act_xs = sem("act_xs")
        dve_mod = sem("dve_mod")
        act_bt = sem("act_bt")
        pe_bt = sem("pe_bt")
        pe_mod = sem("pe_mod")
        pe_xT = sem("pe_xT")
        act_hT = sem("act_hT")
        dve_hT = sem("dve_hT")
        pe_unit = sem("pe_unit")
        act_ev = sem("act_ev")
        dve_ev = sem("dve_ev")
        act_gate = sem("act_gate")
        pe_vT = sem("pe_vT")
        act_vout = sem("act_vout")
        dve_vout = sem("dve_vout")
        pe_s = sem("pe_s")
        dve_ttr = sem("dve_ttr")
        act_exp = sem("act_exp")
        pe_t = sem("pe_t")
        dve_pt = sem("dve_pt")
        pe_pv = sem("pe_pv")
        dve_o = sem("dve_o")
        act_lse = sem("act_lse")
        dve_lse = sem("dve_lse")
        dve_ob = sem("dve_ob")
        pe_oT = sem("pe_oT")
        act_oT = sem("act_oT")
        dve_oT = sem("dve_oT")
        pe_y = sem("pe_y")
        dve_m = sem("dve_m")
        pe_wo = sem("pe_wo")
        dve_u = sem("dve_u")
        pe_h2 = sem("pe_h2")
        act_h2 = sem("act_h2")
        dve_h2 = sem("dve_h2")
        pe_rt = sem("pe_rt")
        act_rt = sem("act_rt")
        dve_sel = sem("dve_sel")
        dve_tabs = sem("dve_tabs")
        dve_ovf = sem("dve_ovf")
        dve_list = sem("dve_list")
        pe_sh = sem("pe_sh")
        act_sh = sem("act_sh")
        dve_sh = sem("dve_sh")
        act_ysh = sem("act_ysh")
        dve_ysh = sem("dve_ysh")
        dve_zx = sem("dve_zx")
        dve_oh = sem("dve_oh")
        pe_info = sem("pe_info")
        dve_info = sem("dve_info")
        dve_idx = sem("dve_idx")
        pe_ht = sem("pe_ht")
        act_ht = sem("act_ht")
        dve_ht = sem("dve_ht")
        pe_gu = sem("pe_gu")
        act_th = sem("act_th")
        dve_g = sem("dve_g")
        dve_act = sem("dve_act")
        pe_at = sem("pe_at")
        dve_at = sem("dve_at")
        pe_dn = sem("pe_dn")
        act_y = sem("act_y")
        dve_y = sem("dve_y")
        dve_idr = sem("dve_idr")
        dve_sum = sem("dve_sum")
        act_fss = sem("act_fss")
        act_fsd = sem("act_fsd")
        dve_fv = sem("dve_fv")
        dve_fin = sem("dve_fin")

        block = ctx.enter_context(nc.Block())

        def bview(src, off, dims):
            return bass.AP(tensor=src.tensor, offset=src.offset + off, ap=[list(src.ap[0])] + dims)

        def unit_places(u):
            if u < QK_UNITS:
                dst = qkt[:, u, :]
                g = -1 if u < 8 else (u - 8) % 6 // 2
            else:
                dst = vT[u % VSTAGE]
                g = -1 if u < QK_UNITS + 4 else (u - QK_UNITS - 4) // 2
            if g < 0:
                return dst.rearrange("p (t r c) -> p r t c", t=NT, r=ROWS), \
                    (lambda a: a.rearrange("p (r t c) -> p r t c", t=NT, r=ROWS))
            if g == 0:
                return dst, lambda a: a
            return dst.rearrange("p (r u) -> p u r", r=DIL[g]), lambda a: a.rearrange("p (u r) -> p u r", r=DIL[g])

        xt = x[0].rearrange("(n p) d -> p n d", p=P)
        NJ = len(JOBS)

        @block.sync
        def _(sp):
            def ada_src(part, k):
                return w_ada[0].rearrange("(p k) n -> p k n", k=KD)[:, k, 2048 * part:2048 * (part + 1)]

            sp.dma_start(c_col[:], c.rearrange("a (p k) -> (a p) k", k=KD)).then_inc(s_small, 16)
            sp.dma_start(bada[:], b_ada[0].rearrange("(s p k) -> p s k", s=6, k=KD)).then_inc(s_small, 16)
            sp.dma_start(gmix[:], g_mix[0].rearrange("(p k) -> p k", k=KD)).then_inc(s_small, 16)
            sp.dma_start(gffn[:], g_ffn[0].rearrange("(p k) -> p k", k=KD)).then_inc(s_small, 16)
            sp.dma_start(x_first, xt).then_inc(s_x, 16)
            for k in range(KD):
                sp.dma_start(ada_first[k], ada_src(0, k)).then_inc(s_ada0[k], 16)
            sp.dma_start(bg_rows[:], b_gate[0].rearrange("(m p) -> m p", p=P)).then_inc(s_bg, 16)

            def w_chunk(i):
                if i >= WSLOTS:
                    sp.wait_ge(pe_unit, 2 * (i - WSLOTS + 1))
                src = w_in[0].rearrange("(p k) n -> p k n", k=KD)[:, :, CHUNKS[i]:CHUNKS[i] + CW]
                sp.dma_start(wbuf[i % WSLOTS], src).then_inc(s_w[i % WSLOTS], 16)

            def ada_chunk(j):
                if j != 1:
                    sp.wait_ge(dve_ada, KD if j == 0 else KD + j - 1)
                sp.dma_start(ada_ring[j % 2], ada_src(1 + j // KD, j % KD)).then_inc(s_adar[j % 2], 16)

            for i in range(WSLOTS):
                w_chunk(i)
            ada_chunk(0)
            ada_chunk(1)
            sp.dma_start(gt1[:], b_ada[0, 2 * D:3 * D].partition_broadcast(P)).then_inc(s_rows, 16)
            sp.dma_start(gt2[:], b_ada[0, 5 * D:6 * D].partition_broadcast(P)).then_inc(s_rows, 16)
            sp.dma_start(ebias[:], e_bias[0].partition_broadcast(P)).then_inc(s_rows, 16)
            for i in range(WSLOTS, len(CHUNKS)):
                w_chunk(i)
                for j in range(2 * (i - WSLOTS + 1), min(2 * (i - WSLOTS + 2), ADA_CHUNKS)):
                    ada_chunk(j)
                if i == 18:
                    sp.wait_ge(dve_o, 2 * GH)
                    sp.dma_start(dil_dram[0].rearrange("(p r) f -> p r f", r=4), og[1]).then_inc(s_dil, 16)
                    d2 = dil_dram[1].rearrange("(u t r) f -> r u t f", t=NT, r=4)
                    for r in range(4):
                        sp.dma_start(d2[r], og[2][32 * r:32 * r + 32, :, :]).then_inc(s_dil, 16)
            sp.wait_ge(s_dil, 80)
            sp.wait_ge(pe_pv, NJ)
            for i in range(2):
                sp.dma_start(ogn[1 + i], dil_dram[i].rearrange("(n p) f -> p n f", p=P)).then_inc(s_ogn, 16)
            sp.dma_start(wpa, w_pa[0].rearrange("(k p) f -> p k f", p=P)).then_inc(s_wp, 16)
            sp.dma_start(wpb, w_pb[0].rearrange("(k p) f -> p k f", p=P)).then_inc(s_wp, 16)
            sp.wait_ge(pe_unit, UNITS + GATE_UNITS)
            sp.dma_start(wo, w_o[0].rearrange("(k p) f -> p k f", p=P)).then_inc(s_wo, 16)
            sp.dma_start(x2, xt).then_inc(s_xr, 16)

            def w_expert(e, k, reused):
                gate = we_gate[0, e] if isinstance(e, int) else we_gate[0, bass.ds(e, 1)].rearrange("a d f -> (a d) f")
                up = we_up[0, e] if isinstance(e, int) else we_up[0, bass.ds(e, 1)].rearrange("a d f -> (a d) f")
                down = we_down[0, e] if isinstance(e, int) else we_down[0, bass.ds(e, 1)].rearrange("a d f -> (a d) f")
                if reused:
                    sp.wait_ge(pe_gu, e - 3)
                sp.dma_start(wgu[k][:, 0], gate.rearrange("(p k) f -> p k f", k=KD)).then_inc(s_wgu[k], 16)
                sp.dma_start(wgu[k][:, 1], up.rearrange("(p k) f -> p k f", k=KD)).then_inc(s_wgu[k], 16)
                if reused:
                    sp.wait_ge(pe_dn, e - 3)
                sp.dma_start(wd[k], down.rearrange("(p k) f -> p k f", k=2)).then_inc(s_wd[k], 16)

            sp.wait_ge(dve_ob, 1)
            sp.dma_start(wr, w_router[0].rearrange("(p k) e -> p k e", k=KD)).then_inc(s_wr, 16)
            sp.wait_ge(pe_y, KD)
            sp.wait_ge(dve_m, 3 * KD)
            sp.dma_start(wgu[3][:, 0], ws_gate[0].rearrange("(p k) f -> p k f", k=KD)).then_inc(s_wsh, 16)
            sp.dma_start(wgu[3][:, 1], ws_up[0].rearrange("(p k) f -> p k f", k=KD)).then_inc(s_wsh, 16)
            sp.dma_start(wd[3], ws_down[0].rearrange("(k p) f -> p k f", p=P)).then_inc(s_wsh, 16)
            w_expert(0, 0, False)
            sp.wait_ge(pe_wo, 2 * NT)
            sp.wait_ge(dve_u, 4 * NT)
            sp.dma_start(gfin[:], g_final.partition_broadcast(P)).then_inc(s_gfin, 16)
            w_expert(1, 1, False)
            for n in range(NT):
                sp.wait_ge(act_xs, NT + n + 1)
                sp.dma_start(xn_dram[n * P:(n + 1) * P, :], xs[:, n, :]).then_inc(s_xn, 16)
            w_expert(2, 2, False)
            sp.wait_ge(pe_sh, 4 + 2 * NT)
            w_expert(3, 3, False)
            with sp.Fori(1, NE // 4) as i:
                for k in range(4):
                    w_expert(4 * i + k, k, True)
            sp.wait_ge(dve_list, 1)
            blocks = sp.value_load(ovlist[0:1, 64:65], min_val=0, max_val=31)
            with sp.If(blocks > 0):
                with sp.Fori(0, blocks) as i:
                    e = sp.value_load(ovlist[0:1, bass.ds(i, 1)], min_val=0, max_val=NE - 1)
                    sp.wait_ge(pe_dn, i + NE)
                    w_expert(e, 0, False)
            sp.wait_ge(s_scatter[0], blocks * 16 + NE // 4 * 16)
            for k in range(1, 4):
                sp.wait_ge(s_scatter[k], NE // 4 * 16)
            for n in range(NT):
                if n >= 2:
                    sp.wait_ge(dve_sum, 4 * (n - 2) + 1)
                sp.dma_start(pairs[n % 2], pair_dram[n * P * TOPK:(n + 1) * P * TOPK, :]
                             .rearrange("(p q) d -> p q d", q=TOPK)).then_inc(s_pair[n % 2], 16)
            for n in range(NT):
                sp.wait_ge(dve_fin, n + 1)
                sp.dma_start(out[0, n * P:(n + 1) * P, :], fin[:, n, :]).then_inc(s_out, 16)
            sp.wait_ge(s_out, 16 * NT)

        @block.gpsimd
        def _(pool):
            pool.memset(ident[:], 0.0).then_inc(pool_c, 1)
            pool.memset(flip[:], 0.0).then_inc(pool_c, 1)
            pool.wait_ge(pool_c, 2)
            pool.affine_select(out=ident[:], in_=ident[:], compare_op=ALU.not_equal, fill=1.0, base=0,
                               pattern=[[-1, P]], channel_multiplier=1).then_inc(pool_c, 1)
            pool.affine_select(out=flip[:], in_=flip[:], compare_op=ALU.not_equal, fill=1.0, base=1 - P,
                               pattern=[[1, P]], channel_multiplier=1).then_inc(pool_c, 1)
            pool.iota(part_i[:, 0:1], pattern=[[0, 1]], base=0, channel_multiplier=1).then_inc(pool_c, 1)
            pool.iota(col_i, pattern=[[1, 384]], base=0, channel_multiplier=0).then_inc(pool_c, 1)
            pool.memset(tri[:], 1.0).then_inc(pool_c, 1)
            pool.memset(before[:], 1.0).then_inc(pool_c, 1)
            pool.wait_ge(pool_c, 8)
            pool.affine_select(out=tri[:], in_=tri[:], compare_op=ALU.is_gt, fill=0.0, base=0,
                               pattern=[[1, P]], channel_multiplier=-1).then_inc(pool_c, 1)
            pool.affine_select(out=before[:], in_=before[:], compare_op=ALU.is_gt, fill=0.0, base=0,
                               pattern=[[1, NGRP], [-1, NGRP]], channel_multiplier=0).then_inc(pool_c, 1)
            pool.memset(onesb[:], 1.0).then_inc(pool_c, 1)

            done = -1
            pool.wait_ge(dve_tab, 4)
            pool.wait_ge(act_bt, 7)
            pool.wait_ge(pe_mod, 3)
            for j, (kind, g, h, t) in enumerate(JOBS):
                u = BIAS_OF[j]
                if u == done:
                    continue
                done = u
                if u >= 3:
                    pool.wait_ge(dve_ttr, last_of(BIAS_OF, u - 3) + 1)
                if kind == "na":
                    w = 16 * len(NEAR[t])
                    off = RPAD + 16 * NEAR[t][0] - 16 * t + h * RPBH
                    pool.tensor_tensor(bias[u % 3][:, 0:ROWS * w].rearrange("p (j r c) -> p j r c", r=ROWS, c=16),
                                       bview(bt8, off, [[16, w // 16], [RPBW, ROWS], [1, 16]]),
                                       bview(nmask[:, t, :], 0, [[16, w // 16], [0, ROWS], [1, 16]]),
                                       ALU.add).then_inc(pool_bias, 1)
                else:
                    w = 384 if kind == "band" else P
                    pool.tensor_scalar(bias[u % 3][:, 0:w], dist[g][:, 0:w], -SLOPES[g * GH + h] / SCALE, None,
                                       ALU.mult).then_inc(pool_bias, 1)

            pool.wait_ge(dve_ob, 1)
            pool.iota(slot_id.rearrange("p b s -> p (b s)"), pattern=[[1, 4 * P]], base=0,
                      channel_multiplier=0, allow_small_or_imprecise_dtypes=True).then_inc(pool_c, 1)

            last_token, last_pair = pool.to_reg(S - 1), pool.to_reg(S * TOPK - 1)

            def gather(n, k):
                pool.wait_ge(dve_idx, n + 1)
                pool.sem_inc(pool_seq, 1)
                pool.indirect_dma_start(xg[k], None, xn_dram,
                                        bass.IndirectOffsetOnAxis(ap=idx_t[:, k, :], axis=0),
                                        bounds_check=last_token, oob_is_err=False).then_inc(s_gather[k], 16)

            def scatter(n, k):
                pool.wait_ge(act_y, n + 1)
                pool.wait_ge(dve_y, n + 1)
                pool.sem_inc(pool_seq, 1)
                pool.indirect_dma_start(pair_dram, bass.IndirectOffsetOnAxis(ap=idx_r[:, k, :], axis=0), ysb[k], None,
                                        bounds_check=last_pair, oob_is_err=False).then_inc(s_scatter[k], 16)

            def body(e, k):
                if not isinstance(e, int) or e + AHEAD < NE:
                    gather(e + AHEAD, k)
                scatter(e, k)

            pool.wait_ge(s_xn, 16 * NT)
            pool.wait_ge(dve_zx, 4)
            for e in range(AHEAD):
                gather(e, e)
            for e in range(4):
                body(e, e)
            with pool.Fori(1, NE // 4 - 1) as i:
                for k in range(4):
                    body(4 * i + k, k)
            for e in range(NE - 4, NE):
                body(e, e % 4)
            blocks = pool.value_load(ovlist[0:1, 64:65], min_val=0, max_val=31)
            with pool.If(blocks > 0):
                with pool.Fori(0, blocks) as i:
                    gather(NE + i, 0)
                    scatter(NE + i, 0)

        @block.scalar
        def _(act):
            act.wait_ge(dve_one, 2)
            act.dma_start(rpb_pad[0:RPAD], zero16[0, :]).then_inc(s_pad, 16)
            act.dma_start(rpb_pad[RPAD + NAH * RPBH:], zero16[0, :]).then_inc(s_pad, 16)
            act.dma_start(rpb_pad[RPAD:RPAD + NAH * RPBH], rpb[0].rearrange("h a b -> (h a b)")).then_inc(s_pad, 16)
            act.wait_ge(s_pad, 48)
            for r in range(ROWS):
                act.dma_start(bt_rev[16 * r:16 * r + 16, :],
                              bass.AP(tensor=rpb_pad.tensor, offset=rpb_pad.offset + RPBW * r,
                                      ap=[[1, 16], [1, BT]])).then_inc(s_btr, 16)
            act.wait_ge(s_small, 64)
            act.activation(c_th[:], c_col[:], ACT.Tanh, scale=0.5).then_inc(act_cth, 1)

            def sum_squares(src, junk, n, done):
                act.activation(junk, src, ACT.Square, accum_out=ss[:, n:n + 1]).then_inc(done, 1)

            act.wait_ge(s_x, 16)
            for n in range(NT):
                sum_squares(x_first[:, n, :], at(A_HT + 1024 * n, 1024), n, act_ss)
            act.wait_ge(dve_var, 1)
            act.activation(rt[:], var[:], ACT.Sqrt).then_inc(act_sd, 1)
            act.wait_ge(dve_rs, 1)
            for n in range(NT):
                act.activation(x_first[:, n, :], x_first[:, n, :], ACT.Copy,
                               scale=rs[:, n:n + 1]).then_inc(act_xs, 1)
            act.wait_ge(dve_mod, 1)
            for k in range(0, KD, 2):
                act.wait_ge(pe_xT, k + 1)
                act.activation(hT[:, k, :], bank[XT_BANK[k]][:, :], ACT.Identity, bias=modc[:, 0, k:k + 1],
                               scale=a1[:, k:k + 1]).then_inc(act_hT, 1)

            def unit_out(u):
                act.wait_ge(pe_unit, u + 1)
                if u >= QK_UNITS + VSTAGE:
                    act.wait_ge(pe_vT, u - QK_UNITS - VSTAGE + 1)
                dst, of = unit_places(u)
                act.copy(dst, of(ps_proj[0][:, :])).then_inc(act_ev, 1)

            def v_out(f):
                act.wait_ge(pe_vT, f + 1)
                act.copy(vbuf[:, :, P * f:P * f + P],
                         bank[2 + f % 2][:, :].rearrange("p (n f) -> p n f", n=NT)).then_inc(act_vout, 1)

            for u in range(0, UNITS, 2):
                unit_out(u)
                if u == BT_UNIT:
                    for i in range(7):
                        act.wait_ge(pe_bt, i + 1)
                        w = min(512, BT - 512 * i)
                        act.activation(bt8[:, 512 * i:512 * i + w], bank[2 + i % 6][:, 0:w], ACT.Copy,
                                       scale=1.0 / SCALE).then_inc(act_bt, 1)
                if u >= QK_UNITS + 2:
                    v_out(u - QK_UNITS - 2)
            v_out(V_UNITS - 2)

            def gate_out(m):
                act.wait_ge(pe_unit, UNITS + m + 1)
                if m == 0:
                    act.wait_ge(dve_mod, 3)
                act.activation(gates[:, m, :], ps_proj[m % 2][:, :], ACT.Tanh, bias=bg_half[:, m:m + 1],
                               scale=0.5).then_inc(act_gate, 1)

            gate = 0
            for i, (kind, g, h, t) in enumerate(JOBS):
                act.wait_ge(dve_ttr, i + 1)
                if i >= 2:
                    act.wait_ge(pe_t, i - 1)
                if kind == "group":
                    for q in range(NT):
                        w = slice(P * q, P * q + P)
                        ins = act.activation(prob[i % 2][:, w], sneg[i % 2][:, w], ACT.Exp, scale=-1.0,
                                             bias=og[g][:, q, 256 + h:257 + h],
                                             accum_out=og[g][:, q, 260 + h:261 + h])
                else:
                    w = P * len(NEAR[t])
                    nm = og[0][:, t, 256 + h:257 + h] if kind == "band" else nm_na[:, h, t:t + 1]
                    z = og[0][:, t, 260 + h:261 + h] if kind == "band" else z_na[:, h, t:t + 1]
                    ins = act.activation(prob[i % 2][:, 0:w], sneg[i % 2][:, 0:w], ACT.Exp, scale=-1.0,
                                         bias=nm, accum_out=z)
                ins.then_inc(act_exp, 1)
                while gate < GATE_UNITS - 2 and 8 * (gate + 1) <= FILL * i:
                    gate_out(gate)
                    gate += 1
            act.wait_ge(dve_lse, NG)
            act.activation(lse[:, 0:3], lse[:, 4:7], ACT.Exp).then_inc(act_lse, 1)
            while gate < GATE_UNITS:
                gate_out(gate)
                gate += 1
            for k in range(4):
                act.wait_ge(pe_oT, k + 1)
                src = bank[2 + k][:, :].rearrange("p (t r c) -> p t r c", t=NT, r=ROWS)
                dst = oaT[:, k, :].rearrange("p (r t c) -> p t r c", t=NT, r=ROWS)
                act.copy(dst, src).then_inc(act_oT, 1)
            for n in range(NT):
                act.wait_ge(dve_u, 4 * n + 4)
                sum_squares(x2[:, n, :], xs[:, n, :], n, act_ss)
                act.wait_ge(dve_var, 2 + n)
                act.activation(rt[:, n:n + 1], var[:, n:n + 1], ACT.Sqrt).then_inc(act_sd, 1)
                act.wait_ge(dve_rs, 2 + n)
                act.wait_ge(act_ss, NT + n + 1)
                act.activation(xs[:, n, :], x2[:, n, :], ACT.Copy, scale=rs[:, n:n + 1]).then_inc(act_xs, 1)
            for k in range(0, KD, 2):
                act.wait_ge(pe_h2, k + 1)
                act.activation(h2T[:, k, :], bank[k % 4][:, :], ACT.Identity, bias=modc[:, 3, k:k + 1],
                               scale=a2[:, k:k + 1]).then_inc(act_h2, 1)
            act.wait_ge(pe_rt, 1)
            act.activation(score.rearrange("p n e -> p (n e)"), bank[7][:, 0:NT * NE], ACT.Exp,
                           scale=-1.0).then_inc(act_rt, 1)
            for m in range(2):
                act.wait_ge(pe_sh, 2 * m + 1)
                act.activation(sh_tmp[:, m, :], bank[2 * m][:, :], ACT.Tanh, scale=0.5).then_inc(act_sh, 1)
            for u in range(0, 2 * NT, 2):
                act.wait_ge(pe_sh, 4 + u + 1)
                act.activation(ysh[:, u // 2, 0:512], bank[2 + u % 4][:, :], ACT.Copy, scale=0.5).then_inc(act_ysh, 1)

            def rows_out(n, b):
                act.wait_ge(pe_ht, n + 1)
                for k in range(4):
                    ins = act.activation(hTs[b][:, k, :], bank[0][:, P * k:P * k + P], ACT.Identity,
                                         bias=modc[:, 3, k:k + 1], scale=a2[:, k:k + 1])
                ins.then_inc(act_ht, 1)

            def tanh(n, b):
                act.wait_ge(pe_gu, n + 1)
                act.activation(th[b], bank[2 + b][:, 0:FE], ACT.Tanh, scale=0.5).then_inc(act_th, 1)

            def y_out(n, k, e, scattered):
                act.wait_ge(pe_dn, n + 1)
                if scattered is not None:
                    act.wait_ge(s_scatter[k], scattered)
                w = info[:, e, 2:3] if isinstance(e, int) else info[:, bass.ds(e, 1), 2:3].rearrange("p a b -> p (a b)")
                act.activation(ysb[k][:, 0:512], bank[4][:, :], ACT.Copy, scale=w).then_inc(act_y, 1)

            def body(e, k, i):
                tanh(e, k % 2)
                if not isinstance(e, int) or e + 2 < NE:
                    rows_out(e + 2, k % 2)
                y_out(e, k, e, None if isinstance(e, int) and e < 4 else 16 * i)

            rows_out(0, 0)
            rows_out(1, 1)
            for e in range(4):
                body(e, e, 0)
            with act.Fori(1, NE // 4 - 1) as i:
                for k in range(4):
                    body(4 * i + k, k, i)
            for e in range(NE - 4, NE):
                body(e, e % 4, NE // 4 - 1)
            blocks = act.value_load(ovlist[0:1, 64:65], min_val=0, max_val=31)
            with act.If(blocks > 0):
                with act.Fori(0, blocks) as i:
                    rows_out(NE + i, 0)
                    tanh(NE + i, 0)
                    y_out(NE + i, 0, NE, i * 16 + NE // 4 * 16)
            for n in range(NT):
                act.wait_ge(dve_sum, 4 * n + 4)
                act.activation(ysh[:, n, :], fin[:, n, :], ACT.Square, accum_out=ss[:, n:n + 1]).then_inc(act_fss, 1)
                act.wait_ge(dve_fv, n + 1)
                act.activation(rt[:, n:n + 1], var[:, n:n + 1], ACT.Sqrt).then_inc(act_fsd, 1)

        @block.vector
        def _(dve):
            steps = [0]

            def link(ins):
                steps[0] += 1
                ins.then_inc(dve_c, 1)
                dve.wait_ge(dve_c, steps[0])

            dve.memset(ones[:], 1.0).then_inc(dve_one, 1)
            dve.memset(zero16[:], 0.0).then_inc(dve_one, 1)

            dve.wait_ge(pool_c, 6)
            link(dve.tensor_copy(col_f, col_i))
            link(dve.tensor_copy(cl[:, 0:1], part_i[:, 0:1]))
            link(dve.tensor_scalar(mtmp, col_f, cl[:, 0:1], -float(P), ALU.subtract, ALU.add))
            link(dve.tensor_scalar(dist[0][:], mtmp, -1.0, None, ALU.mult))
            link(dve.tensor_tensor(dist[0][:], dist[0][:], mtmp, ALU.max))
            link(dve.tensor_scalar(mtmp, dist[0][:], RADIUS + 0.5, BIG, ALU.is_gt, ALU.mult))
            link(dve.tensor_scalar(dist[1][:], dist[0][:, P:2 * P], float(DIL[1]), None, ALU.mult))
            link(dve.tensor_tensor(dist[1][:], dist[1][:], mtmp[:, P:2 * P], ALU.add))
            link(dve.tensor_scalar(dist[2][:], dist[0][:, P:2 * P], float(DIL[2]), None, ALU.mult))
            dve.tensor_tensor(dist[0][:], dist[0][:], mtmp, ALU.add).then_inc(dve_tab, 1)
            link(dve.tensor_single_scalar(part_i[:, 1:2], part_i[:, 0:1], 5, ALU.logical_shift_right))
            link(dve.tensor_copy(cl[:, 1:2], part_i[:, 1:2]))
            link(dve.tensor_single_scalar(col_i[:, 0:P], col_i[:, 0:P], 5, ALU.logical_shift_right))
            link(dve.tensor_copy(mtmp[:, 0:P], col_i[:, 0:P]))
            link(dve.tensor_scalar(mtmp[:, 0:P], mtmp[:, 0:P], cl[:, 1:2], BIG, ALU.not_equal, ALU.mult))
            dve.tensor_tensor(dist[2][:], dist[2][:], mtmp[:, 0:P], ALU.add).then_inc(dve_tab, 1)
            link(dve.tensor_single_scalar(part_i[:, 1:2], part_i[:, 0:1], 15, ALU.bitwise_and))
            link(dve.tensor_copy(cl[:, 1:2], part_i[:, 1:2]))
            for t in range(NT):
                link(dve.tensor_scalar(win[:, t, 0:1], cl[:, 1:2], 16.0 * t - WC // 2, 0.0, ALU.add, ALU.max))
                link(dve.tensor_scalar(win[:, t, 0:1], win[:, t, 0:1], float(GRID - WC), -16.0 * NEAR[t][0],
                                       ALU.min, ALU.add))
                link(dve.tensor_scalar(win[:, t, 1:2], win[:, t, 0:1], float(WC), None, ALU.add))
                link(dve.tensor_scalar(nmask[:, t, :], col_f[:, 0:48], win[:, t, 0:1], None, ALU.is_ge))
                link(dve.tensor_scalar(mtmp[:, 0:48], col_f[:, 0:48], win[:, t, 1:2], None, ALU.is_lt))
                link(dve.tensor_tensor(nmask[:, t, :], nmask[:, t, :], mtmp[:, 0:48], ALU.mult))
                ins = dve.tensor_scalar(nmask[:, t, :], nmask[:, t, :], -1.0, BIG, ALU.add, ALU.mult)
                if t < NT - 1:
                    link(ins)
            ins.then_inc(dve_tab, 2)

            dve.wait_ge(act_cth, 1)
            link(dve.tensor_scalar(c_th[:], c_th[:], 1.0, 0.5, ALU.add, ALU.mult))
            link(dve.tensor_tensor(c_act[:], c_th[:], c_col[:], ALU.mult))

            def variance(n0, n1, done, v):
                dve.tensor_scalar(var[:, n0:n1], ss[:, n0:n1], 1.0 / D, EPS, ALU.mult, ALU.add).then_inc(done, 1)
                dve.wait_ge(done, v)

            def inverse_root(n0, n1, last):
                y = rs[:, n0:n1]
                link(dve.reciprocal(y, rt[:, n0:n1]))
                link(dve.tensor_tensor(rt[:, n0:n1], y, y, ALU.mult))
                link(dve.tensor_tensor(rt[:, n0:n1], rt[:, n0:n1], var[:, n0:n1], ALU.mult))
                link(dve.tensor_scalar(rt[:, n0:n1], rt[:, n0:n1], -0.5, 1.5, ALU.mult, ALU.add))
                ins = dve.tensor_tensor(y, y, rt[:, n0:n1], ALU.mult)
                if last is None:
                    link(ins)
                else:
                    ins.then_inc(last, 1)

            dve.wait_ge(act_ss, NT)
            variance(0, NT, dve_var, 1)
            dve.wait_ge(act_sd, 1)
            inverse_root(0, NT, dve_rs)

            def accumulate(j):
                k = j % KD
                if j < KD:
                    src = ada_first[k]
                    dve.wait_ge(s_ada0[k], 16)
                else:
                    r = j - KD
                    src = ada_ring[r % 2]
                    dve.wait_ge(s_adar[r % 2], 16 * (r // 2 + 1))
                if k == 0:
                    if j:
                        dve.wait_ge(pe_mod, j // KD)
                    dve.tensor_scalar(acc, src, c_act[:, 0:1], None, ALU.mult).then_inc(dve_ada, 1)
                else:
                    dve.wait_ge(dve_ada, j)
                    dve.scalar_tensor_tensor(out=acc, in0=src, scalar=c_act[:, k:k + 1], in1=acc, op0=ALU.mult,
                                             op1=ALU.add).then_inc(dve_ada, 1)

            for j in range(KD):
                accumulate(j)
            dve.wait_ge(s_small, 64)
            dve.wait_ge(pe_mod, 1)
            link(dve.tensor_tensor(modc[:, 0:2, :], ps_proj[0][:, 0:16].rearrange("p (s k) -> p s k", s=2),
                                   bada[:, 0:2, :], ALU.add))
            dve.scalar_tensor_tensor(out=a1[:], in0=modc[:, 1, :], scalar=1.0, in1=gmix[:], op0=ALU.add,
                                     op1=ALU.mult).then_inc(dve_mod, 1)
            dve.wait_ge(dve_mod, 1)
            for k in range(1, KD, 2):
                dve.wait_ge(pe_xT, k + 1)
                dve.tensor_scalar(hT[:, k, :], bank[XT_BANK[k]][:, :], a1[:, k:k + 1], modc[:, 0, k:k + 1],
                                  ALU.mult, ALU.add).then_inc(dve_hT, 1)

            def unit_out(u):
                dve.wait_ge(pe_unit, u + 1)
                if u >= QK_UNITS + VSTAGE:
                    dve.wait_ge(pe_vT, u - QK_UNITS - VSTAGE + 1)
                dst, of = unit_places(u)
                dve.tensor_copy(dst, of(ps_proj[1][:, :])).then_inc(dve_ev, 1)

            def v_out(f):
                dve.wait_ge(pe_vT, f + 1)
                dve.tensor_copy(vbuf[:, :, P * f:P * f + P],
                         bank[2 + f % 2][:, :].rearrange("p (n f) -> p n f", n=NT)).then_inc(dve_vout, 1)

            def residual_gate(row, b0, half):
                for i in range(2):
                    o = row[:, 512 * i:512 * i + 512]
                    link(dve.tensor_tensor(o, bank[b0 + i][:, :], o, ALU.add))
                    if half:
                        link(dve.tensor_scalar(o, o, 0.5, None, ALU.mult))

            j = KD
            for u in range(1, UNITS, 2):
                unit_out(u)
                if u >= QK_UNITS + 2:
                    v_out(u - QK_UNITS - 2)
                for _ in range(2):
                    if j < KD + ADA_CHUNKS:
                        accumulate(j)
                        j += 1
                if u == 9:
                    dve.wait_ge(pe_mod, 2)
                    dve.wait_ge(s_rows, 48)
                    residual_gate(gt1[:], 2, True)
                    dve.tensor_tensor(modc[:, 3, :], bank[4][:, 0:KD], bada[:, 3, :], ALU.add).then_inc(dve_mod, 1)
                if u == 17:
                    dve.wait_ge(pe_mod, 3)
                    residual_gate(gt2[:], 6, False)
                    link(dve.tensor_scalar(bg_half[:], bank[4][:, 16:32], 0.5, None, ALU.mult))
                    link(dve.tensor_tensor(modc[:, 4, :], bank[5][:, 0:KD], bada[:, 4, :], ALU.add))
                    dve.scalar_tensor_tensor(out=a2[:], in0=modc[:, 4, :], scalar=1.0, in1=gffn[:], op0=ALU.add,
                                             op1=ALU.mult).then_inc(dve_mod, 1)
                    dve.wait_ge(dve_mod, 3)

            v_out(V_UNITS - 1)

            def biased_scores(i):
                kind, g, h, t = JOBS[i]
                dve.wait_ge(pe_s, i + 1)
                dve.wait_ge(pool_bias, BIAS_OF[i] + 1)
                if i >= 2:
                    dve.wait_ge(act_exp, i - 1)
                bt = bias[BIAS_OF[i] % 3]
                pieces = []
                if kind == "group":
                    for q in range(NT):
                        pieces.append((slice(P * q, P * q + P), bt[:, 0:P], og[g][:, q, 256 + h:257 + h]))
                else:
                    w = P * len(NEAR[t])
                    if kind == "band":
                        o = P * (NEAR[t][0] - t + 1)
                        pieces.append((slice(0, w), bt[:, o:o + w], og[0][:, t, 256 + h:257 + h]))
                    else:
                        pieces.append((slice(0, w), bt[:, 0:w], nm_na[:, h, t:t + 1]))
                for w, b, nm in pieces:
                    ins = dve.tensor_tensor_reduce(out=sneg[i % 2][:, w], in0=ps_s[i % 2][:, w], in1=b,
                                                   scale=-SCALE, scalar=3e38, op0=ALU.add, op1=ALU.min,
                                                   accum_out=nm)
                ins.then_inc(dve_ttr, 1)

            def transposed_out(i):
                kind, g, h, t = JOBS[i]
                w = 512 if t is None else P * len(NEAR[t])
                dve.wait_ge(pe_t, i + 1)
                if i >= 2:
                    dve.wait_ge(pe_pv, i - 1)
                dve.tensor_copy(pT[i % 2][:, 0:w], ps_t[i % 2][:, 0:w]).then_inc(dve_pt, 1)

            def head_out(i):
                kind, g, h, t = JOBS[i]
                u = HEAD_OF[i]
                if t is not None and t != NT - 1:
                    return
                dve.wait_ge(pe_pv, i + 1)
                src = ps_o[u % 2][:, 0:NT * HD].rearrange("p (n d) -> p n d", n=NT)
                if kind == "na":
                    link(dve.reciprocal(rz_na[:, h, :], z_na[:, h, :]))
                    dve.tensor_tensor(o_na[:, :, HD * h:HD * h + HD], src,
                                      bview(rz_na[:, h, :], 0, [[1, NT], [0, HD]]), ALU.mult).then_inc(dve_o, 1)
                else:
                    dve.tensor_copy(og[g][:, :, HD * h:HD * h + HD], src).then_inc(dve_o, 1)

            dve.wait_ge(act_bt, 7)
            for i in range(NJ + 2):
                if i < NJ:
                    biased_scores(i)
                if 1 <= i <= NJ:
                    transposed_out(i - 1)
                if i >= 2:
                    head_out(i - 2)

            nm = [ogn[g][:, :, 256:260] for g in range(NG)]
            zz = [ogn[g][:, :, 260:264] for g in range(NG)]
            dve.wait_ge(s_ogn, 32)
            link(dve.tensor_tensor(lse[:, 3], nm[0], nm[1], ALU.min))
            link(dve.tensor_tensor(lse[:, 3], lse[:, 3], nm[2], ALU.min))
            for g in range(NG):
                dve.tensor_tensor(lse[:, 4 + g], lse[:, 3], nm[g], ALU.subtract).then_inc(dve_lse, 1)
            dve.wait_ge(act_lse, 1)
            link(dve.tensor_tensor(lse[:, 7], lse[:, 0], zz[0], ALU.mult))
            for g in (1, 2):
                link(dve.tensor_tensor(lse[:, 3 + g], lse[:, g], zz[g], ALU.mult))
                link(dve.tensor_tensor(lse[:, 7], lse[:, 7], lse[:, 3 + g], ALU.add))
            link(dve.reciprocal(lse[:, 7], lse[:, 7]))
            for g in range(NG):
                link(dve.tensor_tensor(lse[:, g], lse[:, g], lse[:, 7], ALU.mult))

            def weighted(dst, g):
                link(dve.tensor_tensor(dst.rearrange("p n (h d) -> p n h d", h=GH),
                                       ogn[g][:, :, 0:256].rearrange("p n (h d) -> p n h d", h=GH),
                                       bview(lse[:, g], 0, [[GH, NT], [1, GH], [0, HD]]), ALU.mult))

            weighted(prod[0], 0)
            weighted(prod[1], 1)
            link(dve.tensor_tensor(prod[0], prod[0], prod[1], ALU.add))
            weighted(prod[1], 2)
            dve.tensor_tensor(prod[0], prod[0], prod[1], ALU.add).then_inc(dve_ob, 1)
            for k in range(2):
                dve.wait_ge(pe_oT, 4 + k + 1)
                dve.tensor_copy(obT[:, k, :], bank[6 + k][:, :]).then_inc(dve_oT, 1)

            for m in range(KD):
                dve.wait_ge(pe_y, m + 1)
                dve.wait_ge(act_gate, GATE_UNITS)
                t1, t2 = ytmp[2 * (m % 2)], ytmp[2 * (m % 2) + 1]
                dve.scalar_tensor_tensor(out=t1, in0=gates[:, m, :], scalar=1.0, in1=ps_proj[m % 2][:, :],
                                         op0=ALU.add, op1=ALU.mult).then_inc(dve_m, 1)
                dve.scalar_tensor_tensor(out=t2, in0=gates[:, KD + m, :], scalar=1.0, in1=ps_s[m % 2][:, :],
                                         op0=ALU.add, op1=ALU.mult).then_inc(dve_m, 1)
                dve.wait_ge(dve_m, 3 * m + 2)
                dve.tensor_tensor(merged[:, m, :], t1, t2, ALU.add).then_inc(dve_m, 1)

            dve.wait_ge(s_xr, 16)
            for n in range(NT):
                for i in range(2):
                    u = 2 * n + i
                    dve.wait_ge(pe_wo, u + 1)
                    cut = slice(512 * i, 512 * i + 512)
                    ut = prod[0].rearrange("p n f -> p (n f)")[:, cut]
                    if u >= 2:
                        dve.wait_ge(dve_u, 2 * u - 2)
                    dve.tensor_tensor(ut, bank[4 + u % 4][:, :], gt1[:, cut], ALU.mult).then_inc(dve_u, 1)
                    dve.wait_ge(dve_u, 2 * u + 1)
                    dve.tensor_tensor(x2[:, n, cut], x2[:, n, cut], ut, ALU.add).then_inc(dve_u, 1)
                dve.wait_ge(act_ss, NT + n + 1)
                variance(n, n + 1, dve_var, 2 + n)
                dve.wait_ge(act_sd, 2 + n)
                inverse_root(n, n + 1, dve_rs)
            for k in range(1, KD, 2):
                dve.wait_ge(pe_h2, k + 1)
                dve.tensor_scalar(h2T[:, k, :], bank[k % 4][:, :], a2[:, k:k + 1], modc[:, 3, k:k + 1],
                                  ALU.mult, ALU.add).then_inc(dve_h2, 1)
            dve.wait_ge(s_xn, 16 * NT)
            for i in range(2):
                dve.memset(xg[i], 0.0).then_inc(dve_zx, 1)

            dve.wait_ge(act_rt, 1)
            dve.wait_ge(s_rows, 48)
            dve.wait_ge(pool_c, 12)
            link(dve.tensor_scalar(score, score, 1.0, None, ALU.add))
            link(dve.reciprocal(score, score))
            link(dve.tensor_tensor(biased, score, bview(ebias[:], 0, [[0, NT], [1, NE]]), ALU.add))
            b8 = biased.rearrange("p n (g e) -> p (n g) e", g=NGRP)
            for i in range(NT * NGRP):
                ins = dve.max(grp8[:, i, :], b8[:, i, :])
            link(ins)
            link(dve.tensor_tensor(grp[:].rearrange("p n g -> p (n g)"), grp8[:, :, 0], grp8[:, :, 1], ALU.add))
            other = bview(grp[:], 0, [[NGRP, NT], [0, NGRP], [1, NGRP]])
            own = bview(grp[:], 0, [[NGRP, NT], [1, NGRP], [0, NGRP]])
            link(dve.tensor_tensor(cmp, other, own, ALU.is_gt))
            link(dve.tensor_tensor(cmq, other, own, ALU.is_equal))
            link(dve.tensor_tensor(cmq, cmq, bview(before[:], 0, [[0, NT], [NGRP, NGRP], [1, NGRP]]),
                                   ALU.mult))
            link(dve.tensor_tensor(cmp, cmp, cmq, ALU.add))
            link(dve.tensor_reduce(gsel[:], cmp, AX.X, ALU.add))
            link(dve.tensor_scalar(gsel[:], gsel[:], TOPG - 0.5, None, ALU.is_lt))
            link(dve.tensor_scalar(gpen[:], gsel[:], -1.0, BIG, ALU.add, ALU.mult))
            spread = [[NGRP, NT], [1, NGRP], [0, NE // NGRP]]
            b4 = biased.rearrange("p n (g e) -> p n g e", g=NGRP)
            link(dve.tensor_tensor(b4, b4, bview(gsel[:], 0, spread), ALU.mult))
            link(dve.tensor_tensor(b4, b4, bview(gpen[:], 0, spread), ALU.add))
            for n in range(NT):
                ins = dve.max(top8[:, n, :], biased[:, n, :])
            link(ins)
            for n in range(NT):
                ins = dve.match_replace(wt[:, n, :], top8[:, n, :], biased[:, n, :], -3e38)
            link(ins)
            link(dve.tensor_scalar(sel, wt, -2e38, None, ALU.is_lt))
            dve.tensor_copy(selb, sel).then_inc(dve_sel, 1)
            link(dve.tensor_tensor(wt, score, sel, ALU.mult))
            link(dve.tensor_reduce(wsum[:], wt, AX.X, ALU.add))
            link(dve.reciprocal(wsum[:], wsum[:]))
            link(dve.tensor_tensor(wt, wt, bview(wsum[:], 0, [[1, NT], [0, NE]]), ALU.mult))
            link(dve.tensor_scalar(wt, wt, ROUTED / 2, None, ALU.mult))
            link(dve.tensor_copy(rhs9[:, :, :, 2, 0], wt))
            link(dve.tensor_tensor(wt, wt, rhs9[:, :, :, 2, 0], ALU.subtract))
            link(dve.tensor_copy(rhs9[:, :, :, 2, 1], wt))
            link(dve.tensor_tensor(wt, wt, rhs9[:, :, :, 2, 1], ALU.subtract))
            link(dve.tensor_copy(rhs9[:, :, :, 2, 2], wt))
            for n in range(NT):
                ins = dve.tensor_tensor_scan(kth[:, n, :], ones[:, 0:NE], sel[:, n, :], 0.0, ALU.mult, ALU.add)
            link(ins)
            link(dve.tensor_scalar(rhs9[:, :, :, 1, 2], kth, -1.0, None, ALU.add))
            link(dve.memset(rhs9[:, :, :, 0, 2], 0.0))
            link(dve.tensor_scalar(kth, sel, 0.0, cl[:, 0:1], ALU.mult, ALU.add))
            link(dve.tensor_copy(rhs9[:, :, :, 0, 0], kth))
            link(dve.tensor_scalar(rhs9[:, :, :, 1, 0], kth, float(TOPK), None, ALU.mult))
            for n in range(NT):
                dve.memset(rhs9[:, n, :, 0, 1], 128.0 * n - 1024.0)
                ins = dve.memset(rhs9[:, n, :, 1, 1], 1024.0 * n - 8192.0)
            link(ins)
            dve.wait_ge(pe_rt, 2)
            link(dve.scalar_tensor_tensor(out=posm[:].rearrange("p n e -> p (n e)"), in0=bank[6][:, 0:NT * NE],
                                          scalar=1.0, in1=sel.rearrange("p n e -> p (n e)"), op0=ALU.add,
                                          op1=ALU.mult))
            dve.tensor_scalar(posm[:], posm[:], -1.0, None, ALU.add).then_inc(dve_tabs, 1)
            dve.wait_ge(dve_tabs, 1)

            link(dve.tensor_copy(cnt_e[:], bank[7][0:NE, 256:257]))
            for b in range(3):
                link(dve.tensor_scalar(ovf[:, b:b + 1], cnt_e[:], P * (b + 1) + 0.5, None, ALU.is_gt))
                link(dve.memset(eval_[:, b + 1:b + 2], b + 1.0))
            link(dve.tensor_copy(eval_[:, 0:1], cl[0:NE, 0:1]))
            dve.tensor_copy(ovfb[:], ovf[:]).then_inc(dve_ovf, 1)
            dve.wait_ge(pe_rt, 3)
            link(dve.tensor_copy(ovr[:], bank[7][0:NE, 260:263]))
            for b in range(3):
                ins = dve.tensor_scalar(ov1h[:, b, :], slot_id[0:NE, 0, 0:32], ovr[:, b:b + 1], ovf[:, b:b + 1],
                                        ALU.is_equal, ALU.mult)
            ins.then_inc(dve_ovf, 1)
            dve.wait_ge(pe_rt, 4)
            dve.tensor_copy(ovlist[0:1, 0:65], bank[7][0:1, 264:329]).then_inc(dve_list, 1)

            for m in range(2):
                dve.wait_ge(act_sh, m + 1)
                dve.wait_ge(pe_sh, 2 * m + 2)
                link(dve.scalar_tensor_tensor(out=sh_tmp[:, m, :], in0=sh_tmp[:, m, :], scalar=1.0,
                                              in1=bank[2 * m][:, :], op0=ALU.add, op1=ALU.mult))
                dve.tensor_tensor(sh_act[:, m, :], sh_tmp[:, m, :], bank[2 * m + 1][:, :],
                                  ALU.mult).then_inc(dve_sh, 1)

            def one_hot(n, k, e, b):
                if b is None:
                    if not isinstance(n, int) or n >= 2:
                        dve.wait_ge(pe_info, n - 1)
                    ids = bview(slot_id, 0, [[0, NT], [1, P]])
                    place = bview(posm[:], e, [[NE, NT], [0, P]]) if isinstance(e, int) else \
                        posm[:, :, bass.ds(e, 1)].to_broadcast([P, NT, P])
                else:
                    ids = slot_id[:, bass.ds(b, 1), :].to_broadcast([P, NT, P])
                    place = posm[:, :, bass.ds(e, 1)].to_broadcast([P, NT, P])
                dve.tensor_tensor(onehot[k % 2], ids, place, ALU.is_equal).then_inc(dve_oh, 1)

            def of_expert(e, c):
                if isinstance(e, int):
                    return info[:, e, c]
                return info[:, bass.ds(e, 1), c].rearrange("p a b -> p (a b)")

            def indices(n, k, e, gathered):
                dve.wait_ge(pe_info, n + 1)
                dve.tensor_reduce(of_expert(e, slice(0, 3)), bank[6][:, 16 * (k % 2):16 * (k % 2) + 9]
                                  .rearrange("p (c a) -> p c a", a=3), AX.X, ALU.add).then_inc(dve_info, 1)
                dve.wait_ge(dve_info, n + 1)
                if gathered is not None:
                    dve.wait_ge(s_gather[k], gathered)
                dve.tensor_scalar(idx_t[:, k, :], of_expert(e, slice(0, 1)), 1024.0, None, ALU.add).then_inc(dve_idx, 1)

            def rows_out(n, b):
                dve.wait_ge(pe_ht, n + 1)
                for k in range(4, KD):
                    ins = dve.tensor_scalar(hTs[b][:, k, :], bank[1][:, P * (k - 4):P * (k - 3)], a2[:, k:k + 1],
                                            modc[:, 3, k:k + 1], ALU.mult, ALU.add)
                ins.then_inc(dve_ht, 1)

            def activations(n, b):
                dve.wait_ge(act_th, n + 1)
                dve.scalar_tensor_tensor(out=gth[b], in0=th[b], scalar=1.0, in1=bank[2 + b][:, 0:FE], op0=ALU.add,
                                         op1=ALU.mult).then_inc(dve_g, 1)
                dve.wait_ge(dve_g, n + 1)
                dve.tensor_tensor(act_t[b], gth[b], bank[2 + b][:, FE:2 * FE], ALU.mult).then_inc(dve_act, 1)

            def act_transposed(n, b):
                dve.wait_ge(pe_at, n + 1)
                dve.tensor_copy(aT[b], bank[7][:, 0:256].rearrange("p (k s) -> p k s", k=2)).then_inc(dve_at, 1)

            def y_out(n, k, e, scattered):
                dve.wait_ge(pe_dn, n + 1)
                if scattered is not None:
                    dve.wait_ge(s_scatter[k], scattered)
                dve.tensor_scalar(idx_r[:, k, :], of_expert(e, slice(1, 2)), 8192.0, None, ALU.add).then_inc(dve_idr, 1)
                dve.tensor_scalar(ysb[k][:, 512:1024], bank[5][:, :], of_expert(e, slice(2, 3)), None,
                                  ALU.mult).then_inc(dve_y, 1)

            def body(e, k, i):
                ahead = not isinstance(e, int) or e + AHEAD < NE
                if ahead:
                    one_hot(e + AHEAD, k, e + AHEAD, None)
                activations(e, k % 2)
                act_transposed(e, k % 2)
                if not isinstance(e, int) or e + 2 < NE:
                    rows_out(e + 2, k % 2)
                if ahead:
                    indices(e + AHEAD, k, e + AHEAD, 16 * i + 16)
                y_out(e, k, e, None if isinstance(e, int) and e < 4 else 16 * i)

            for i in range(2, 4):
                dve.memset(xg[i], 0.0).then_inc(dve_zx, 1)
            for u in range(1, 2 * NT, 2):
                dve.wait_ge(pe_sh, 4 + u + 1)
                dve.tensor_scalar(ysh[:, u // 2, 512:1024], bank[2 + u % 4][:, :], 0.5, None,
                                  ALU.mult).then_inc(dve_ysh, 1)
            for e in range(AHEAD):
                one_hot(e, e, e, None)
                indices(e, e, e, None)
            rows_out(0, 0)
            rows_out(1, 1)
            for e in range(4):
                body(e, e, 0)
            with dve.Fori(1, NE // 4 - 1) as i:
                for k in range(4):
                    body(4 * i + k, k, i)
            for e in range(NE - 4, NE):
                body(e, e % 4, NE // 4 - 1)
            blocks = dve.value_load(ovlist[0:1, 64:65], min_val=0, max_val=31)
            with dve.If(blocks > 0):
                with dve.Fori(0, blocks) as i:
                    e = dve.value_load(ovlist[0:1, bass.ds(i, 1)], min_val=0, max_val=NE - 1)
                    b = dve.value_load(ovlist[0:1, bass.ds(i + 32, 1)], min_val=1, max_val=3)
                    dve.wait_ge(pe_dn, i + NE)
                    dve.wait_ge(s_scatter[0], i * 16 + NE // 4 * 16)
                    one_hot(NE + i, 0, e, b)
                    indices(NE + i, 0, NE, None)
                    rows_out(NE + i, 0)
                    activations(NE + i, 0)
                    act_transposed(NE + i, 0)
                    y_out(NE + i, 0, NE, None)

            for n in range(NT):
                f = fin[:, n, :]
                dve.wait_ge(s_pair[n % 2], 16 * (n // 2 + 1))
                dve.tensor_reduce(f, pairs[n % 2].rearrange("p q d -> p d q"), AX.X, ALU.add).then_inc(dve_sum, 1)
                dve.wait_ge(dve_sum, 4 * n + 1)
                dve.wait_ge(act_ysh, NT)
                dve.tensor_tensor(f, f, ysh[:, n, :], ALU.add).then_inc(dve_sum, 1)
                dve.wait_ge(dve_sum, 4 * n + 2)
                dve.tensor_tensor(f, f, gt2[:], ALU.mult).then_inc(dve_sum, 1)
                dve.wait_ge(dve_sum, 4 * n + 3)
                dve.tensor_tensor(f, f, x2[:, n, :], ALU.add).then_inc(dve_sum, 1)
                dve.wait_ge(act_fss, n + 1)
                variance(n, n + 1, dve_fv, n + 1)
                dve.wait_ge(act_fsd, n + 1)
                inverse_root(n, n + 1, None)
                dve.wait_ge(s_gfin, 16)
                dve.scalar_tensor_tensor(out=f, in0=f, scalar=rs[:, n:n + 1], in1=gfin[:], op0=ALU.mult,
                                         op1=ALU.mult).then_inc(dve_fin, 1)

        @block.tensor
        def _(pe):
            def bias_table():
                pe.wait_ge(s_btr, 16 * ROWS)
                for i in range(7):
                    w = min(512, BT - 512 * i)
                    if i == 0:
                        pe.wait_ge(act_hT, 4)
                        pe.wait_ge(dve_hT, 4)
                    if i == 6:
                        pe.wait_ge(act_bt, 1)
                    pe.matmul(bank[2 + i % 6][:, 0:w], flip[:], bt_rev[:, 512 * i:512 * i + w], start=True,
                              stop=True).then_inc(pe_bt, 1)

            pe.wait_ge(pool_c, 4)

            def x_transposes(k):
                for n in range(NT):
                    src = x_first[:, n, :].rearrange("p (f k) -> p k f", k=KD)[:, k, :]
                    mm = pe.transpose(bank[XT_BANK[k]][:, P * n:P * n + P], src, ident[:])
                mm.then_inc(pe_xT, 1)

            pe.wait_ge(act_xs, NT)
            for k in range(6):
                x_transposes(k)

            def column(dst, o):
                cols = acc[:, o:o + D].rearrange("p (f k) -> p k f", k=KD)
                for k in range(KD):
                    mm = pe.matmul(dst[:, k:k + 1], cols[:, k, :], ones[:, 0:1], start=True, stop=True)
                return mm

            pe.wait_ge(dve_one, 1)
            pe.wait_ge(dve_ada, KD)
            column(ps_proj[0][:, 0:8], 0)
            column(ps_proj[0][:, 8:16], D).then_inc(pe_mod, 1)
            x_transposes(6)
            pe.wait_ge(dve_mod, 1)
            x_transposes(7)

            def free_bank(u):
                if u < 2:
                    return
                if u - 2 >= UNITS:
                    pe.wait_ge(act_gate, u - 2 - UNITS + 1)
                elif u % 2:
                    pe.wait_ge(dve_ev, (u - 2) // 2 + 1)
                else:
                    pe.wait_ge(act_ev, (u - 2) // 2 + 1)

            def chunk(i):
                pe.wait_ge(s_w[i % WSLOTS], 16 * (i // WSLOTS + 1))

            pe.wait_ge(act_hT, 4)
            pe.wait_ge(dve_hT, 4)
            def v_transposes(f):
                u = QK_UNITS + f
                pe.wait_ge(dve_ev if u % 2 else act_ev, u // 2 + 1)
                if f >= 2:
                    pe.wait_ge(dve_vout if f % 2 else act_vout, (f - 2) // 2 + 1)
                for n in range(NT):
                    mm = pe.transpose(bank[2 + f % 2][:, P * n:P * n + P], vT[u % VSTAGE][:, P * n:P * n + P],
                                      ident[:])
                mm.then_inc(pe_vT, 1)

            for u in range(UNITS):
                if u % 2 == 0:
                    chunk(u // 2)
                free_bank(u)
                if u == 9:
                    pe.wait_ge(dve_ada, 2 * KD)
                    pe.wait_ge(act_bt, 7)
                    for i in range(2):
                        pe.matmul(bank[2 + i][:, :], ones[:], acc[:, 512 * i:512 * i + 512], start=True, stop=True)
                    column(bank[4][:, 0:8], D).then_inc(pe_mod, 1)
                if u == 17:
                    pe.wait_ge(dve_ada, 3 * KD)
                    pe.wait_ge(dve_mod, 2)
                    pe.wait_ge(s_bg, 16)
                    column(bank[5][:, 0:8], 0)
                    pe.transpose(bank[4][:, 16:32], bg_rows[:], ident[0:16, 0:16])
                    for k in range(2):
                        mm = pe.matmul(bank[6 + k][:, :], ones[:], acc[:, D + 512 * k:D + 512 * k + 512], start=True,
                                       stop=True)
                    mm.then_inc(pe_mod, 1)
                for k in range(KD):
                    mm = pe.matmul(ps_proj[u % 2][:, :], wbuf[u // 2 % WSLOTS][:, k, P * (u % 2):P * (u % 2) + P],
                                   hT[:, k, :], start=(k == 0), stop=(k == KD - 1))
                mm.then_inc(pe_unit, 1)
                if u == BT_UNIT:
                    bias_table()
                if u >= QK_UNITS + 1:
                    v_transposes(u - QK_UNITS - 1)
            v_transposes(V_UNITS - 1)
            gate_mm = [0]

            def gate_products(upto):
                while gate_mm[0] < upto:
                    m, k = gate_mm[0] // KD, gate_mm[0] % KD
                    i = N_QK + N_V + m // 2
                    if k == 0:
                        if m % 2 == 0:
                            chunk(i)
                        free_bank(UNITS + m)
                    mm = pe.matmul(ps_proj[m % 2][:, :], wbuf[i % WSLOTS][:, k, P * (m % 2):P * (m % 2) + P],
                                   hT[:, k, :], start=(k == 0), stop=(k == KD - 1))
                    if k == KD - 1:
                        mm.then_inc(pe_unit, 1)
                    gate_mm[0] += 1

            def heads(kind, g, h):
                if kind == "na":
                    return qkt[:, h // 2, :], qkt[:, 4 + h // 2, :], HD * (h % 2), HD * h
                n = g * GH + h
                return (qkt[:, 8 + n // 2, :], qkt[:, 14 + n // 2, :], HD * (n % 2), NAH * HD + HD * n)

            def scores(i):
                kind, g, h, t = JOBS[i]
                q, k, p0, _ = heads(kind, g, h)
                q, k = q[p0:p0 + HD, :], k[p0:p0 + HD, :]
                if i >= 2:
                    pe.wait_ge(dve_ttr, i - 1)
                dst = ps_s[i % 2]
                for q_tile in (range(NT) if t is None else [t]):
                    k0, w = (q_tile, 1) if t is None else (NEAR[t][0], len(NEAR[t]))
                    c0 = P * q_tile if t is None else 0
                    mm = pe.matmul(dst[:, c0:c0 + P * w], q[:, P * q_tile:P * q_tile + P],
                                   k[:, P * k0:P * (k0 + w)], start=True, stop=True)
                mm.then_inc(pe_s, 1)

            def transposes(i):
                kind, g, h, t = JOBS[i]
                pe.wait_ge(act_exp, i + 1)
                if i >= 2:
                    pe.wait_ge(dve_pt, i - 1)
                w = NT if t is None else len(NEAR[t])
                for j in range(w):
                    mm = pe.transpose(ps_t[i % 2][:, P * j:P * j + P], prob[i % 2][:, P * j:P * j + P], ident[:])
                mm.then_inc(pe_t, 1)

            def values(i):
                kind, g, h, t = JOBS[i]
                u = HEAD_OF[i]
                f = heads(kind, g, h)[3]
                pe.wait_ge(dve_pt, i + 1)
                if t in (None, 0) and u >= 2:
                    pe.wait_ge(dve_o, u - 1)
                for q in (range(NT) if t is None else [t]):
                    near = [q] if t is None else NEAR[t]
                    for j, kt in enumerate(near):
                        c0 = P * (q if t is None else j)
                        mm = pe.matmul(ps_o[u % 2][:, HD * q:HD * q + HD], pT[i % 2][:, c0:c0 + P],
                                       vbuf[:, kt, f:f + HD], start=(j == 0), stop=(j == len(near) - 1))
                mm.then_inc(pe_pv, 1)

            pe.wait_ge(act_vout, V_UNITS // 2)
            pe.wait_ge(dve_vout, V_UNITS // 2)
            pe.wait_ge(dve_mod, 3)
            for i in range(NJ + 2):
                if i < NJ:
                    scores(i)
                    gate_products(FILL * (i + 1))
                if 1 <= i <= NJ:
                    transposes(i - 1)
                if i >= 2:
                    values(i - 2)
            gate_products(KD * GATE_UNITS)

            pe.wait_ge(dve_o, N_HEADS)
            for k in range(4):
                for t in range(NT):
                    mm = pe.transpose(bank[2 + k][:, P * t:P * t + P], o_na[:, t, P * k:P * k + P], ident[:])
                mm.then_inc(pe_oT, 1)
            pe.wait_ge(dve_ob, 1)
            for k in range(2):
                for n in range(NT):
                    mm = pe.transpose(bank[6 + k][:, P * n:P * n + P], prod[0][:, n, P * k:P * k + P], ident[:])
                mm.then_inc(pe_oT, 1)
            pe.wait_ge(act_gate, GATE_UNITS)
            pe.wait_ge(act_oT, 4)
            pe.wait_ge(dve_oT, 2)
            pe.wait_ge(s_wp, 32)
            for m in range(KD):
                if m >= 2:
                    pe.wait_ge(dve_m, 3 * (m - 2) + 2)
                for k in range(4):
                    pe.matmul(ps_proj[m % 2][:, :], wpa[:, k, P * m:P * m + P], oaT[:, k, :], start=(k == 0),
                              stop=(k == 3))
                for k in range(2):
                    mm = pe.matmul(ps_s[m % 2][:, :], wpb[:, k, P * m:P * m + P], obT[:, k, :], start=(k == 0),
                                   stop=(k == 1))
                mm.then_inc(pe_y, 1)
            pe.wait_ge(dve_m, 3 * KD)
            pe.wait_ge(s_wo, 16)
            for u in range(2 * NT):
                n, i = u // 2, u % 2
                if u >= 4:
                    pe.wait_ge(dve_u, 2 * (u - 4) + 1)
                for k in range(KD):
                    mm = pe.matmul(bank[4 + u % 4][:, :], merged[:, k, P * n:P * n + P],
                                   wo[:, k, 512 * i:512 * i + 512], start=(k == 0), stop=(k == KD - 1))
                mm.then_inc(pe_wo, 1)
            pe.wait_ge(act_xs, 2 * NT)
            for k in range(KD):
                if k >= 4:
                    pe.wait_ge(dve_h2 if k % 2 else act_h2, (k - 4) // 2 + 1)
                for n in range(NT):
                    src = xs[:, n, :].rearrange("p (f k) -> p k f", k=KD)[:, k, :]
                    mm = pe.transpose(bank[k % 4][:, P * n:P * n + P], src, ident[:])
                mm.then_inc(pe_h2, 1)
            pe.wait_ge(act_h2, 4)
            pe.wait_ge(dve_h2, 4)
            pe.wait_ge(s_wr, 16)
            pe.wait_ge(dve_u, 4 * NT)
            for n in range(NT):
                for k in range(KD):
                    mm = pe.matmul(bank[7][:, NE * n:NE * n + NE], h2T[:, k, P * n:P * n + P], wr[:, k, :],
                                   start=(k == 0), stop=(k == KD - 1))
            mm.then_inc(pe_rt, 1)
            pe.wait_ge(s_wsh, 48)
            for m in range(2):
                for a in range(2):
                    for k in range(KD):
                        mm = pe.matmul(bank[2 * m + a][:, :], wgu[3][:, a, k, P * m:P * m + P], h2T[:, k, :],
                                       start=(k == 0), stop=(k == KD - 1))
                    mm.then_inc(pe_sh, 1)
            pe.wait_ge(dve_sel, 1)
            for n in range(NT):
                for m in range(n + 1):
                    mm = pe.matmul(bank[6][:, NE * n:NE * n + NE], tri[:] if m == n else onesb[:], selb[:, m, :],
                                   start=(m == 0), stop=(m == n))
            for n in range(NT):
                mm = pe.matmul(bank[7][0:NE, 256:257], selb[:, n, :], onesb[:, 0:1], start=(n == 0),
                               stop=(n == NT - 1))
            mm.then_inc(pe_rt, 1)
            pe.wait_ge(dve_ovf, 1)
            pe.matmul(bank[7][0:NE, 260:263], tri[0:NE, 0:NE], ovfb[:], start=True, stop=False, skip_group_check=True)
            pe.matmul(bank[7][0:NE, 261:263], onesb[0:NE, 0:NE], ovfb[:, 0:2], start=False, stop=False,
                      skip_group_check=True)
            pe.matmul(bank[7][0:NE, 262:263], onesb[0:NE, 0:NE], ovfb[:, 0:1], start=False, stop=True,
                      skip_group_check=True).then_inc(pe_rt, 1)
            pe.wait_ge(dve_ovf, 2)
            for b in range(3):
                pe.matmul(bank[7][0:1, 264:296], eval_[:, 0:1], ov1h[:, b, :], start=(b == 0), stop=(b == 2))
            for b in range(3):
                pe.matmul(bank[7][0:1, 296:328], eval_[:, b + 1:b + 2], ov1h[:, b, :], start=(b == 0), stop=(b == 2))
            for b in range(3):
                mm = pe.matmul(bank[7][0:1, 328:329], ones[0:NE, 0:1], ovf[:, b:b + 1], start=(b == 0), stop=(b == 2))
            mm.then_inc(pe_rt, 1)
            pe.wait_ge(dve_sh, 2)
            for u in range(2 * NT):
                n, i = u // 2, u % 2
                if u >= 4:
                    pe.wait_ge(dve_ysh if u % 2 else act_ysh, (u - 4) // 2 + 1)
                for m in range(2):
                    mm = pe.matmul(bank[2 + u % 4][:, :], sh_act[:, m, P * n:P * n + P],
                                   wd[3][:, m, 512 * i:512 * i + 512], start=(m == 0), stop=(m == 1))
                mm.then_inc(pe_sh, 1)

            def slots(n, k, e):
                pe.wait_ge(dve_oh, n + 1)
                if not isinstance(n, int) or n >= 1:
                    pe.wait_ge(dve_info, n)
                for t in range(NT):
                    rhs = rhs9[:, t, e, :, :] if isinstance(e, int) else rhs9[:, t, bass.ds(e, 1), :, :]
                    mm = pe.matmul(bank[6][:, 16 * (k % 2):16 * (k % 2) + 9], onehot[k % 2][:, t, :], rhs,
                                   start=(t == 0), stop=(t == NT - 1))
                mm.then_inc(pe_info, 1)

            def rows(n, b, gathered):
                pe.wait_ge(s_gather[b], gathered)
                if not isinstance(n, int) or n >= 1:
                    pe.wait_ge(act_ht, n)
                    pe.wait_ge(dve_ht, n)
                for k in range(KD):
                    src = xg[b].rearrange("p (f k) -> p k f", k=KD)[:, k, :]
                    mm = pe.transpose(bank[k // 4][:, P * (k % 4):P * (k % 4) + P], src, ident[:])
                mm.then_inc(pe_ht, 1)

            def gate_up(n, k, loaded):
                b = k % 2
                pe.wait_ge(act_ht, n + 1)
                pe.wait_ge(dve_ht, n + 1)
                pe.wait_ge(s_wgu[k], loaded)
                if not isinstance(n, int) or n >= 2:
                    pe.wait_ge(dve_act, n - 1)
                for j in range(KD):
                    mm = pe.matmul(bank[2 + b][:, :], hTs[b][:, j, :], wgu[k][:, :, j, :], start=(j == 0),
                                   stop=(j == KD - 1))
                mm.then_inc(pe_gu, 1)

            def act_transposes(n, b):
                pe.wait_ge(dve_act, n + 1)
                for j in range(2):
                    src = act_t[b].rearrange("p (f k) -> p k f", k=2)[:, j, :]
                    mm = pe.transpose(bank[7][:, P * j:P * j + P], src, ident[:])
                mm.then_inc(pe_at, 1)

            def down(n, k, loaded):
                pe.wait_ge(dve_at, n + 1)
                pe.wait_ge(s_wd[k], loaded)
                if not isinstance(n, int) or n >= 1:
                    pe.wait_ge(act_y, n)
                    pe.wait_ge(dve_y, n)
                for i in range(2):
                    for j in range(2):
                        mm = pe.matmul(bank[4 + i][:, :], aT[k % 2][:, j, :], wd[k][:, j, 512 * i:512 * i + 512],
                                       start=(j == 0), stop=(j == 1))
                mm.then_inc(pe_dn, 1)

            def body(e, k, i):
                if not isinstance(e, int) or e + 1 < NE:
                    gate_up(e + 1, (k + 1) % 4, 32 * (i + 1) if k < 3 else 32 * (i + 2))
                act_transposes(e, k % 2)
                if not isinstance(e, int) or e + 2 < NE:
                    rows(e + 2, (k + 2) % 4, 16 * i + 16 + 16 * (k // 2))
                if not isinstance(e, int) or e + AHEAD < NE:
                    slots(e + AHEAD, k, e + AHEAD)
                down(e, k, 16 * (i + 1))

            pe.wait_ge(dve_tabs, 1)
            pe.wait_ge(act_ysh, NT)
            pe.wait_ge(dve_ysh, NT)
            pe.wait_ge(dve_list, 1)
            for e in range(AHEAD):
                slots(e, e, e)
            rows(0, 0, 16)
            rows(1, 1, 16)
            gate_up(0, 0, 32)
            for e in range(4):
                body(e, e, 0)
            with pe.Fori(1, NE // 4 - 1) as i:
                for k in range(4):
                    body(4 * i + k, k, i)
            for e in range(NE - 4, NE):
                body(e, e % 4, NE // 4 - 1)
            blocks = pe.value_load(ovlist[0:1, 64:65], min_val=0, max_val=31)
            with pe.If(blocks > 0):
                with pe.Fori(0, blocks) as i:
                    e = pe.value_load(ovlist[0:1, bass.ds(i, 1)], min_val=0, max_val=NE - 1)
                    slots(NE + i, 0, e)
                    rows(NE + i, 0, i * 16 + NE // 4 * 16 + 16)
                    gate_up(NE + i, 0, i * 32 + NE // 4 * 32 + 32)
                    act_transposes(NE + i, 0)
                    down(NE + i, 0, i * 16 + NE // 4 * 16 + 16)


_INS = ["x", "c", "w_ada", "b_ada", "g_mix", "w_in", "b_gate", "rpb", "w_pa", "w_pb", "w_o", "g_ffn", "w_router",
        "e_bias", "we_gate", "we_up", "we_down", "ws_gate", "ws_up", "ws_down", "g_final"]


def kernel(**inputs):
    import numpy as np
    import concourse.bacc as bacc
    from concourse.bass_utils import run_bass_kernel_spmd

    nc = bacc.Bacc("TRN2", target_bir_lowering=False, num_devices=1)
    arrays, args = {}, []
    for name in _INS:
        a = np.ascontiguousarray(inputs[name])
        arrays[f"in_{name}"] = a
        args.append(nc.dram_tensor(f"in_{name}", a.shape, mybir.dt.from_np(a.dtype), kind="ExternalInput").ap())
    out = nc.dram_tensor("out_0", (1, S, D), F32, kind="ExternalOutput").ap()
    build(nc, *args, out)
    r = run_bass_kernel_spmd(nc, [arrays], core_ids=[0])
    return r.results[0]["out_0"]
```

```python
from contextlib import ExitStack

import concourse.bass as bass
from concourse import mybir

F32 = mybir.dt.float32
BF16 = mybir.dt.bfloat16
I32 = mybir.dt.int32
U32 = mybir.dt.uint32
ALU = mybir.AluOpType
ACT = mybir.ActivationFunctionType
AX = mybir.AxisListType

P = 128
D = 1024
S = 512
NT = S // P
KD = D // P
HD = 64
GRID = 64
ROWS = S // GRID
NAH, WR, WC = 8, 8, 16
NG, GH = 3, 4
RADIUS = 64
DIL = (1, 4, 16)
NE, TOPK, NGRP, TOPG, FE = 64, 8, 8, 4, 256
ROUTED = 2.5
EPS = 1e-6
BIG = 1e30
SCALE = HD ** -0.5
SLOPES = [2.0 ** (-8.0 * (i + 1) / (NG * GH)) for i in range(NG * GH)]
RPBH = (2 * WR - 1) * (2 * WC - 1)
RPBW = 2 * WC - 1
BT = (NAH - 1) * RPBH + (ROWS - 1) * RPBW + 48
RPAD = WC
CW = 256

DIL0 = 3 * NAH * HD
GATE0 = DIL0 + 3 * NG * GH * HD
CHUNKS = ([0, 256, 512, 768] + [DIL0 + CW * i for i in range(6)] + [1024, 1280]
          + [DIL0 + 1536 + CW * i for i in range(3)] + [GATE0 + CW * i for i in range(8)])
N_QK, N_V, N_GATE = 10, 5, 8
QK_UNITS, V_UNITS, GATE_UNITS = 2 * N_QK, 2 * N_V, 2 * N_GATE
VSTAGE = 4
UNITS = QK_UNITS + V_UNITS
WSLOTS = 3
ADA_CHUNKS = 2 * KD

NEAR = [[0, 1], [0, 1, 2], [1, 2, 3], [2, 3]]


def jobs():
    out = [("group", g, h, None) for g in (2, 1) for h in range(GH)]
    out += [("band", 0, h, t) for h in range(GH) for t in range(NT)]
    out += [("na", 0, h, t) for h in range(NAH) for t in range(NT)]
    return out


JOBS = jobs()
HEAD_OF = []
BIAS_OF = []
_h = _b = -1
for _kind, _g, _hh, _t in JOBS:
    if _t in (None, 0):
        _h += 1
    if _kind != "band" or _t == 0:
        _b += 1
    HEAD_OF.append(_h)
    BIAS_OF.append(_b)
N_HEADS, N_BIAS = _h + 1, _b + 1


def last_of(table, value):
    return max(i for i, x in enumerate(table) if x == value)


A_QKT, A_V, A_HT, A_W, A_BT, A_JOB, A_GATE, A_O = 0, 10240, 15360, 19456, 25600, 29120, 33344, 41536
A_END = 46784
B_WPA, B_OAT, B_OGN, B_TMP, B_WO, B_X = 0, 6144, 10240, 12352, 19456, 27648
SLOT = [0, 12288, 18432, 6144]
SLOT_WORDS = 6144
C_XS, C_H2T, C_YSH, C_WR = 33344, 37440, 41536, 45632
C_Y, C_OH, C_AT, C_ACT, C_XG, C_HTS = 24576, 26624, 27136, 31744, 33344, 35392
XT_BANK = [2, 3, 4, 5, 6, 7, 1, 0]
BT_UNIT = 4
PBUF = 3
OVF = 2
AHEAD = 4
FILL = 2


def build(nc, x, c, w_ada, b_ada, g_mix, w_in, b_gate, rpb, w_pa, w_pb, w_o, g_ffn, w_router, e_bias,
          we_gate, we_up, we_down, ws_gate, ws_up, ws_down, g_final, out):
    rpb_pad = nc.dram_tensor("rpb_pad", [2 * RPAD + NAH * RPBH], F32, kind="Internal").ap()
    dil_dram = nc.dram_tensor("dil_dram", [2, S, 264], F32, kind="Internal").ap()
    xn_dram = nc.dram_tensor("xn_dram", [S, D], F32, kind="Internal").ap()
    pair_dram = nc.dram_tensor("pair_dram", [S * TOPK, D], F32, kind="Internal").ap()

    with ExitStack() as ctx:
        def sb(name, shape, dt=F32):
            return ctx.enter_context(nc.sbuf_tensor(name, shape, dt))

        def sem(name):
            return ctx.enter_context(nc.semaphore(name))

        arena = sb("arena", [P, A_END])

        def at(off, n):
            return arena[:, off:off + n]

        ada_first = [at(2048 * k, 2048) for k in range(7)] + [at(A_GATE + 4096, 2048)]
        ada_ring = [at(A_GATE + 4096, 2048), at(A_GATE + 6144, 2048)]
        x_first = at(A_GATE, 4096).rearrange("p (n d) -> p n d", n=NT)
        acc = at(A_JOB, 2048)
        bt_rev = at(A_O, BT)
        qkt = at(A_QKT, 10240).rearrange("p (m t) -> p m t", m=20)
        vbuf = at(A_V, 5120).rearrange("p (n f) -> p n f", n=NT)
        hT = at(A_HT, 4096).rearrange("p (k t) -> p k t", k=KD)
        vT = [at(A_GATE + 512 * i, 512) for i in range(VSTAGE)]
        wbuf = [at(A_W + 2048 * i, 2048).rearrange("p (k f) -> p k f", k=KD) for i in range(WSLOTS)]
        bt8 = at(A_BT, BT)
        bias = [at(A_JOB + 384 * i, 384) for i in range(3)]
        sneg = [at(A_JOB + 1152 + 512 * i, 512) for i in range(2)]
        prob = [at(A_JOB + 2176 + 512 * i, 512) for i in range(2)]
        pT = [at(A_JOB + 3200 + 512 * i, 512) for i in range(2)]
        gates = at(A_GATE, 8192).rearrange("p (m t) -> p m t", m=16)
        o_na = at(A_O, 2048).rearrange("p (n f) -> p n f", n=NT)
        og = [at(A_O + 2048 + 1056 * g, 1056).rearrange("p (n f) -> p n f", n=NT) for g in range(NG)]
        wpa = at(B_WPA, 4096).rearrange("p (k f) -> p k f", k=4)
        wpb = at(B_WPA + 4096, 2048).rearrange("p (k f) -> p k f", k=2)
        oaT = at(B_OAT, 2048).rearrange("p (k t) -> p k t", k=4)
        obT = at(B_OAT + 2048, 1024).rearrange("p (k t) -> p k t", k=2)
        ogn = [og[0]] + [at(B_OGN + 1056 * i, 1056).rearrange("p (n f) -> p n f", n=NT) for i in range(2)]
        prod = [at(B_TMP + 1024 * i, 1024).rearrange("p (n f) -> p n f", n=NT) for i in range(2)]
        merged = at(A_HT, 4096).rearrange("p (k t) -> p k t", k=KD)
        wo = at(B_WO, 8192).rearrange("p (k f) -> p k f", k=KD)
        x2 = at(B_X, 4096).rearrange("p (n d) -> p n d", n=NT)
        xs = at(C_XS, 4096).rearrange("p (n d) -> p n d", n=NT)
        ytmp = [at(B_OGN + 512 * i, 512) for i in range(4)]
        h2T = at(C_H2T, 4096).rearrange("p (k t) -> p k t", k=KD)
        ysh = at(C_YSH, 4096).rearrange("p (n d) -> p n d", n=NT)
        wgu = [at(SLOT[i], 4096).rearrange("p (a k f) -> p a k f", a=2, k=KD) for i in range(4)]
        wd = [at(SLOT[i] + 4096, 2048).rearrange("p (k f) -> p k f", k=2) for i in range(4)]
        sh_act = at(C_Y, 1024).rearrange("p (m t) -> p m t", m=2)
        sh_tmp = at(C_Y + 1024, 1024).rearrange("p (m t) -> p m t", m=2)
        ysb = [at((C_Y if i < 2 else C_H2T) + 1024 * i, 1024) for i in range(4)]
        onehot = [at(C_OH + 256 * i, 256).bitcast(BF16).rearrange("p (n s) -> p n s", n=NT) for i in range(2)]
        aT = [at(C_AT + 256 * i, 256).rearrange("p (k s) -> p k s", k=2) for i in range(2)]
        th = [at(C_ACT + 768 * i, 256) for i in range(2)]
        gth = [at(C_ACT + 768 * i + 256, 256) for i in range(2)]
        act_t = [at(C_ACT + 768 * i + 512, 256) for i in range(2)]
        xg = [at(C_XG + 1024 * i if i < 2 else C_H2T + 1024 * (i - 2), 1024) for i in range(4)]
        hTs = [at(C_HTS + 1024 * i, 1024).rearrange("p (k s) -> p k s", k=KD) for i in range(2)]
        pairs = [at(8192 * i, 8192).rearrange("p (q d) -> p q d", q=TOPK) for i in range(PBUF)]
        fin = at(C_XG, 4096).rearrange("p (n d) -> p n d", n=NT)

        gt1 = sb("gt1", [P, D])
        gt2 = sb("gt2", [P, D])
        gfin = gt1
        ident = sb("ident", [P, P])
        flip = sb("flip", [P, P])
        ones = sb("ones", [P, P])
        zero16 = sb("zero16", [1, RPAD])
        c_col = sb("c_col", [P, KD])
        c_th = sb("c_th", [P, KD])
        c_act = sb("c_act", [P, KD])
        bada = sb("bada", [P, 6, KD])
        gmix = sb("gmix", [P, KD])
        gffn = sb("gffn", [P, KD])
        modc = sb("modc", [P, 6, KD])
        a1 = sb("a1", [P, KD])
        a2 = sb("a2", [P, KD])
        bg_rows = sb("bg_rows", [16, P])
        bg_half = sb("bg_half", [P, 16])
        ss = sb("ss", [P, NT])
        rs = sb("rs", [P, NT])
        var = sb("var", [P, NT])
        rt = sb("rt", [P, NT])
        nm_na = sb("nm_na", [P, NAH, NT])
        z_na = sb("z_na", [P, NAH, NT])
        rz_na = sb("rz_na", [P, NAH, NT])
        part_i = sb("part_i", [P, 2], I32)
        cl = sb("cl", [P, 2])
        win = sb("win", [P, NT, 2])
        shared = sb("shared", [P, 1152])
        col_i = shared[:, 0:384].bitcast(I32)
        col_f = shared[:, 384:768]
        nmask = sb("nmask", [P, NT, 48])
        mtmp = shared[:, 768:1152]
        dist = [sb(f"dist{g}", [P, 384 if g == 0 else P]) for g in range(NG)]
        lse = sb("lse", [P, 8, NT, GH])
        wr = at(C_WR, 512).rearrange("p (k e) -> p k e", k=KD)
        ebias = sb("ebias", [P, NE])
        score = at(C_ACT, 256).rearrange("p (n e) -> p n e", n=NT)
        biased = at(C_ACT + 256, 256).rearrange("p (n e) -> p n e", n=NT)
        grp8 = at(C_ACT + 512, 256).rearrange("p (n e) -> p n e", e=8)
        grp = sb("grp", [P, NT, NGRP])
        cmp = at(C_ACT + 768, 256).rearrange("p (n g h) -> p n g h", n=NT, g=NGRP)
        cmq = at(C_ACT + 1024, 256).rearrange("p (n g h) -> p n g h", n=NT, g=NGRP)
        before = sb("before", [P, NGRP, NGRP])
        gsel = sb("gsel", [P, NT, NGRP])
        gpen = sb("gpen", [P, NT, NGRP])
        top8 = sb("top8", [P, NT, 8])
        sel = at(C_OH, 256).rearrange("p (n e) -> p n e", n=NT)
        selb = at(C_AT, 128).bitcast(BF16).rearrange("p (n e) -> p n e", n=NT)
        wt = at(C_ACT + 1280, 256).rearrange("p (n e) -> p n e", n=NT)
        wsum = sb("wsum", [P, NT])
        kth = at(C_OH + 256, 256).rearrange("p (n e) -> p n e", n=NT)
        posm = sb("posm", [P, NT, NE])
        rhs9 = shared[:, :].bitcast(BF16).rearrange("p (n e c a) -> p n e c a", n=NT, e=NE, c=3)
        tri = sb("tri", [P, P], BF16)
        onesb = sb("onesb", [P, P], BF16)
        slot_id = at(C_WR + 512, 640).rearrange("p (b s) -> p b s", b=5)
        info = sb("info", [P, NE + OVF, 3])
        idx_t = sb("idx_t", [P, 4, 1], U32)
        idx_r = sb("idx_r", [P, 4, 1], U32)
        cnt_e = sb("cnt_e", [NE, 1])
        eval_ = sb("eval_", [NE, 4])
        ovf = sb("ovf", [NE, 3])
        ovfb = sb("ovfb", [NE, 3], BF16)
        ovr = sb("ovr", [NE, 3])
        ov1h = sb("ov1h", [NE, 3, 32])
        ovlist = sb("ovlist", [1, 96], U32)

        bank = [ctx.enter_context(nc.psum_tensor(f"bank{i}", [P, 512], F32)) for i in range(8)]
        ps_proj, ps_s, ps_t, ps_o = bank[0:2], bank[2:4], bank[4:6], bank[6:8]

        s_small = sem("s_small")
        s_rows = sem("s_rows")
        s_bg = sem("s_bg")
        s_x = sem("s_x")
        s_ada0 = [sem(f"s_ada0_{k}") for k in range(KD)]
        s_adar = [sem(f"s_adar_{k}") for k in range(2)]
        s_pad = sem("s_pad")
        s_btr = sem("s_btr")
        s_w = [sem(f"s_w_{i}") for i in range(WSLOTS)]
        s_dil = sem("s_dil")
        s_ogn = sem("s_ogn")
        s_wp = sem("s_wp")
        s_wo = sem("s_wo")
        s_xr = sem("s_xr")
        s_wsh = sem("s_wsh")
        s_wr = sem("s_wr")
        s_gfin = sem("s_gfin")
        s_wgu = [sem(f"s_wgu_{i}") for i in range(4)]
        s_wd = [sem(f"s_wd_{i}") for i in range(4)]
        s_xn = sem("s_xn")
        s_gather = [sem(f"s_gather_{i}") for i in range(4)]
        s_scatter = [sem(f"s_scatter_{i}") for i in range(4)]
        s_pair = [[sem(f"s_pair_{i}_{j}") for j in range(PBUF)] for i in range(2)]
        s_out = sem("s_out")
        pool_c = sem("pool_c")
        sp_seq = sem("sp_seq")
        pool_seq = sem("pool_seq")
        pool_bias = sem("pool_bias")
        dve_c = sem("dve_c")
        act_c = sem("act_c")
        dve_one = sem("dve_one")
        dve_tab = sem("dve_tab")
        dve_ada = sem("dve_ada")
        dve_rs = sem("dve_rs")
        dve_var = sem("dve_var")
        act_ss = sem("act_ss")
        act_sd = sem("act_sd")
        act_cth = sem("act_cth")
        act_xs = sem("act_xs")
        dve_mod = sem("dve_mod")
        act_bt = sem("act_bt")
        pe_bt = sem("pe_bt")
        pe_mod = sem("pe_mod")
        pe_xT = sem("pe_xT")
        act_hT = sem("act_hT")
        dve_hT = sem("dve_hT")
        pe_unit = sem("pe_unit")
        act_ev = sem("act_ev")
        dve_ev = sem("dve_ev")
        act_gate = sem("act_gate")
        pe_vT = sem("pe_vT")
        act_vout = sem("act_vout")
        dve_vout = sem("dve_vout")
        pe_s = sem("pe_s")
        dve_ttr = sem("dve_ttr")
        act_exp = sem("act_exp")
        pe_t = sem("pe_t")
        dve_pt = sem("dve_pt")
        pe_pv = sem("pe_pv")
        dve_o = sem("dve_o")
        act_lse = sem("act_lse")
        dve_lse = sem("dve_lse")
        dve_ob = sem("dve_ob")
        pe_oT = sem("pe_oT")
        act_oT = sem("act_oT")
        dve_oT = sem("dve_oT")
        pe_y = sem("pe_y")
        dve_m = sem("dve_m")
        pe_wo = sem("pe_wo")
        dve_u = sem("dve_u")
        pe_h2 = sem("pe_h2")
        act_h2 = sem("act_h2")
        dve_h2 = sem("dve_h2")
        pe_rt = sem("pe_rt")
        act_rt = sem("act_rt")
        dve_sel = sem("dve_sel")
        dve_tabs = sem("dve_tabs")
        dve_ovf = sem("dve_ovf")
        dve_list = sem("dve_list")
        pe_sh = sem("pe_sh")
        act_sh = sem("act_sh")
        dve_sh = sem("dve_sh")
        act_ysh = sem("act_ysh")
        dve_ysh = sem("dve_ysh")
        dve_zx = sem("dve_zx")
        dve_oh = sem("dve_oh")
        pe_info = sem("pe_info")
        dve_info = sem("dve_info")
        dve_idx = sem("dve_idx")
        pe_ht = sem("pe_ht")
        act_ht = sem("act_ht")
        dve_ht = sem("dve_ht")
        pe_gu = sem("pe_gu")
        act_th = sem("act_th")
        dve_g = sem("dve_g")
        dve_act = sem("dve_act")
        pe_at = sem("pe_at")
        dve_at = sem("dve_at")
        pe_dn = sem("pe_dn")
        act_y = sem("act_y")
        dve_y = sem("dve_y")
        dve_idr = sem("dve_idr")
        dve_sum = sem("dve_sum")
        pe_sum = sem("pe_sum")
        act_fss = sem("act_fss")
        act_fsd = sem("act_fsd")
        dve_fv = sem("dve_fv")
        dve_fin = sem("dve_fin")

        block = ctx.enter_context(nc.Block())

        def bview(src, off, dims):
            return bass.AP(tensor=src.tensor, offset=src.offset + off, ap=[list(src.ap[0])] + dims)

        def unit_places(u):
            if u < QK_UNITS:
                dst = qkt[:, u, :]
                g = -1 if u < 8 else (u - 8) % 6 // 2
            else:
                dst = vT[u % VSTAGE]
                g = -1 if u < QK_UNITS + 4 else (u - QK_UNITS - 4) // 2
            if g < 0:
                return dst.rearrange("p (t r c) -> p r t c", t=NT, r=ROWS), \
                    (lambda a: a.rearrange("p (r t c) -> p r t c", t=NT, r=ROWS))
            if g == 0:
                return dst, lambda a: a
            return dst.rearrange("p (r u) -> p u r", r=DIL[g]), lambda a: a.rearrange("p (u r) -> p u r", r=DIL[g])

        xt = x[0].rearrange("(n p) d -> p n d", p=P)
        NJ = len(JOBS)

        @block.sync
        def _(sp):
            def ada_src(part, k):
                return w_ada[0].rearrange("(p k) n -> p k n", k=KD)[:, k, 2048 * part:2048 * (part + 1)]

            sp.dma_start(c_col[:], c.rearrange("a (p k) -> (a p) k", k=KD)).then_inc(s_small, 16)
            sp.dma_start(bada[:], b_ada[0].rearrange("(s p k) -> p s k", s=6, k=KD)).then_inc(s_small, 16)
            sp.dma_start(gmix[:], g_mix[0].rearrange("(p k) -> p k", k=KD)).then_inc(s_small, 16)
            sp.dma_start(gffn[:], g_ffn[0].rearrange("(p k) -> p k", k=KD)).then_inc(s_small, 16)
            sp.dma_start(x_first, xt).then_inc(s_x, 16)
            for k in range(KD):
                sp.dma_start(ada_first[k], ada_src(0, k)).then_inc(s_ada0[k], 16)
            sp.dma_start(bg_rows[:], b_gate[0].rearrange("(m p) -> m p", p=P)).then_inc(s_bg, 16)

            def w_chunk(i):
                if i >= WSLOTS:
                    sp.wait_ge(pe_unit, 2 * (i - WSLOTS + 1))
                src = w_in[0].rearrange("(p k) n -> p k n", k=KD)[:, :, CHUNKS[i]:CHUNKS[i] + CW]
                sp.dma_start(wbuf[i % WSLOTS], src).then_inc(s_w[i % WSLOTS], 16)

            def ada_chunk(j):
                if j != 1:
                    sp.wait_ge(dve_ada, KD if j == 0 else KD + j - 1)
                sp.dma_start(ada_ring[j % 2], ada_src(1 + j // KD, j % KD)).then_inc(s_adar[j % 2], 16)

            for i in range(WSLOTS):
                w_chunk(i)
            ada_chunk(0)
            ada_chunk(1)
            sp.dma_start(gt1[:], b_ada[0, 2 * D:3 * D].partition_broadcast(P)).then_inc(s_rows, 16)
            sp.dma_start(gt2[:], b_ada[0, 5 * D:6 * D].partition_broadcast(P)).then_inc(s_rows, 16)
            sp.dma_start(ebias[:], e_bias[0].partition_broadcast(P)).then_inc(s_rows, 16)
            for i in range(WSLOTS, len(CHUNKS)):
                w_chunk(i)
                for j in range(2 * (i - WSLOTS + 1), min(2 * (i - WSLOTS + 2), ADA_CHUNKS)):
                    ada_chunk(j)
                if i == 18:
                    sp.wait_ge(dve_o, 2 * GH)
                    sp.dma_start(dil_dram[0].rearrange("(p r) f -> p r f", r=4), og[1]).then_inc(s_dil, 16)
                    d2 = dil_dram[1].rearrange("(u t r) f -> r u t f", t=NT, r=4)
                    for r in range(4):
                        sp.dma_start(d2[r], og[2][32 * r:32 * r + 32, :, :]).then_inc(s_dil, 16)
            sp.wait_ge(s_dil, 80)
            sp.wait_ge(pe_pv, NJ)
            for i in range(2):
                sp.dma_start(ogn[1 + i], dil_dram[i].rearrange("(n p) f -> p n f", p=P)).then_inc(s_ogn, 16)
            sp.dma_start(wpa, w_pa[0].rearrange("(k p) f -> p k f", p=P)).then_inc(s_wp, 16)
            sp.dma_start(wpb, w_pb[0].rearrange("(k p) f -> p k f", p=P)).then_inc(s_wp, 16)
            sp.wait_ge(pe_unit, UNITS + GATE_UNITS)
            sp.dma_start(wo, w_o[0].rearrange("(k p) f -> p k f", p=P)).then_inc(s_wo, 16)
            sp.dma_start(x2, xt).then_inc(s_xr, 16)

            def w_expert(e, k, reused):
                gate = we_gate[0, e] if isinstance(e, int) else we_gate[0, bass.ds(e, 1)].rearrange("a d f -> (a d) f")
                up = we_up[0, e] if isinstance(e, int) else we_up[0, bass.ds(e, 1)].rearrange("a d f -> (a d) f")
                down = we_down[0, e] if isinstance(e, int) else we_down[0, bass.ds(e, 1)].rearrange("a d f -> (a d) f")
                if reused is not None:
                    sp.wait_ge(pe_gu, reused)
                sp.dma_start(wgu[k][:, 0], gate.rearrange("(p k) f -> p k f", k=KD)).then_inc(s_wgu[k], 16)
                sp.dma_start(wgu[k][:, 1], up.rearrange("(p k) f -> p k f", k=KD)).then_inc(s_wgu[k], 16)
                if reused is not None:
                    sp.wait_ge(pe_dn, reused)
                sp.dma_start(wd[k], down.rearrange("(p k) f -> p k f", k=2)).then_inc(s_wd[k], 16)

            sp.wait_ge(dve_ob, 1)
            sp.dma_start(wr, w_router[0].rearrange("(p k) e -> p k e", k=KD)).then_inc(s_wr, 16)
            sp.wait_ge(pe_y, KD)
            sp.wait_ge(dve_m, 3 * KD)
            sp.dma_start(wgu[3][:, 0], ws_gate[0].rearrange("(p k) f -> p k f", k=KD)).then_inc(s_wsh, 16)
            sp.dma_start(wgu[3][:, 1], ws_up[0].rearrange("(p k) f -> p k f", k=KD)).then_inc(s_wsh, 16)
            sp.dma_start(wd[3], ws_down[0].rearrange("(k p) f -> p k f", p=P)).then_inc(s_wsh, 16)
            w_expert(0, 0, None)
            sp.wait_ge(pe_wo, 2 * NT)
            sp.wait_ge(dve_u, 4 * NT)
            sp.dma_start(gfin[:], g_final.partition_broadcast(P)).then_inc(s_gfin, 16)
            w_expert(1, 1, None)
            for n in range(NT):
                sp.wait_ge(act_xs, NT + n + 1)
                sp.dma_start(xn_dram[n * P:(n + 1) * P, :], xs[:, n, :]).then_inc(s_xn, 16)
            w_expert(2, 2, None)
            sp.wait_ge(pe_sh, 4 + 2 * NT)
            w_expert(3, 3, None)
            with sp.Fori(1, NE // 4) as i:
                for k in range(4):
                    w_expert(4 * i + k, k, 4 * i + k - 3)
            sp.wait_ge(dve_list, 1)
            for k in range(OVF):
                e = sp.value_load(ovlist[0:1, k:k + 1], min_val=0, max_val=NE - 1)
                w_expert(e, k, NE - 4 + k + 1)
            passes = sp.value_load(ovlist[0:1, 65:66], min_val=0, max_val=16)
            with sp.If(passes > 0):
                with sp.Fori(0, passes) as i:
                    for k in range(OVF):
                        e = sp.value_load(ovlist[0:1, bass.ds(2 * i + 2 + k, 1)], min_val=0, max_val=NE - 1)
                        w_expert(e, k, NE + 2 * i + k + 1)
            for k in range(OVF):
                sp.wait_ge(s_scatter[k], passes * 16 + NE // 4 * 16)
                sp.sem_inc(sp_seq, 1)
            for k in range(OVF):
                sp.wait_ge(s_wd[k], passes * 16 + (NE // 4 + 1) * 16)
                sp.sem_inc(sp_seq, 1)
                sp.wait_ge(s_wgu[k], passes * 32 + (NE // 4 + 1) * 32)
                sp.sem_inc(sp_seq, 1)
            for k in range(OVF, 4):
                sp.wait_ge(s_scatter[k], NE // 4 * 16)
            for n in range(NT):
                if n >= PBUF:
                    sp.wait_ge(pe_sum, n - PBUF + 1)
                    sp.wait_ge(dve_sum, 4 * (n - PBUF) + 1)
                src = pair_dram[n * P * TOPK:(n + 1) * P * TOPK, :].rearrange("(p q) d -> p q d", q=TOPK)
                for i in (1, 0):
                    sp.dma_start(pairs[n % PBUF][:, :, 512 * i:512 * i + 512],
                                 src[:, :, 512 * i:512 * i + 512]).then_inc(s_pair[i][n % PBUF], 16)
            for n in range(NT):
                sp.wait_ge(dve_fin, n + 1)
                sp.dma_start(out[0, n * P:(n + 1) * P, :], fin[:, n, :]).then_inc(s_out, 16)
            sp.wait_ge(s_out, 16 * NT)

        @block.gpsimd
        def _(pool):
            pool.memset(ident[:], 0.0).then_inc(pool_c, 1)
            pool.memset(flip[:], 0.0).then_inc(pool_c, 1)
            pool.wait_ge(pool_c, 2)
            pool.affine_select(out=ident[:], in_=ident[:], compare_op=ALU.not_equal, fill=1.0, base=0,
                               pattern=[[-1, P]], channel_multiplier=1).then_inc(pool_c, 1)
            pool.affine_select(out=flip[:], in_=flip[:], compare_op=ALU.not_equal, fill=1.0, base=1 - P,
                               pattern=[[1, P]], channel_multiplier=1).then_inc(pool_c, 1)
            pool.iota(part_i[:, 0:1], pattern=[[0, 1]], base=0, channel_multiplier=1).then_inc(pool_c, 1)
            pool.iota(col_i, pattern=[[1, 384]], base=0, channel_multiplier=0).then_inc(pool_c, 1)
            pool.memset(tri[:], 1.0).then_inc(pool_c, 1)
            pool.memset(before[:], 1.0).then_inc(pool_c, 1)
            pool.wait_ge(pool_c, 8)
            pool.affine_select(out=tri[:], in_=tri[:], compare_op=ALU.is_gt, fill=0.0, base=0,
                               pattern=[[1, P]], channel_multiplier=-1).then_inc(pool_c, 1)
            pool.affine_select(out=before[:], in_=before[:], compare_op=ALU.is_gt, fill=0.0, base=0,
                               pattern=[[1, NGRP], [-1, NGRP]], channel_multiplier=0).then_inc(pool_c, 1)
            pool.memset(onesb[:], 1.0).then_inc(pool_c, 1)

            done = -1
            pool.wait_ge(dve_tab, 4)
            pool.wait_ge(act_bt, 7)
            pool.wait_ge(pe_mod, 3)
            for j, (kind, g, h, t) in enumerate(JOBS):
                u = BIAS_OF[j]
                if u == done:
                    continue
                done = u
                if u >= 3:
                    pool.wait_ge(dve_ttr, last_of(BIAS_OF, u - 3) + 1)
                if kind == "na":
                    w = 16 * len(NEAR[t])
                    off = RPAD + 16 * NEAR[t][0] - 16 * t + h * RPBH
                    pool.tensor_tensor(bias[u % 3][:, 0:ROWS * w].rearrange("p (j r c) -> p j r c", r=ROWS, c=16),
                                       bview(bt8, off, [[16, w // 16], [RPBW, ROWS], [1, 16]]),
                                       bview(nmask[:, t, :], 0, [[16, w // 16], [0, ROWS], [1, 16]]),
                                       ALU.add).then_inc(pool_bias, 1)
                else:
                    w = 384 if kind == "band" else P
                    pool.tensor_scalar(bias[u % 3][:, 0:w], dist[g][:, 0:w], -SLOPES[g * GH + h] / SCALE, None,
                                       ALU.mult).then_inc(pool_bias, 1)

            pool.wait_ge(dve_ob, 1)
            pool.iota(slot_id[:, 0, :], pattern=[[1, P]], base=4 * P,
                      channel_multiplier=0, allow_small_or_imprecise_dtypes=True).then_inc(pool_c, 1)
            pool.iota(slot_id[:, 1:4, :].rearrange("p b s -> p (b s)"), pattern=[[1, 3 * P]], base=P,
                      channel_multiplier=0, allow_small_or_imprecise_dtypes=True).then_inc(pool_c, 1)
            pool.iota(slot_id[:, 4, :], pattern=[[1, P]], base=0,
                      channel_multiplier=0, allow_small_or_imprecise_dtypes=True).then_inc(pool_c, 1)
            pool.memset(rhs9[:, :, :, 0, 2], 0.0).then_inc(pool_c, 1)
            for n in range(NT):
                pool.iota(rhs9[:, n, :, 0, 0], pattern=[[0, NE]], base=0, channel_multiplier=1,
                          allow_small_or_imprecise_dtypes=True).then_inc(pool_c, 1)
                pool.iota(rhs9[:, n, :, 1, 0], pattern=[[0, NE]], base=0, channel_multiplier=TOPK,
                          allow_small_or_imprecise_dtypes=True).then_inc(pool_c, 1)
                pool.memset(rhs9[:, n, :, 0, 1], 128.0 * n - 1024.0).then_inc(pool_c, 1)
                pool.memset(rhs9[:, n, :, 1, 1], 1024.0 * n - 8192.0).then_inc(pool_c, 1)

            last_token, last_pair = pool.to_reg(S - 1), pool.to_reg(S * TOPK - 1)

            def gather(n, k):
                pool.wait_ge(dve_idx, n + 1)
                pool.sem_inc(pool_seq, 1)
                pool.indirect_dma_start(xg[k], None, xn_dram,
                                        bass.IndirectOffsetOnAxis(ap=idx_t[:, k, :], axis=0),
                                        bounds_check=last_token, oob_is_err=False).then_inc(s_gather[k], 16)

            def scatter(n, k):
                pool.wait_ge(act_y, n + 1)
                pool.wait_ge(dve_y, n + 1)
                pool.sem_inc(pool_seq, 1)
                pool.indirect_dma_start(pair_dram, bass.IndirectOffsetOnAxis(ap=idx_r[:, k, :], axis=0), ysb[k], None,
                                        bounds_check=last_pair, oob_is_err=False).then_inc(s_scatter[k], 16)

            def body(e, k):
                if not isinstance(e, int) or e + AHEAD < NE + OVF:
                    gather(e + AHEAD, k)
                scatter(e, k)

            pool.wait_ge(s_xn, 16 * NT)
            for e in range(AHEAD):
                pool.wait_ge(dve_zx, e + 1)
                gather(e, e)
            for e in range(4):
                body(e, e)
            with pool.Fori(1, NE // 4 - 1) as i:
                for k in range(4):
                    body(4 * i + k, k)
            for e in range(NE - 4, NE):
                body(e, e % 4)
            passes = pool.value_load(ovlist[0:1, 65:66], min_val=0, max_val=16)
            with pool.If(passes > 0):
                with pool.Fori(0, passes) as i:
                    for k in range(OVF):
                        scatter(NE + 2 * i + k, k)
                        gather(NE + 2 * i + 2 + k, k)

        @block.scalar
        def _(act):
            act.wait_ge(dve_one, 2)
            act.dma_start(rpb_pad[0:RPAD], zero16[0, :]).then_inc(s_pad, 16)
            act.dma_start(rpb_pad[RPAD + NAH * RPBH:], zero16[0, :]).then_inc(s_pad, 16)
            act.dma_start(rpb_pad[RPAD:RPAD + NAH * RPBH], rpb[0].rearrange("h a b -> (h a b)")).then_inc(s_pad, 16)
            act.wait_ge(s_pad, 48)
            for r in range(ROWS):
                act.dma_start(bt_rev[16 * r:16 * r + 16, :],
                              bass.AP(tensor=rpb_pad.tensor, offset=rpb_pad.offset + RPBW * r,
                                      ap=[[1, 16], [1, BT]])).then_inc(s_btr, 16)
            act.wait_ge(s_small, 64)
            act.activation(c_th[:], c_col[:], ACT.Tanh, scale=0.5).then_inc(act_cth, 1)

            def sum_squares(src, junk, n, done):
                act.activation(junk, src, ACT.Square, accum_out=ss[:, n:n + 1]).then_inc(done, 1)

            act.wait_ge(s_x, 16)
            for n in range(NT):
                sum_squares(x_first[:, n, :], at(A_HT + 1024 * n, 1024), n, act_ss)
            act.wait_ge(dve_var, 1)
            act.activation(rt[:], var[:], ACT.Sqrt).then_inc(act_sd, 1)
            act.wait_ge(dve_rs, 1)
            for n in range(NT):
                act.activation(x_first[:, n, :], x_first[:, n, :], ACT.Copy,
                               scale=rs[:, n:n + 1]).then_inc(act_xs, 1)
            act.wait_ge(dve_mod, 1)
            for k in range(0, KD, 2):
                act.wait_ge(pe_xT, k + 1)
                act.activation(hT[:, k, :], bank[XT_BANK[k]][:, :], ACT.Identity, bias=modc[:, 0, k:k + 1],
                               scale=a1[:, k:k + 1]).then_inc(act_hT, 1)

            def unit_out(u):
                act.wait_ge(pe_unit, u + 1)
                if u >= QK_UNITS + VSTAGE:
                    act.wait_ge(pe_vT, u - QK_UNITS - VSTAGE + 1)
                dst, of = unit_places(u)
                act.copy(dst, of(ps_proj[0][:, :])).then_inc(act_ev, 1)

            def v_out(f):
                act.wait_ge(pe_vT, f + 1)
                act.copy(vbuf[:, :, P * f:P * f + P],
                         bank[2 + f % 2][:, :].rearrange("p (n f) -> p n f", n=NT)).then_inc(act_vout, 1)

            for u in range(0, UNITS, 2):
                unit_out(u)
                if u == BT_UNIT:
                    for i in range(7):
                        act.wait_ge(pe_bt, i + 1)
                        w = min(512, BT - 512 * i)
                        act.activation(bt8[:, 512 * i:512 * i + w], bank[2 + i % 6][:, 0:w], ACT.Copy,
                                       scale=1.0 / SCALE).then_inc(act_bt, 1)
                if u >= QK_UNITS + 2:
                    v_out(u - QK_UNITS - 2)
            v_out(V_UNITS - 2)

            def gate_out(m):
                act.wait_ge(pe_unit, UNITS + m + 1)
                if m == 0:
                    act.wait_ge(dve_mod, 3)
                act.activation(gates[:, m, :], ps_proj[m % 2][:, :], ACT.Tanh, bias=bg_half[:, m:m + 1],
                               scale=0.5).then_inc(act_gate, 1)

            gate = 0
            for i, (kind, g, h, t) in enumerate(JOBS):
                act.wait_ge(dve_ttr, i + 1)
                if i >= 2:
                    act.wait_ge(pe_t, i - 1)
                if kind == "group":
                    for q in range(NT):
                        w = slice(P * q, P * q + P)
                        ins = act.activation(prob[i % 2][:, w], sneg[i % 2][:, w], ACT.Exp, scale=-1.0,
                                             bias=og[g][:, q, 256 + h:257 + h],
                                             accum_out=og[g][:, q, 260 + h:261 + h])
                else:
                    w = P * len(NEAR[t])
                    nm = og[0][:, t, 256 + h:257 + h] if kind == "band" else nm_na[:, h, t:t + 1]
                    z = og[0][:, t, 260 + h:261 + h] if kind == "band" else z_na[:, h, t:t + 1]
                    ins = act.activation(prob[i % 2][:, 0:w], sneg[i % 2][:, 0:w], ACT.Exp, scale=-1.0,
                                         bias=nm, accum_out=z)
                ins.then_inc(act_exp, 1)
                while gate < GATE_UNITS - 2 and 8 * (gate + 1) <= FILL * i:
                    gate_out(gate)
                    gate += 1
            act.wait_ge(dve_lse, NG)
            act.activation(lse[:, 0:3], lse[:, 4:7], ACT.Exp).then_inc(act_lse, 1)
            while gate < GATE_UNITS:
                gate_out(gate)
                gate += 1
            for k in range(4):
                act.wait_ge(pe_oT, k + 1)
                src = bank[2 + k][:, :].rearrange("p (t r c) -> p t r c", t=NT, r=ROWS)
                dst = oaT[:, k, :].rearrange("p (r t c) -> p t r c", t=NT, r=ROWS)
                act.copy(dst, src).then_inc(act_oT, 1)
            for n in range(NT):
                act.wait_ge(dve_u, 4 * n + 4)
                sum_squares(x2[:, n, :], xs[:, n, :], n, act_ss)
                act.wait_ge(dve_var, 2 + n)
                act.activation(rt[:, n:n + 1], var[:, n:n + 1], ACT.Sqrt).then_inc(act_sd, 1)
                act.wait_ge(dve_rs, 2 + n)
                act.wait_ge(act_ss, NT + n + 1)
                act.activation(xs[:, n, :], x2[:, n, :], ACT.Copy, scale=rs[:, n:n + 1]).then_inc(act_xs, 1)
            for k in range(0, KD, 2):
                act.wait_ge(pe_h2, k + 1)
                act.activation(h2T[:, k, :], bank[k % 4][:, :], ACT.Identity, bias=modc[:, 3, k:k + 1],
                               scale=a2[:, k:k + 1]).then_inc(act_h2, 1)
            act.wait_ge(pe_rt, 1)
            act.activation(score.rearrange("p n e -> p (n e)"), bank[7][:, 0:NT * NE], ACT.Exp,
                           scale=-1.0).then_inc(act_rt, 1)
            for m in range(2):
                act.wait_ge(pe_sh, 2 * m + 1)
                act.activation(sh_tmp[:, m, :], bank[2 * m][:, :], ACT.Tanh, scale=0.5).then_inc(act_sh, 1)

            def shared_out(u):
                act.wait_ge(pe_sh, 4 + u + 1)
                act.activation(ysh[:, u // 2, 0:512], bank[2 + u % 4][:, :], ACT.Copy, scale=0.5).then_inc(act_ysh, 1)

            def rows_out(n, b):
                act.wait_ge(pe_ht, n + 1)
                for k in range(4):
                    ins = act.activation(hTs[b][:, k, :], bank[0][:, P * k:P * k + P], ACT.Identity,
                                         bias=modc[:, 3, k:k + 1], scale=a2[:, k:k + 1])
                ins.then_inc(act_ht, 1)

            def tanh(n, b):
                act.wait_ge(pe_gu, n + 1)
                act.activation(th[b], bank[2 + b][:, 0:FE], ACT.Tanh, scale=0.5).then_inc(act_th, 1)

            def y_out(n, k, e, scattered):
                act.wait_ge(pe_dn, n + 1)
                if scattered is not None:
                    act.wait_ge(s_scatter[k], scattered)
                w = info[:, e, 2:3] if isinstance(e, int) else info[:, bass.ds(e, 1), 2:3].rearrange("p a b -> p (a b)")
                act.activation(ysb[k][:, 0:512], bank[4][:, :], ACT.Copy, scale=w).then_inc(act_y, 1)

            def body(e, k, i):
                tanh(e, k % 2)
                if not isinstance(e, int) or e + 2 < NE + OVF:
                    rows_out(e + 2, k % 2)
                y_out(e, k, e, None if isinstance(e, int) and e < 4 else 16 * i)

            for b in range(2):
                rows_out(b, b)
                shared_out(4 * b)
                shared_out(4 * b + 2)
            for e in range(4):
                body(e, e, 0)
            with act.Fori(1, NE // 4 - 1) as i:
                for k in range(4):
                    body(4 * i + k, k, i)
            for e in range(NE - 4, NE):
                body(e, e % 4, NE // 4 - 1)
            passes = act.value_load(ovlist[0:1, 65:66], min_val=0, max_val=16)
            with act.If(passes > 0):
                with act.Fori(0, passes) as i:
                    for k in range(OVF):
                        tanh(NE + 2 * i + k, k)
                    for k in range(OVF):
                        y_out(NE + 2 * i + k, k, NE + k, i * 16 + NE // 4 * 16)
                    for k in range(OVF):
                        rows_out(NE + 2 * i + 2 + k, k)
            for n in range(NT):
                act.wait_ge(dve_sum, 4 * n + 4)
                act.activation(ysh[:, n, :], fin[:, n, :], ACT.Square, accum_out=ss[:, n:n + 1]).then_inc(act_fss, 1)
                act.wait_ge(dve_fv, n + 1)
                act.activation(rt[:, n:n + 1], var[:, n:n + 1], ACT.Sqrt).then_inc(act_fsd, 1)

        @block.vector
        def _(dve):
            steps = [0]

            def link(ins):
                steps[0] += 1
                ins.then_inc(dve_c, 1)
                dve.wait_ge(dve_c, steps[0])

            dve.memset(ones[:], 1.0).then_inc(dve_one, 1)
            dve.memset(zero16[:], 0.0).then_inc(dve_one, 1)

            dve.wait_ge(pool_c, 6)
            link(dve.tensor_copy(col_f, col_i))
            link(dve.tensor_copy(cl[:, 0:1], part_i[:, 0:1]))
            link(dve.tensor_scalar(mtmp, col_f, cl[:, 0:1], -float(P), ALU.subtract, ALU.add))
            link(dve.tensor_scalar(dist[0][:], mtmp, -1.0, None, ALU.mult))
            link(dve.tensor_tensor(dist[0][:], dist[0][:], mtmp, ALU.max))
            link(dve.tensor_scalar(mtmp, dist[0][:], RADIUS + 0.5, BIG, ALU.is_gt, ALU.mult))
            link(dve.tensor_scalar(dist[1][:], dist[0][:, P:2 * P], float(DIL[1]), None, ALU.mult))
            link(dve.tensor_tensor(dist[1][:], dist[1][:], mtmp[:, P:2 * P], ALU.add))
            link(dve.tensor_scalar(dist[2][:], dist[0][:, P:2 * P], float(DIL[2]), None, ALU.mult))
            dve.tensor_tensor(dist[0][:], dist[0][:], mtmp, ALU.add).then_inc(dve_tab, 1)
            link(dve.tensor_single_scalar(part_i[:, 1:2], part_i[:, 0:1], 5, ALU.logical_shift_right))
            link(dve.tensor_copy(cl[:, 1:2], part_i[:, 1:2]))
            link(dve.tensor_single_scalar(col_i[:, 0:P], col_i[:, 0:P], 5, ALU.logical_shift_right))
            link(dve.tensor_copy(mtmp[:, 0:P], col_i[:, 0:P]))
            link(dve.tensor_scalar(mtmp[:, 0:P], mtmp[:, 0:P], cl[:, 1:2], BIG, ALU.not_equal, ALU.mult))
            dve.tensor_tensor(dist[2][:], dist[2][:], mtmp[:, 0:P], ALU.add).then_inc(dve_tab, 1)
            link(dve.tensor_single_scalar(part_i[:, 1:2], part_i[:, 0:1], 15, ALU.bitwise_and))
            link(dve.tensor_copy(cl[:, 1:2], part_i[:, 1:2]))
            for t in range(NT):
                link(dve.tensor_scalar(win[:, t, 0:1], cl[:, 1:2], 16.0 * t - WC // 2, 0.0, ALU.add, ALU.max))
                link(dve.tensor_scalar(win[:, t, 0:1], win[:, t, 0:1], float(GRID - WC), -16.0 * NEAR[t][0],
                                       ALU.min, ALU.add))
                link(dve.tensor_scalar(win[:, t, 1:2], win[:, t, 0:1], float(WC), None, ALU.add))
                link(dve.tensor_scalar(nmask[:, t, :], col_f[:, 0:48], win[:, t, 0:1], None, ALU.is_ge))
                link(dve.tensor_scalar(mtmp[:, 0:48], col_f[:, 0:48], win[:, t, 1:2], None, ALU.is_lt))
                link(dve.tensor_tensor(nmask[:, t, :], nmask[:, t, :], mtmp[:, 0:48], ALU.mult))
                ins = dve.tensor_scalar(nmask[:, t, :], nmask[:, t, :], -1.0, BIG, ALU.add, ALU.mult)
                if t < NT - 1:
                    link(ins)
            ins.then_inc(dve_tab, 2)

            dve.wait_ge(act_cth, 1)
            link(dve.tensor_scalar(c_th[:], c_th[:], 1.0, 0.5, ALU.add, ALU.mult))
            link(dve.tensor_tensor(c_act[:], c_th[:], c_col[:], ALU.mult))

            def variance(n0, n1, done, v):
                dve.tensor_scalar(var[:, n0:n1], ss[:, n0:n1], 1.0 / D, EPS, ALU.mult, ALU.add).then_inc(done, 1)
                dve.wait_ge(done, v)

            def inverse_root(n0, n1, last):
                y = rs[:, n0:n1]
                link(dve.reciprocal(y, rt[:, n0:n1]))
                link(dve.tensor_tensor(rt[:, n0:n1], y, y, ALU.mult))
                link(dve.tensor_tensor(rt[:, n0:n1], rt[:, n0:n1], var[:, n0:n1], ALU.mult))
                link(dve.tensor_scalar(rt[:, n0:n1], rt[:, n0:n1], -0.5, 1.5, ALU.mult, ALU.add))
                ins = dve.tensor_tensor(y, y, rt[:, n0:n1], ALU.mult)
                if last is None:
                    link(ins)
                else:
                    ins.then_inc(last, 1)

            dve.wait_ge(act_ss, NT)
            variance(0, NT, dve_var, 1)
            dve.wait_ge(act_sd, 1)
            inverse_root(0, NT, dve_rs)

            def accumulate(j):
                k = j % KD
                if j < KD:
                    src = ada_first[k]
                    dve.wait_ge(s_ada0[k], 16)
                else:
                    r = j - KD
                    src = ada_ring[r % 2]
                    dve.wait_ge(s_adar[r % 2], 16 * (r // 2 + 1))
                if k == 0:
                    if j:
                        dve.wait_ge(pe_mod, j // KD)
                    dve.tensor_scalar(acc, src, c_act[:, 0:1], None, ALU.mult).then_inc(dve_ada, 1)
                else:
                    dve.wait_ge(dve_ada, j)
                    dve.scalar_tensor_tensor(out=acc, in0=src, scalar=c_act[:, k:k + 1], in1=acc, op0=ALU.mult,
                                             op1=ALU.add).then_inc(dve_ada, 1)

            for j in range(KD):
                accumulate(j)
            dve.wait_ge(s_small, 64)
            dve.wait_ge(pe_mod, 1)
            link(dve.tensor_tensor(modc[:, 0:2, :], ps_proj[0][:, 0:16].rearrange("p (s k) -> p s k", s=2),
                                   bada[:, 0:2, :], ALU.add))
            dve.scalar_tensor_tensor(out=a1[:], in0=modc[:, 1, :], scalar=1.0, in1=gmix[:], op0=ALU.add,
                                     op1=ALU.mult).then_inc(dve_mod, 1)
            dve.wait_ge(dve_mod, 1)
            for k in range(1, KD, 2):
                dve.wait_ge(pe_xT, k + 1)
                dve.tensor_scalar(hT[:, k, :], bank[XT_BANK[k]][:, :], a1[:, k:k + 1], modc[:, 0, k:k + 1],
                                  ALU.mult, ALU.add).then_inc(dve_hT, 1)

            def unit_out(u):
                dve.wait_ge(pe_unit, u + 1)
                if u >= QK_UNITS + VSTAGE:
                    dve.wait_ge(pe_vT, u - QK_UNITS - VSTAGE + 1)
                dst, of = unit_places(u)
                dve.tensor_copy(dst, of(ps_proj[1][:, :])).then_inc(dve_ev, 1)

            def v_out(f):
                dve.wait_ge(pe_vT, f + 1)
                dve.tensor_copy(vbuf[:, :, P * f:P * f + P],
                         bank[2 + f % 2][:, :].rearrange("p (n f) -> p n f", n=NT)).then_inc(dve_vout, 1)

            def residual_gate(row, b0, half):
                for i in range(2):
                    o = row[:, 512 * i:512 * i + 512]
                    link(dve.tensor_tensor(o, bank[b0 + i][:, :], o, ALU.add))
                    if half:
                        link(dve.tensor_scalar(o, o, 0.5, None, ALU.mult))

            j = KD
            for u in range(1, UNITS, 2):
                unit_out(u)
                if u >= QK_UNITS + 2:
                    v_out(u - QK_UNITS - 2)
                for _ in range(2):
                    if j < KD + ADA_CHUNKS:
                        accumulate(j)
                        j += 1
                if u == 9:
                    dve.wait_ge(pe_mod, 2)
                    dve.wait_ge(s_rows, 48)
                    residual_gate(gt1[:], 2, True)
                    dve.tensor_tensor(modc[:, 3, :], bank[4][:, 0:KD], bada[:, 3, :], ALU.add).then_inc(dve_mod, 1)
                if u == 17:
                    dve.wait_ge(pe_mod, 3)
                    residual_gate(gt2[:], 6, False)
                    link(dve.tensor_scalar(bg_half[:], bank[4][:, 16:32], 0.5, None, ALU.mult))
                    link(dve.tensor_tensor(modc[:, 4, :], bank[5][:, 0:KD], bada[:, 4, :], ALU.add))
                    dve.scalar_tensor_tensor(out=a2[:], in0=modc[:, 4, :], scalar=1.0, in1=gffn[:], op0=ALU.add,
                                             op1=ALU.mult).then_inc(dve_mod, 1)
                    dve.wait_ge(dve_mod, 3)

            v_out(V_UNITS - 1)

            def biased_scores(i):
                kind, g, h, t = JOBS[i]
                dve.wait_ge(pe_s, i + 1)
                dve.wait_ge(pool_bias, BIAS_OF[i] + 1)
                if i >= 2:
                    dve.wait_ge(act_exp, i - 1)
                bt = bias[BIAS_OF[i] % 3]
                pieces = []
                if kind == "group":
                    for q in range(NT):
                        pieces.append((slice(P * q, P * q + P), bt[:, 0:P], og[g][:, q, 256 + h:257 + h]))
                else:
                    w = P * len(NEAR[t])
                    if kind == "band":
                        o = P * (NEAR[t][0] - t + 1)
                        pieces.append((slice(0, w), bt[:, o:o + w], og[0][:, t, 256 + h:257 + h]))
                    else:
                        pieces.append((slice(0, w), bt[:, 0:w], nm_na[:, h, t:t + 1]))
                for w, b, nm in pieces:
                    ins = dve.tensor_tensor_reduce(out=sneg[i % 2][:, w], in0=ps_s[i % 2][:, w], in1=b,
                                                   scale=-SCALE, scalar=3e38, op0=ALU.add, op1=ALU.min,
                                                   accum_out=nm)
                ins.then_inc(dve_ttr, 1)

            def transposed_out(i):
                kind, g, h, t = JOBS[i]
                w = 512 if t is None else P * len(NEAR[t])
                dve.wait_ge(pe_t, i + 1)
                if i >= 2:
                    dve.wait_ge(pe_pv, i - 1)
                dve.tensor_copy(pT[i % 2][:, 0:w], ps_t[i % 2][:, 0:w]).then_inc(dve_pt, 1)

            def head_out(i):
                kind, g, h, t = JOBS[i]
                u = HEAD_OF[i]
                if t is not None and t != NT - 1:
                    return
                dve.wait_ge(pe_pv, i + 1)
                src = ps_o[u % 2][:, 0:NT * HD].rearrange("p (n d) -> p n d", n=NT)
                if kind == "na":
                    link(dve.reciprocal(rz_na[:, h, :], z_na[:, h, :]))
                    dve.tensor_tensor(o_na[:, :, HD * h:HD * h + HD], src,
                                      bview(rz_na[:, h, :], 0, [[1, NT], [0, HD]]), ALU.mult).then_inc(dve_o, 1)
                else:
                    dve.tensor_copy(og[g][:, :, HD * h:HD * h + HD], src).then_inc(dve_o, 1)

            dve.wait_ge(act_bt, 7)
            for i in range(NJ + 2):
                if i < NJ:
                    biased_scores(i)
                if 1 <= i <= NJ:
                    transposed_out(i - 1)
                if i >= 2:
                    head_out(i - 2)

            nm = [ogn[g][:, :, 256:260] for g in range(NG)]
            zz = [ogn[g][:, :, 260:264] for g in range(NG)]
            dve.wait_ge(s_ogn, 32)
            link(dve.tensor_tensor(lse[:, 3], nm[0], nm[1], ALU.min))
            link(dve.tensor_tensor(lse[:, 3], lse[:, 3], nm[2], ALU.min))
            for g in range(NG):
                dve.tensor_tensor(lse[:, 4 + g], lse[:, 3], nm[g], ALU.subtract).then_inc(dve_lse, 1)
            dve.wait_ge(act_lse, 1)
            link(dve.tensor_tensor(lse[:, 7], lse[:, 0], zz[0], ALU.mult))
            for g in (1, 2):
                link(dve.tensor_tensor(lse[:, 3 + g], lse[:, g], zz[g], ALU.mult))
                link(dve.tensor_tensor(lse[:, 7], lse[:, 7], lse[:, 3 + g], ALU.add))
            link(dve.reciprocal(lse[:, 7], lse[:, 7]))
            for g in range(NG):
                link(dve.tensor_tensor(lse[:, g], lse[:, g], lse[:, 7], ALU.mult))

            def weighted(dst, g):
                link(dve.tensor_tensor(dst.rearrange("p n (h d) -> p n h d", h=GH),
                                       ogn[g][:, :, 0:256].rearrange("p n (h d) -> p n h d", h=GH),
                                       bview(lse[:, g], 0, [[GH, NT], [1, GH], [0, HD]]), ALU.mult))

            weighted(prod[0], 0)
            weighted(prod[1], 1)
            link(dve.tensor_tensor(prod[0], prod[0], prod[1], ALU.add))
            weighted(prod[1], 2)
            dve.tensor_tensor(prod[0], prod[0], prod[1], ALU.add).then_inc(dve_ob, 1)
            for k in range(2):
                dve.wait_ge(pe_oT, 4 + k + 1)
                dve.tensor_copy(obT[:, k, :], bank[6 + k][:, :]).then_inc(dve_oT, 1)

            for m in range(KD):
                dve.wait_ge(pe_y, m + 1)
                dve.wait_ge(act_gate, GATE_UNITS)
                t1, t2 = ytmp[2 * (m % 2)], ytmp[2 * (m % 2) + 1]
                dve.scalar_tensor_tensor(out=t1, in0=gates[:, m, :], scalar=1.0, in1=ps_proj[m % 2][:, :],
                                         op0=ALU.add, op1=ALU.mult).then_inc(dve_m, 1)
                dve.scalar_tensor_tensor(out=t2, in0=gates[:, KD + m, :], scalar=1.0, in1=ps_s[m % 2][:, :],
                                         op0=ALU.add, op1=ALU.mult).then_inc(dve_m, 1)
                dve.wait_ge(dve_m, 3 * m + 2)
                dve.tensor_tensor(merged[:, m, :], t1, t2, ALU.add).then_inc(dve_m, 1)

            dve.wait_ge(s_xr, 16)
            for n in range(NT):
                for i in range(2):
                    u = 2 * n + i
                    dve.wait_ge(pe_wo, u + 1)
                    cut = slice(512 * i, 512 * i + 512)
                    ut = prod[0].rearrange("p n f -> p (n f)")[:, cut]
                    if u >= 2:
                        dve.wait_ge(dve_u, 2 * u - 2)
                    dve.tensor_tensor(ut, bank[4 + u % 4][:, :], gt1[:, cut], ALU.mult).then_inc(dve_u, 1)
                    dve.wait_ge(dve_u, 2 * u + 1)
                    dve.tensor_tensor(x2[:, n, cut], x2[:, n, cut], ut, ALU.add).then_inc(dve_u, 1)
                dve.wait_ge(act_ss, NT + n + 1)
                variance(n, n + 1, dve_var, 2 + n)
                dve.wait_ge(act_sd, 2 + n)
                inverse_root(n, n + 1, dve_rs)
            for k in range(1, KD, 2):
                dve.wait_ge(pe_h2, k + 1)
                dve.tensor_scalar(h2T[:, k, :], bank[k % 4][:, :], a2[:, k:k + 1], modc[:, 3, k:k + 1],
                                  ALU.mult, ALU.add).then_inc(dve_h2, 1)
            dve.wait_ge(s_xn, 16 * NT)
            for i in range(2):
                dve.memset(xg[i], 0.0).then_inc(dve_zx, 1)

            dve.wait_ge(act_rt, 1)
            dve.wait_ge(s_rows, 48)
            dve.wait_ge(pool_c, 15 + 4 * NT)
            link(dve.tensor_scalar(score, score, 1.0, None, ALU.add))
            link(dve.reciprocal(score, score))
            link(dve.tensor_tensor(biased, score, bview(ebias[:], 0, [[0, NT], [1, NE]]), ALU.add))
            b8 = biased.rearrange("p n (g e) -> p (n g) e", g=NGRP)
            for i in range(NT * NGRP):
                ins = dve.max(grp8[:, i, :], b8[:, i, :])
            link(ins)
            link(dve.tensor_tensor(grp[:].rearrange("p n g -> p (n g)"), grp8[:, :, 0], grp8[:, :, 1], ALU.add))
            other = bview(grp[:], 0, [[NGRP, NT], [0, NGRP], [1, NGRP]])
            own = bview(grp[:], 0, [[NGRP, NT], [1, NGRP], [0, NGRP]])
            link(dve.tensor_tensor(cmp, other, own, ALU.is_gt))
            link(dve.tensor_tensor(cmq, other, own, ALU.is_equal))
            link(dve.tensor_tensor(cmq, cmq, bview(before[:], 0, [[0, NT], [NGRP, NGRP], [1, NGRP]]),
                                   ALU.mult))
            link(dve.tensor_tensor(cmp, cmp, cmq, ALU.add))
            link(dve.tensor_reduce(gsel[:], cmp, AX.X, ALU.add))
            link(dve.tensor_scalar(gsel[:], gsel[:], TOPG - 0.5, None, ALU.is_lt))
            link(dve.tensor_scalar(gpen[:], gsel[:], -1.0, BIG, ALU.add, ALU.mult))
            spread = [[NGRP, NT], [1, NGRP], [0, NE // NGRP]]
            b4 = biased.rearrange("p n (g e) -> p n g e", g=NGRP)
            link(dve.tensor_tensor(b4, b4, bview(gsel[:], 0, spread), ALU.mult))
            link(dve.tensor_tensor(b4, b4, bview(gpen[:], 0, spread), ALU.add))
            for n in range(NT):
                ins = dve.max(top8[:, n, :], biased[:, n, :])
            link(ins)
            for n in range(NT):
                ins = dve.match_replace(wt[:, n, :], top8[:, n, :], biased[:, n, :], -3e38)
            link(ins)
            link(dve.tensor_scalar(sel, wt, -2e38, None, ALU.is_lt))
            dve.tensor_copy(selb, sel).then_inc(dve_sel, 1)
            link(dve.tensor_tensor(wt, score, sel, ALU.mult))
            link(dve.tensor_reduce(wsum[:], wt, AX.X, ALU.add))
            link(dve.reciprocal(wsum[:], wsum[:]))
            link(dve.tensor_scalar(wsum[:], wsum[:], ROUTED / 2, None, ALU.mult))
            link(dve.tensor_tensor(wt, wt, bview(wsum[:], 0, [[1, NT], [0, NE]]), ALU.mult))
            link(dve.tensor_copy(rhs9[:, :, :, 2, 0], wt))
            link(dve.tensor_tensor(wt, wt, rhs9[:, :, :, 2, 0], ALU.subtract))
            link(dve.tensor_copy(rhs9[:, :, :, 2, 1], wt))
            link(dve.tensor_tensor(wt, wt, rhs9[:, :, :, 2, 1], ALU.subtract))
            link(dve.tensor_copy(rhs9[:, :, :, 2, 2], wt))
            for n in range(NT):
                ins = dve.tensor_tensor_scan(kth[:, n, :], ones[:, 0:NE], sel[:, n, :], 0.0, ALU.mult, ALU.add)
            link(ins)
            link(dve.tensor_scalar(rhs9[:, :, :, 1, 2], kth, -1.0, None, ALU.add))
            dve.wait_ge(pe_rt, 2)
            link(dve.scalar_tensor_tensor(out=posm[:].rearrange("p n e -> p (n e)"), in0=bank[6][:, 0:NT * NE],
                                          scalar=1.0, in1=sel.rearrange("p n e -> p (n e)"), op0=ALU.add,
                                          op1=ALU.mult))
            dve.tensor_scalar(posm[:], posm[:], -1.0, None, ALU.add).then_inc(dve_tabs, 1)
            dve.wait_ge(dve_tabs, 1)

            def overflow():
                link(dve.tensor_copy(cnt_e[:], bank[7][0:NE, 256:257]))
                for b in range(3):
                    link(dve.tensor_scalar(ovf[:, b:b + 1], cnt_e[:], P * (b + 1) + 0.5, None, ALU.is_gt))
                    link(dve.memset(eval_[:, b + 1:b + 2], b + 1.0))
                link(dve.tensor_copy(eval_[:, 0:1], cl[0:NE, 0:1]))
                dve.tensor_copy(ovfb[:], ovf[:]).then_inc(dve_ovf, 1)

            def overflow_places():
                dve.wait_ge(pe_rt, 3)
                link(dve.tensor_copy(ovr[:], bank[7][0:NE, 260:263]))
                for b in range(3):
                    ins = dve.tensor_scalar(ov1h[:, b, :], slot_id[0:NE, 4, 0:32], ovr[:, b:b + 1], ovf[:, b:b + 1],
                                            ALU.is_equal, ALU.mult)
                ins.then_inc(dve_ovf, 1)

            def overflow_list():
                dve.wait_ge(pe_rt, 4)
                link(dve.tensor_copy(ovlist[0:1, 0:65], bank[7][0:1, 264:329]))
                link(dve.tensor_scalar(ovlist[0:1, 65:66], bank[7][0:1, 328:329], OVF - 1.0, None, ALU.add))
                pass_count = ovlist[0:1, 65:66].bitcast(I32)
                dve.tensor_single_scalar(pass_count, pass_count, OVF.bit_length() - 1,
                                         ALU.logical_shift_right).then_inc(dve_list, 1)
                dve.wait_ge(dve_list, 1)

            def shared_activations(m):
                dve.wait_ge(act_sh, m + 1)
                dve.wait_ge(pe_sh, 2 * m + 2)
                link(dve.scalar_tensor_tensor(out=sh_tmp[:, m, :], in0=sh_tmp[:, m, :], scalar=1.0,
                                              in1=bank[2 * m][:, :], op0=ALU.add, op1=ALU.mult))
                dve.tensor_tensor(sh_act[:, m, :], sh_tmp[:, m, :], bank[2 * m + 1][:, :],
                                  ALU.mult).then_inc(dve_sh, 1)

            def shared_out(u):
                dve.wait_ge(pe_sh, 4 + u + 1)
                dve.tensor_scalar(ysh[:, u // 2, 512:1024], bank[2 + u % 4][:, :], 0.5, None,
                                  ALU.mult).then_inc(dve_ysh, 1)

            def one_hot(n, k, e, b):
                if b is None:
                    if not isinstance(n, int) or n >= 2:
                        dve.wait_ge(pe_info, n - 1)
                    ids = bview(slot_id, 4 * P, [[0, NT], [1, P]])
                    place = bview(posm[:], e, [[NE, NT], [0, P]]) if isinstance(e, int) else \
                        posm[:, :, bass.ds(e, 1)].to_broadcast([P, NT, P])
                else:
                    ids = slot_id[:, bass.ds(b, 1), :].to_broadcast([P, NT, P])
                    place = posm[:, :, bass.ds(e, 1)].to_broadcast([P, NT, P])
                dve.tensor_tensor(onehot[k % 2], ids, place, ALU.is_equal).then_inc(dve_oh, 1)

            def of_expert(e, c):
                if isinstance(e, int):
                    return info[:, e, c]
                return info[:, bass.ds(e, 1), c].rearrange("p a b -> p (a b)")

            def indices(n, k, e, gathered):
                dve.wait_ge(pe_info, n + 1)
                dve.tensor_reduce(of_expert(e, slice(0, 3)), bank[6][:, 16 * (k % 2):16 * (k % 2) + 9]
                                  .rearrange("p (c a) -> p c a", a=3), AX.X, ALU.add).then_inc(dve_info, 1)
                dve.wait_ge(dve_info, n + 1)
                if gathered is not None:
                    dve.wait_ge(s_gather[k], gathered)
                dve.tensor_scalar(idx_t[:, k, :], of_expert(e, slice(0, 1)), 1024.0, None, ALU.add).then_inc(dve_idx, 1)

            def rows_out(n, b):
                dve.wait_ge(pe_ht, n + 1)
                for k in range(4, KD):
                    ins = dve.tensor_scalar(hTs[b][:, k, :], bank[1][:, P * (k - 4):P * (k - 3)], a2[:, k:k + 1],
                                            modc[:, 3, k:k + 1], ALU.mult, ALU.add)
                ins.then_inc(dve_ht, 1)

            def activations(n, b):
                dve.wait_ge(act_th, n + 1)
                dve.scalar_tensor_tensor(out=gth[b], in0=th[b], scalar=1.0, in1=bank[2 + b][:, 0:FE], op0=ALU.add,
                                         op1=ALU.mult).then_inc(dve_g, 1)
                dve.wait_ge(dve_g, n + 1)
                dve.tensor_tensor(act_t[b], gth[b], bank[2 + b][:, FE:2 * FE], ALU.mult).then_inc(dve_act, 1)

            def act_transposed(n, b):
                dve.wait_ge(pe_at, n + 1)
                dve.tensor_copy(aT[b], bank[7][:, 0:256].rearrange("p (k s) -> p k s", k=2)).then_inc(dve_at, 1)

            def y_out(n, k, e, scattered):
                dve.wait_ge(pe_dn, n + 1)
                if scattered is not None:
                    dve.wait_ge(s_scatter[k], scattered)
                dve.tensor_scalar(idx_r[:, k, :], of_expert(e, slice(1, 2)), 8192.0, None, ALU.add).then_inc(dve_idr, 1)
                dve.tensor_scalar(ysb[k][:, 512:1024], bank[5][:, :], of_expert(e, slice(2, 3)), None,
                                  ALU.mult).then_inc(dve_y, 1)

            def overflow_block(j):
                return (dve.value_load(ovlist[0:1, bass.ds(j, 1)], min_val=0, max_val=NE - 1),
                        dve.value_load(ovlist[0:1, bass.ds(j + 32, 1)], min_val=0, max_val=3))

            def body(e, k, i):
                ahead = not isinstance(e, int) or e + AHEAD < NE + OVF
                if isinstance(e, int) and NE - AHEAD <= e < NE + OVF - AHEAD:
                    j = e + AHEAD - NE
                    one_hot(e + AHEAD, k, dve.value_load(ovlist[0:1, j:j + 1], min_val=0, max_val=NE - 1),
                            dve.value_load(ovlist[0:1, 32 + j:33 + j], min_val=0, max_val=3))
                elif ahead:
                    one_hot(e + AHEAD, k, e + AHEAD, None)
                activations(e, k % 2)
                act_transposed(e, k % 2)
                if not isinstance(e, int) or e + 2 < NE + OVF:
                    rows_out(e + 2, k % 2)
                if ahead:
                    indices(e + AHEAD, k, e + AHEAD, 16 * i + 16)
                y_out(e, k, e, None if isinstance(e, int) and e < 4 else 16 * i)

            for e in range(2):
                one_hot(e, e, e, None)
            indices(0, 0, 0, None)
            shared_activations(0)
            for e in range(2, AHEAD):
                one_hot(e, e, e, None)
                indices(e - 1, e - 1, e - 1, None)
            indices(AHEAD - 1, AHEAD - 1, AHEAD - 1, None)
            shared_activations(1)
            for i in range(2, 4):
                dve.memset(xg[i], 0.0).then_inc(dve_zx, 1)
            rows_out(0, 0)
            overflow()
            shared_out(1)
            shared_out(3)
            overflow_places()
            rows_out(1, 1)
            shared_out(5)
            shared_out(7)
            overflow_list()
            for e in range(4):
                body(e, e, 0)
                if e == 0:
                    dve.wait_ge(act_ysh, NT)
                    dve.wait_ge(dve_ysh, NT)
                link(dve.tensor_tensor(ysh[:, e, :], ysh[:, e, :], gt2[:], ALU.mult))
                link(dve.tensor_tensor(x2[:, e, :], x2[:, e, :], ysh[:, e, :], ALU.add))
            with dve.Fori(1, NE // 4 - 1) as i:
                for k in range(4):
                    body(4 * i + k, k, i)
            for e in range(NE - 4, NE):
                body(e, e % 4, NE // 4 - 1)
            passes = dve.value_load(ovlist[0:1, 65:66], min_val=0, max_val=16)
            with dve.If(passes > 0):
                with dve.Fori(0, passes) as i:
                    ahead = [overflow_block(2 * i + 2 + k) for k in range(OVF)]
                    for k in range(OVF):
                        one_hot(NE + 2 * i + 2 + k, k, *ahead[k])
                    activations(NE + 2 * i, 0)
                    act_transposed(NE + 2 * i, 0)
                    activations(NE + 2 * i + 1, 1)
                    for k in range(OVF):
                        if k:
                            act_transposed(NE + 2 * i + k, k)
                        y_out(NE + 2 * i + k, k, NE + k, i * 16 + NE // 4 * 16)
                        dve.wait_ge(dve_y, NE + 2 * i + k + 1)
                        dve.wait_ge(act_y, NE + 2 * i + k + 1)
                        indices(NE + 2 * i + 2 + k, k, NE + k, i * 16 + (NE // 4 + 1) * 16)
                    for k in range(OVF):
                        rows_out(NE + 2 * i + 2 + k, k)

            for n in range(NT):
                f = fin[:, n, :]
                dve.wait_ge(s_pair[0][n % PBUF], 16 * (n // PBUF + 1))
                dve.tensor_reduce(f[:, 0:512], pairs[n % PBUF][:, :, 0:512].rearrange("p q d -> p d q"), AX.X,
                                  ALU.add).then_inc(dve_sum, 1)
                dve.wait_ge(dve_sum, 4 * n + 1)
                dve.tensor_tensor(f[:, 0:512], f[:, 0:512], gt2[:, 0:512], ALU.mult).then_inc(dve_sum, 1)
                dve.wait_ge(pe_sum, n + 1)
                dve.tensor_tensor(f[:, 512:1024], bank[4 + n % 2][:, :], gt2[:, 512:1024], ALU.mult).then_inc(dve_sum, 1)
                dve.wait_ge(dve_sum, 4 * n + 3)
                dve.tensor_tensor(f, f, x2[:, n, :], ALU.add).then_inc(dve_sum, 1)
                dve.wait_ge(act_fss, n + 1)
                variance(n, n + 1, dve_fv, n + 1)
                dve.wait_ge(act_fsd, n + 1)
                inverse_root(n, n + 1, None)
                dve.wait_ge(s_gfin, 16)
                dve.scalar_tensor_tensor(out=f, in0=f, scalar=rs[:, n:n + 1], in1=gfin[:], op0=ALU.mult,
                                         op1=ALU.mult).then_inc(dve_fin, 1)

        @block.tensor
        def _(pe):
            def bias_table():
                pe.wait_ge(s_btr, 16 * ROWS)
                for i in range(7):
                    w = min(512, BT - 512 * i)
                    if i == 0:
                        pe.wait_ge(act_hT, 4)
                        pe.wait_ge(dve_hT, 4)
                    if i == 6:
                        pe.wait_ge(act_bt, 1)
                    pe.matmul(bank[2 + i % 6][:, 0:w], flip[:], bt_rev[:, 512 * i:512 * i + w], start=True,
                              stop=True).then_inc(pe_bt, 1)

            pe.wait_ge(pool_c, 4)

            def x_transposes(k):
                for n in range(NT):
                    src = x_first[:, n, :].rearrange("p (f k) -> p k f", k=KD)[:, k, :]
                    mm = pe.transpose(bank[XT_BANK[k]][:, P * n:P * n + P], src, ident[:])
                mm.then_inc(pe_xT, 1)

            pe.wait_ge(act_xs, NT)
            for k in range(6):
                x_transposes(k)

            def column(dst, o):
                cols = acc[:, o:o + D].rearrange("p (f k) -> p k f", k=KD)
                for k in range(KD):
                    mm = pe.matmul(dst[:, k:k + 1], cols[:, k, :], ones[:, 0:1], start=True, stop=True)
                return mm

            pe.wait_ge(dve_one, 1)
            pe.wait_ge(dve_ada, KD)
            column(ps_proj[0][:, 0:8], 0)
            column(ps_proj[0][:, 8:16], D).then_inc(pe_mod, 1)
            x_transposes(6)
            pe.wait_ge(dve_mod, 1)
            x_transposes(7)

            def free_bank(u):
                if u < 2:
                    return
                if u - 2 >= UNITS:
                    pe.wait_ge(act_gate, u - 2 - UNITS + 1)
                elif u % 2:
                    pe.wait_ge(dve_ev, (u - 2) // 2 + 1)
                else:
                    pe.wait_ge(act_ev, (u - 2) // 2 + 1)

            def chunk(i):
                pe.wait_ge(s_w[i % WSLOTS], 16 * (i // WSLOTS + 1))

            pe.wait_ge(act_hT, 4)
            pe.wait_ge(dve_hT, 4)
            def v_transposes(f):
                u = QK_UNITS + f
                pe.wait_ge(dve_ev if u % 2 else act_ev, u // 2 + 1)
                if f >= 2:
                    pe.wait_ge(dve_vout if f % 2 else act_vout, (f - 2) // 2 + 1)
                for n in range(NT):
                    mm = pe.transpose(bank[2 + f % 2][:, P * n:P * n + P], vT[u % VSTAGE][:, P * n:P * n + P],
                                      ident[:])
                mm.then_inc(pe_vT, 1)

            for u in range(UNITS):
                if u % 2 == 0:
                    chunk(u // 2)
                free_bank(u)
                if u == 9:
                    pe.wait_ge(dve_ada, 2 * KD)
                    pe.wait_ge(act_bt, 7)
                    for i in range(2):
                        pe.matmul(bank[2 + i][:, :], ones[:], acc[:, 512 * i:512 * i + 512], start=True, stop=True)
                    column(bank[4][:, 0:8], D).then_inc(pe_mod, 1)
                if u == 17:
                    pe.wait_ge(dve_ada, 3 * KD)
                    pe.wait_ge(dve_mod, 2)
                    pe.wait_ge(s_bg, 16)
                    column(bank[5][:, 0:8], 0)
                    pe.transpose(bank[4][:, 16:32], bg_rows[:], ident[0:16, 0:16])
                    for k in range(2):
                        mm = pe.matmul(bank[6 + k][:, :], ones[:], acc[:, D + 512 * k:D + 512 * k + 512], start=True,
                                       stop=True)
                    mm.then_inc(pe_mod, 1)
                for k in range(KD):
                    mm = pe.matmul(ps_proj[u % 2][:, :], wbuf[u // 2 % WSLOTS][:, k, P * (u % 2):P * (u % 2) + P],
                                   hT[:, k, :], start=(k == 0), stop=(k == KD - 1))
                mm.then_inc(pe_unit, 1)
                if u == BT_UNIT:
                    bias_table()
                if u >= QK_UNITS + 1:
                    v_transposes(u - QK_UNITS - 1)
            v_transposes(V_UNITS - 1)
            gate_mm = [0]

            def gate_products(upto):
                while gate_mm[0] < upto:
                    m, k = gate_mm[0] // KD, gate_mm[0] % KD
                    i = N_QK + N_V + m // 2
                    if k == 0:
                        if m % 2 == 0:
                            chunk(i)
                        free_bank(UNITS + m)
                    mm = pe.matmul(ps_proj[m % 2][:, :], wbuf[i % WSLOTS][:, k, P * (m % 2):P * (m % 2) + P],
                                   hT[:, k, :], start=(k == 0), stop=(k == KD - 1))
                    if k == KD - 1:
                        mm.then_inc(pe_unit, 1)
                    gate_mm[0] += 1

            def heads(kind, g, h):
                if kind == "na":
                    return qkt[:, h // 2, :], qkt[:, 4 + h // 2, :], HD * (h % 2), HD * h
                n = g * GH + h
                return (qkt[:, 8 + n // 2, :], qkt[:, 14 + n // 2, :], HD * (n % 2), NAH * HD + HD * n)

            def scores(i):
                kind, g, h, t = JOBS[i]
                q, k, p0, _ = heads(kind, g, h)
                q, k = q[p0:p0 + HD, :], k[p0:p0 + HD, :]
                if i >= 2:
                    pe.wait_ge(dve_ttr, i - 1)
                dst = ps_s[i % 2]
                for q_tile in (range(NT) if t is None else [t]):
                    k0, w = (q_tile, 1) if t is None else (NEAR[t][0], len(NEAR[t]))
                    c0 = P * q_tile if t is None else 0
                    mm = pe.matmul(dst[:, c0:c0 + P * w], q[:, P * q_tile:P * q_tile + P],
                                   k[:, P * k0:P * (k0 + w)], start=True, stop=True)
                mm.then_inc(pe_s, 1)

            def transposes(i):
                kind, g, h, t = JOBS[i]
                pe.wait_ge(act_exp, i + 1)
                if i >= 2:
                    pe.wait_ge(dve_pt, i - 1)
                w = NT if t is None else len(NEAR[t])
                for j in range(w):
                    mm = pe.transpose(ps_t[i % 2][:, P * j:P * j + P], prob[i % 2][:, P * j:P * j + P], ident[:])
                mm.then_inc(pe_t, 1)

            def values(i):
                kind, g, h, t = JOBS[i]
                u = HEAD_OF[i]
                f = heads(kind, g, h)[3]
                pe.wait_ge(dve_pt, i + 1)
                if t in (None, 0) and u >= 2:
                    pe.wait_ge(dve_o, u - 1)
                for q in (range(NT) if t is None else [t]):
                    near = [q] if t is None else NEAR[t]
                    for j, kt in enumerate(near):
                        c0 = P * (q if t is None else j)
                        mm = pe.matmul(ps_o[u % 2][:, HD * q:HD * q + HD], pT[i % 2][:, c0:c0 + P],
                                       vbuf[:, kt, f:f + HD], start=(j == 0), stop=(j == len(near) - 1))
                mm.then_inc(pe_pv, 1)

            pe.wait_ge(act_vout, V_UNITS // 2)
            pe.wait_ge(dve_vout, V_UNITS // 2)
            pe.wait_ge(dve_mod, 3)
            for i in range(NJ + 2):
                if i < NJ:
                    scores(i)
                    gate_products(FILL * (i + 1))
                if 1 <= i <= NJ:
                    transposes(i - 1)
                if i >= 2:
                    values(i - 2)
            gate_products(KD * GATE_UNITS)

            pe.wait_ge(dve_o, N_HEADS)
            for k in range(4):
                for t in range(NT):
                    mm = pe.transpose(bank[2 + k][:, P * t:P * t + P], o_na[:, t, P * k:P * k + P], ident[:])
                mm.then_inc(pe_oT, 1)
            pe.wait_ge(dve_ob, 1)
            for k in range(2):
                for n in range(NT):
                    mm = pe.transpose(bank[6 + k][:, P * n:P * n + P], prod[0][:, n, P * k:P * k + P], ident[:])
                mm.then_inc(pe_oT, 1)
            pe.wait_ge(act_gate, GATE_UNITS)
            pe.wait_ge(act_oT, 4)
            pe.wait_ge(dve_oT, 2)
            pe.wait_ge(s_wp, 32)
            for m in range(KD):
                if m >= 2:
                    pe.wait_ge(dve_m, 3 * (m - 2) + 2)
                for k in range(4):
                    pe.matmul(ps_proj[m % 2][:, :], wpa[:, k, P * m:P * m + P], oaT[:, k, :], start=(k == 0),
                              stop=(k == 3))
                for k in range(2):
                    mm = pe.matmul(ps_s[m % 2][:, :], wpb[:, k, P * m:P * m + P], obT[:, k, :], start=(k == 0),
                                   stop=(k == 1))
                mm.then_inc(pe_y, 1)
            pe.wait_ge(dve_m, 3 * KD)
            pe.wait_ge(s_wo, 16)
            for u in range(2 * NT):
                n, i = u // 2, u % 2
                if u >= 4:
                    pe.wait_ge(dve_u, 2 * (u - 4) + 1)
                for k in range(KD):
                    mm = pe.matmul(bank[4 + u % 4][:, :], merged[:, k, P * n:P * n + P],
                                   wo[:, k, 512 * i:512 * i + 512], start=(k == 0), stop=(k == KD - 1))
                mm.then_inc(pe_wo, 1)
            pe.wait_ge(act_xs, 2 * NT)
            for k in range(KD):
                if k >= 4:
                    pe.wait_ge(dve_h2 if k % 2 else act_h2, (k - 4) // 2 + 1)
                for n in range(NT):
                    src = xs[:, n, :].rearrange("p (f k) -> p k f", k=KD)[:, k, :]
                    mm = pe.transpose(bank[k % 4][:, P * n:P * n + P], src, ident[:])
                mm.then_inc(pe_h2, 1)
            pe.wait_ge(act_h2, 4)
            pe.wait_ge(dve_h2, 4)
            pe.wait_ge(s_wr, 16)
            pe.wait_ge(dve_u, 4 * NT)
            for n in range(NT):
                for k in range(KD):
                    mm = pe.matmul(bank[7][:, NE * n:NE * n + NE], h2T[:, k, P * n:P * n + P], wr[:, k, :],
                                   start=(k == 0), stop=(k == KD - 1))
            mm.then_inc(pe_rt, 1)
            def shared_products(m, a, k0, k1):
                for k in range(k0, k1):
                    mm = pe.matmul(bank[2 * m + a][:, :], wgu[3][:, a, k, P * m:P * m + P], h2T[:, k, :],
                                   start=(k == 0), stop=(k == KD - 1))
                if k1 == KD:
                    mm.then_inc(pe_sh, 1)

            def shared_down(u):
                n, i = u // 2, u % 2
                if u >= 4:
                    pe.wait_ge(dve_ysh if u % 2 else act_ysh, (u - 4) // 2 + 1)
                for m in range(2):
                    mm = pe.matmul(bank[2 + u % 4][:, :], sh_act[:, m, P * n:P * n + P],
                                   wd[3][:, m, 512 * i:512 * i + 512], start=(m == 0), stop=(m == 1))
                mm.then_inc(pe_sh, 1)

            pe.wait_ge(s_wsh, 48)
            for a in range(2):
                shared_products(0, a, 0, KD)
            pe.wait_ge(dve_sel, 1)
            for n in range(NT):
                for m in range(n + 1):
                    mm = pe.matmul(bank[6][:, NE * n:NE * n + NE], tri[:] if m == n else onesb[:], selb[:, m, :],
                                   start=(m == 0), stop=(m == n))
            for n in range(NT):
                mm = pe.matmul(bank[7][0:NE, 256:257], selb[:, n, :], onesb[:, 0:1], start=(n == 0),
                               stop=(n == NT - 1))
            mm.then_inc(pe_rt, 1)

            def overflow_places():
                pe.wait_ge(dve_ovf, 1)
                pe.matmul(bank[7][0:NE, 260:263], tri[0:NE, 0:NE], ovfb[:], start=True, stop=False,
                          skip_group_check=True)
                pe.matmul(bank[7][0:NE, 261:263], onesb[0:NE, 0:NE], ovfb[:, 0:2], start=False, stop=False,
                          skip_group_check=True)
                pe.matmul(bank[7][0:NE, 262:263], onesb[0:NE, 0:NE], ovfb[:, 0:1], start=False, stop=True,
                          skip_group_check=True).then_inc(pe_rt, 1)

            def overflow_list():
                pe.wait_ge(dve_ovf, 2)
                for b in range(3):
                    pe.matmul(bank[7][0:1, 264:296], eval_[:, 0:1], ov1h[:, b, :], start=(b == 0), stop=(b == 2))
                for b in range(3):
                    pe.matmul(bank[7][0:1, 296:328], eval_[:, b + 1:b + 2], ov1h[:, b, :], start=(b == 0),
                              stop=(b == 2))
                for b in range(3):
                    mm = pe.matmul(bank[7][0:1, 328:329], ones[0:NE, 0:1], ovf[:, b:b + 1], start=(b == 0),
                                   stop=(b == 2))
                mm.then_inc(pe_rt, 1)

            def slots(n, k, e):
                pe.wait_ge(dve_oh, n + 1)
                if not isinstance(n, int) or n >= 1:
                    pe.wait_ge(dve_info, n)
                for t in range(NT):
                    rhs = rhs9[:, t, e, :, :] if isinstance(e, int) else rhs9[:, t, bass.ds(e, 1), :, :]
                    mm = pe.matmul(bank[6][:, 16 * (k % 2):16 * (k % 2) + 9], onehot[k % 2][:, t, :], rhs,
                                   start=(t == 0), stop=(t == NT - 1))
                mm.then_inc(pe_info, 1)

            def rows(n, b, gathered):
                pe.wait_ge(s_gather[b], gathered)
                if not isinstance(n, int) or n >= 1:
                    pe.wait_ge(act_ht, n)
                    pe.wait_ge(dve_ht, n)
                for k in range(KD):
                    src = xg[b].rearrange("p (f k) -> p k f", k=KD)[:, k, :]
                    mm = pe.transpose(bank[k // 4][:, P * (k % 4):P * (k % 4) + P], src, ident[:])
                mm.then_inc(pe_ht, 1)

            def gate_up(n, k, loaded):
                b = k % 2
                pe.wait_ge(act_ht, n + 1)
                pe.wait_ge(dve_ht, n + 1)
                pe.wait_ge(s_wgu[k], loaded)
                if not isinstance(n, int) or n >= 2:
                    pe.wait_ge(dve_act, n - 1)
                for j in range(KD):
                    mm = pe.matmul(bank[2 + b][:, :], hTs[b][:, j, :], wgu[k][:, :, j, :], start=(j == 0),
                                   stop=(j == KD - 1))
                mm.then_inc(pe_gu, 1)

            def act_transposes(n, b):
                pe.wait_ge(dve_act, n + 1)
                for j in range(2):
                    src = act_t[b].rearrange("p (f k) -> p k f", k=2)[:, j, :]
                    mm = pe.transpose(bank[7][:, P * j:P * j + P], src, ident[:])
                mm.then_inc(pe_at, 1)

            def down(n, k, loaded):
                pe.wait_ge(dve_at, n + 1)
                pe.wait_ge(s_wd[k], loaded)
                if not isinstance(n, int) or n >= 1:
                    pe.wait_ge(act_y, n)
                    pe.wait_ge(dve_y, n)
                for i in range(2):
                    for j in range(2):
                        mm = pe.matmul(bank[4 + i][:, :], aT[k % 2][:, j, :], wd[k][:, j, 512 * i:512 * i + 512],
                                       start=(j == 0), stop=(j == 1))
                mm.then_inc(pe_dn, 1)

            def body(e, k, i):
                if not isinstance(e, int) or e + 1 < NE:
                    gate_up(e + 1, (k + 1) % 4, 32 * (i + 1) if k < 3 else 32 * (i + 2))
                act_transposes(e, k % 2)
                if not isinstance(e, int) or e + 2 < NE + OVF:
                    rows(e + 2, (k + 2) % 4, 16 * i + 16 + 16 * (k // 2))
                if isinstance(e, int) and NE - AHEAD <= e < NE + OVF - AHEAD:
                    j = e + AHEAD - NE
                    slots(e + AHEAD, k, pe.value_load(ovlist[0:1, j:j + 1], min_val=0, max_val=NE - 1))
                elif not isinstance(e, int) or e + AHEAD < NE:
                    slots(e + AHEAD, k, e + AHEAD)
                down(e, k, 16 * (i + 1))

            shared_products(1, 0, 0, KD)
            pe.wait_ge(dve_tabs, 1)
            slots(0, 0, 0)
            shared_products(1, 1, 0, KD // 2)
            slots(1, 1, 1)
            shared_products(1, 1, KD // 2, KD)
            for e in range(2, AHEAD):
                slots(e, e, e)
            pe.wait_ge(dve_sh, 2)
            rows(0, 0, 16)
            shared_down(0)
            shared_down(1)
            overflow_places()
            shared_down(2)
            shared_down(3)
            rows(1, 1, 16)
            overflow_list()
            for u in range(4, 2 * NT):
                shared_down(u)
            pe.wait_ge(act_ysh, NT)
            pe.wait_ge(dve_ysh, NT)
            pe.wait_ge(dve_list, 1)
            gate_up(0, 0, 32)
            for e in range(4):
                body(e, e, 0)
            with pe.Fori(1, NE // 4 - 1) as i:
                for k in range(4):
                    body(4 * i + k, k, i)
            for e in range(NE - 4, NE):
                body(e, e % 4, NE // 4 - 1)
            passes = pe.value_load(ovlist[0:1, 65:66], min_val=0, max_val=16)
            with pe.If(passes > 0):
                with pe.Fori(0, passes) as i:
                    for k in range(OVF):
                        gate_up(NE + 2 * i + k, k, i * 32 + (NE // 4 + 1) * 32)
                    for k in range(OVF):
                        act_transposes(NE + 2 * i + k, k)
                        down(NE + 2 * i + k, k, i * 16 + (NE // 4 + 1) * 16)
                        slots(NE + 2 * i + 2 + k, k,
                              pe.value_load(ovlist[0:1, bass.ds(2 * i + 2 + k, 1)], min_val=0, max_val=NE - 1))
                    for k in range(OVF):
                        rows(NE + 2 * i + 2 + k, k, i * 16 + (NE // 4 + 2) * 16)
            for n in range(NT):
                pe.wait_ge(s_pair[1][n % PBUF], 16 * (n // PBUF + 1))
                if n >= 2:
                    pe.wait_ge(dve_sum, 4 * (n - 2) + 3)
                for q in range(TOPK):
                    mm = pe.matmul(bank[4 + n % 2][:, :], ident[:], pairs[n % PBUF][:, q, 512:1024], start=(q == 0),
                                   stop=(q == TOPK - 1))
                mm.then_inc(pe_sum, 1)


_INS = ["x", "c", "w_ada", "b_ada", "g_mix", "w_in", "b_gate", "rpb", "w_pa", "w_pb", "w_o", "g_ffn", "w_router",
        "e_bias", "we_gate", "we_up", "we_down", "ws_gate", "ws_up", "ws_down", "g_final"]


def kernel(**inputs):
    import numpy as np
    import concourse.bacc as bacc
    from concourse.bass_utils import run_bass_kernel_spmd

    nc = bacc.Bacc("TRN2", target_bir_lowering=False, num_devices=1)
    arrays, args = {}, []
    for name in _INS:
        a = np.ascontiguousarray(inputs[name])
        arrays[f"in_{name}"] = a
        args.append(nc.dram_tensor(f"in_{name}", a.shape, mybir.dt.from_np(a.dtype), kind="ExternalInput").ap())
    out = nc.dram_tensor("out_0", (1, S, D), F32, kind="ExternalOutput").ap()
    build(nc, *args, out)
    r = run_bass_kernel_spmd(nc, [arrays], core_ids=[0])
    return r.results[0]["out_0"]
```

```python
from contextlib import ExitStack

import concourse.bass as bass
from concourse import mybir

F32 = mybir.dt.float32
F32R = mybir.dt.float32r
BF16 = mybir.dt.bfloat16
I32 = mybir.dt.int32
U32 = mybir.dt.uint32
ALU = mybir.AluOpType
ACT = mybir.ActivationFunctionType
AX = mybir.AxisListType

P = 128
D = 1024
S = 512
NT = S // P
KD = D // P
HD = 64
GRID = 64
ROWS = S // GRID
NAH, WR, WC = 8, 8, 16
NG, GH = 3, 4
RADIUS = 64
DIL = (1, 4, 16)
NE, TOPK, NGRP, TOPG, FE = 64, 8, 8, 4, 256
ROUTED = 2.5
EPS = 1e-6
BIG = 1e30
SCALE = HD ** -0.5
SLOPES = [2.0 ** (-8.0 * (i + 1) / (NG * GH)) for i in range(NG * GH)]
RPBH = (2 * WR - 1) * (2 * WC - 1)
RPBW = 2 * WC - 1
BT = (NAH - 1) * RPBH + (ROWS - 1) * RPBW + 48
RPAD = WC
CW = 256

DIL0 = 3 * NAH * HD
GATE0 = DIL0 + 3 * NG * GH * HD
CHUNKS = ([0, 256, 512, 768] + [DIL0 + CW * i for i in range(6)] + [1024, 1280]
          + [DIL0 + 1536 + CW * i for i in range(3)] + [GATE0 + CW * i for i in range(8)])
N_QK, N_V, N_GATE = 10, 5, 8
QK_UNITS, V_UNITS, GATE_UNITS = 2 * N_QK, 2 * N_V, 2 * N_GATE
VSTAGE = 4
UNITS = QK_UNITS + V_UNITS
WSLOTS = 3
ADA_CHUNKS = 2 * KD

NEAR = [[0, 1], [0, 1, 2], [1, 2, 3], [2, 3]]


def jobs():
    out = [("group", g, h, None) for g in (2, 1) for h in range(GH)]
    out += [("band", 0, h, t) for h in range(GH) for t in range(NT)]
    out += [("na", 0, h, t) for h in range(NAH) for t in range(NT)]
    return out


JOBS = jobs()
HEAD_OF = []
BIAS_OF = []
_h = _b = -1
for _kind, _g, _hh, _t in JOBS:
    if _t in (None, 0):
        _h += 1
    if _kind != "band" or _t == 0:
        _b += 1
    HEAD_OF.append(_h)
    BIAS_OF.append(_b)
N_HEADS, N_BIAS = _h + 1, _b + 1


def filled(steps):
    groups = 2 * GH
    total = 3 * KD * GATE_UNITS
    first = FILL_GROUP * min(steps, groups)
    return min(total, first + -(-(total - FILL_GROUP * groups) * max(steps - groups, 0) // (len(JOBS) - groups - SPARE)))


LAST_BAND = max(i for i, job in enumerate(JOBS) if job[0] == "band")
COMBINE = 38


def last_of(table, value):
    return max(i for i, x in enumerate(table) if x == value)


A_QKT, A_V, A_HT, A_W, A_BT, A_JOB, A_GATE, A_LO = 0, 10240, 15360, 19456, 25600, 29120, 33344, 39488
A_ONA, A_GATE2, A_OG = 4096, 6144, 43584
A_END = 46784
B_WPA, B_WPB, B_OAT, B_OGN, B_TMP, B_WO, B_X = 0, 10240, 39488, 8192, 12288, 19456, 27648
SLOT = [0, 12288, 18432, 6144]
C_XS, C_H2T, C_YSH, C_WR = 33344, 37440, 41536, 45632
C_Y, C_OH, C_AT, C_ACT, C_XG, C_HTS = 24576, 26624, 27136, 31744, 33344, 35392
COLS = [4, 6, 8]
SH_BANK = [[3, 4], [0, 1]]
XT_BANK = [2, 3, 4, 5, 6, 7, 1, 0]
DIL_UNIT = 37
FILL_GROUP = 3
SPARE = 1
BT_UNIT = 4
PBUF = 3
OVF = 2
AHEAD = 4


def build(nc, x, c, w_ada, b_ada, g_mix, w_in, b_gate, rpb, w_pa, w_pb, w_o, g_ffn, w_router, e_bias,
          we_gate, we_up, we_down, ws_gate, ws_up, ws_down, g_final, out):
    rpb_pad = nc.dram_tensor("rpb_pad", [2 * RPAD + NAH * RPBH], F32, kind="Internal").ap()
    dil_dram = nc.dram_tensor("dil_dram", [2, S, 264], F32, kind="Internal").ap()
    xn_dram = nc.dram_tensor("xn_dram", [S, D], F32, kind="Internal").ap()
    pair_dram = nc.dram_tensor("pair_dram", [S * TOPK, D], F32, kind="Internal").ap()

    with ExitStack() as ctx:
        def sb(name, shape, dt=F32):
            return ctx.enter_context(nc.sbuf_tensor(name, shape, dt))

        def sem(name):
            return ctx.enter_context(nc.semaphore(name))

        arena_at = (nc.sbuf_base + 31) // 32 * 32
        arena = sb("arena", [P, A_END])

        def rounded(name, off, n):
            return nc.alloc_sbuf_tensor_at(name, [P, n], F32R, offset=arena_at + 4 * off)[:]

        def at(off, n):
            return arena[:, off:off + n]

        ada_first = [at(2048 * k, 2048) for k in range(8)]
        ada_ring = [at(A_V + 2048 * i, 2048) for i in range(2)]
        x_junk = [at(A_BT + 1024 * n if n < 3 else A_OG, 1024) for n in range(NT)]
        x_first = at(A_GATE + 2048, 4096).rearrange("p (n d) -> p n d", n=NT)
        acc = at(A_JOB, 2048)
        bt_rev = at(A_JOB + 2048, BT)
        qkt = at(A_QKT, 10240).rearrange("p (m t) -> p m t", m=20)
        vbuf = at(A_V, 5120).rearrange("p (n f) -> p n f", n=NT)
        h_hi = rounded("h_hi", A_HT, 4096).rearrange("p (k t) -> p k t", k=KD)
        h_full = at(A_LO, 4096).rearrange("p (k t) -> p k t", k=KD)
        h_lo = rounded("h_lo", A_LO, 4096).rearrange("p (k t) -> p k t", k=KD)
        vT = [at(A_GATE + 512 * i, 512) for i in range(VSTAGE)]
        w_full = [at(A_W + 2048 * i, 1024) for i in range(WSLOTS)]
        w_lo = [rounded(f"w_lo_{i}", A_W + 2048 * i, 1024) for i in range(WSLOTS)]
        w_hi = [rounded(f"w_hi_{i}", A_W + 2048 * i + 1024, 1024) for i in range(WSLOTS)]
        bt8 = at(A_BT, BT)
        bias = [at(A_JOB + 384 * i, 384) for i in range(3)]
        sneg = [at(A_JOB + 1152 + 512 * i, 512) for i in range(2)]
        prob = [at(A_JOB + 2176 + 512 * i, 512) for i in range(2)]
        pT = [at(A_JOB + 3200 + 512 * i, 512) for i in range(2)]
        gates = [at(A_GATE + 512 * m if m < 12 else A_GATE2 + 512 * (m - 12), 512) for m in range(16)]
        o_na = at(A_ONA, 2048).rearrange("p (n f) -> p n f", n=NT)
        og = [at(A_OG + 1056 * g, 1056).rearrange("p (n f) -> p n f", n=NT) for g in range(NG)]
        wpa = at(B_WPA, 4096).rearrange("p (k f) -> p k f", k=4)
        wpb = at(B_WPB, 2048).rearrange("p (k f) -> p k f", k=2)
        oaT = at(B_OAT, 2048).rearrange("p (k t) -> p k t", k=4)
        obT = at(B_OAT + 2048, 1024).rearrange("p (k t) -> p k t", k=2)
        ogn = [og[0][:, :, 0:256]] + [at(B_OGN + 1024 * i, 1024).rearrange("p (n f) -> p n f", n=NT) for i in range(2)]
        wo_tmp = at(B_TMP, 1024)
        merged = at(A_HT, 4096).rearrange("p (k t) -> p k t", k=KD)
        wo = at(B_WO, 8192).rearrange("p (k f) -> p k f", k=KD)
        x2 = at(B_X, 4096).rearrange("p (n d) -> p n d", n=NT)
        xs = at(C_XS, 4096).rearrange("p (n d) -> p n d", n=NT)
        ytmp = [at(B_TMP + 512 * i, 512) for i in range(4)]
        h2T = at(C_H2T, 4096).rearrange("p (k t) -> p k t", k=KD)
        ysh = at(C_YSH, 4096).rearrange("p (n d) -> p n d", n=NT)
        wgu = [at(SLOT[i], 4096).rearrange("p (a k f) -> p a k f", a=2, k=KD) for i in range(4)]
        wd = [at(SLOT[i] + 4096, 2048).rearrange("p (k f) -> p k f", k=2) for i in range(4)]
        sh_act = at(C_Y, 1024).rearrange("p (m t) -> p m t", m=2)
        sh_tmp = at(C_Y + 1024, 1024).rearrange("p (m t) -> p m t", m=2)
        ysb = [at((C_Y if i < 2 else C_H2T) + 1024 * i, 1024) for i in range(4)]
        onehot = [at(C_OH + 256 * i, 256).bitcast(BF16).rearrange("p (n s) -> p n s", n=NT) for i in range(2)]
        aT = [at(C_AT + 256 * i, 256).rearrange("p (k s) -> p k s", k=2) for i in range(2)]
        th = [at(C_ACT + 768 * i, 256) for i in range(2)]
        gth = [at(C_ACT + 768 * i + 256, 256) for i in range(2)]
        act_t = [at(C_ACT + 768 * i + 512, 256) for i in range(2)]
        xg = [at(C_XG + 1024 * i if i < 2 else C_H2T + 1024 * (i - 2), 1024) for i in range(4)]
        hTs = [at(C_HTS + 1024 * i, 1024).rearrange("p (k s) -> p k s", k=KD) for i in range(2)]
        pairs = [at(8192 * i, 8192).rearrange("p (q d) -> p q d", q=TOPK) for i in range(PBUF)]
        fin = at(C_XG, 4096).rearrange("p (n d) -> p n d", n=NT)

        gt1 = sb("gt1", [P, D])
        gt2 = sb("gt2", [P, D])
        gfin = gt1
        ident = sb("ident", [P, P])
        flip = sb("flip", [P, P])
        ones = sb("ones", [P, P])
        zero16 = sb("zero16", [1, RPAD])
        c_col = sb("c_col", [P, KD])
        c_th = sb("c_th", [P, KD])
        c_act = sb("c_act", [P, KD])
        bada = sb("bada", [P, 6, KD])
        gmix = sb("gmix", [P, KD])
        gffn = sb("gffn", [P, KD])
        modc = sb("modc", [P, 6, KD])
        a1 = sb("a1", [P, KD])
        a2 = sb("a2", [P, KD])
        bg_rows = sb("bg_rows", [16, P])
        bg_half = sb("bg_half", [P, 16])
        ss = sb("ss", [P, NT])
        rs = sb("rs", [P, NT])
        var = sb("var", [P, NT])
        rt = sb("rt", [P, NT])
        nm_na = sb("nm_na", [P, NAH, NT])
        z_na = sb("z_na", [P, NAH, NT])
        rz_na = sb("rz_na", [P, NAH, NT])
        part_i = sb("part_i", [P, 2], I32)
        cl = sb("cl", [P, 2])
        win = sb("win", [P, NT, 2])
        shared = sb("shared", [P, 1152])
        col_i = shared[:, 0:384].bitcast(I32)
        col_f = shared[:, 384:768]
        nmask = sb("nmask", [P, NT, 48])
        mtmp = shared[:, 768:1152]
        dist = [sb(f"dist{g}", [P, 384 if g == 0 else P]) for g in range(NG)]
        lse = sb("lse", [P, 8, NT, GH])
        nm_z = sb("nm_z", [P, 2, NT, 8])
        wr = at(C_WR, 512).rearrange("p (k e) -> p k e", k=KD)
        ebias = sb("ebias", [P, NE])
        score = at(C_ACT, 256).rearrange("p (n e) -> p n e", n=NT)
        biased = at(C_ACT + 256, 256).rearrange("p (n e) -> p n e", n=NT)
        grp8 = at(C_ACT + 512, 256).rearrange("p (n e) -> p n e", e=8)
        grp = sb("grp", [P, NT, NGRP])
        cmp = at(C_ACT + 768, 256).rearrange("p (n g h) -> p n g h", n=NT, g=NGRP)
        cmq = at(C_ACT + 1024, 256).rearrange("p (n g h) -> p n g h", n=NT, g=NGRP)
        before = sb("before", [P, NGRP, NGRP])
        gsel = sb("gsel", [P, NT, NGRP])
        gpen = sb("gpen", [P, NT, NGRP])
        top8 = sb("top8", [P, NT, 8])
        sel = at(C_OH, 256).rearrange("p (n e) -> p n e", n=NT)
        selb = at(C_AT, 128).bitcast(BF16).rearrange("p (n e) -> p n e", n=NT)
        wt = at(C_ACT + 1280, 256).rearrange("p (n e) -> p n e", n=NT)
        wsum = sb("wsum", [P, NT])
        kth = at(C_OH + 256, 256).rearrange("p (n e) -> p n e", n=NT)
        posm = sb("posm", [P, NT, NE])
        rhs9 = shared[:, :].bitcast(BF16).rearrange("p (n e c a) -> p n e c a", n=NT, e=NE, c=3)
        tri = sb("tri", [P, P], BF16)
        onesb = sb("onesb", [P, P], BF16)
        slot_id = at(C_WR + 512, 640).rearrange("p (b s) -> p b s", b=5)
        info = sb("info", [P, NE + OVF, 3])
        idx_t = sb("idx_t", [P, 4, 1], U32)
        idx_r = sb("idx_r", [P, 4, 1], U32)
        cnt_e = sb("cnt_e", [NE, 1])
        eval_ = sb("eval_", [NE, 4])
        ovf = sb("ovf", [NE, 3])
        ovfb = sb("ovfb", [NE, 3], BF16)
        ovr = sb("ovr", [NE, 3])
        ov1h = sb("ov1h", [NE, 3, 32])
        ovlist = sb("ovlist", [1, 96], U32)

        bank = [ctx.enter_context(nc.psum_tensor(f"bank{i}", [P, 512], F32)) for i in range(8)]
        ps_proj, ps_s, ps_t, ps_o = bank[0:2], bank[2:4], bank[4:6], bank[6:8]

        s_small = sem("s_small")
        s_rows = sem("s_rows")
        s_bg = sem("s_bg")
        s_x = sem("s_x")
        s_ada0 = [sem(f"s_ada0_{k}") for k in range(KD)]
        s_adar = [sem(f"s_adar_{k}") for k in range(2)]
        s_pad = sem("s_pad")
        s_btr = sem("s_btr")
        s_w = [sem(f"s_w_{i}") for i in range(WSLOTS)]
        s_dil = sem("s_dil")
        s_ogn = sem("s_ogn")
        s_wpa = [sem(f"s_wpa_{i}") for i in range(2)]
        s_wpb = sem("s_wpb")
        s_wo = sem("s_wo")
        s_xr = sem("s_xr")
        s_wsh = sem("s_wsh")
        s_wr = sem("s_wr")
        s_gfin = sem("s_gfin")
        s_wgu = [sem(f"s_wgu_{i}") for i in range(4)]
        s_wd = [sem(f"s_wd_{i}") for i in range(4)]
        s_xn = [sem(f"s_xn_{i}") for i in range(2)]
        s_gather = [sem(f"s_gather_{i}") for i in range(4)]
        s_scatter = [sem(f"s_scatter_{i}") for i in range(4)]
        s_pair = [[sem(f"s_pair_{i}_{j}") for j in range(PBUF)] for i in range(2)]
        s_out = sem("s_out")
        pool_c = sem("pool_c")
        sp_seq = sem("sp_seq")
        pool_seq = sem("pool_seq")
        pool_bias = sem("pool_bias")
        dve_c = sem("dve_c")
        act_c = sem("act_c")
        dve_one = sem("dve_one")
        dve_tab = sem("dve_tab")
        dve_ada = sem("dve_ada")
        dve_rs = sem("dve_rs")
        dve_var = sem("dve_var")
        act_ss = sem("act_ss")
        act_sd = sem("act_sd")
        act_cth = sem("act_cth")
        act_xs = sem("act_xs")
        dve_mod = sem("dve_mod")
        act_bt = sem("act_bt")
        pe_bt = sem("pe_bt")
        pe_col = sem("pe_col")
        pe_xT = sem("pe_xT")
        pool_hlo = sem("pool_hlo")
        dve_hfull = sem("dve_hfull")
        act_whi = sem("act_whi")
        pool_wlo = sem("pool_wlo")
        act_hT = sem("act_hT")
        dve_hT = sem("dve_hT")
        pe_unit = sem("pe_unit")
        act_ev = sem("act_ev")
        dve_ev = sem("dve_ev")
        act_gate = sem("act_gate")
        pe_vT = sem("pe_vT")
        act_vout = sem("act_vout")
        dve_vout = sem("dve_vout")
        pe_s = sem("pe_s")
        dve_ttr = sem("dve_ttr")
        act_exp = sem("act_exp")
        pe_t = sem("pe_t")
        dve_pt = sem("dve_pt")
        pe_pv = sem("pe_pv")
        dve_o = sem("dve_o")
        act_lse = sem("act_lse")
        dve_lse = sem("dve_lse")
        dve_ob = sem("dve_ob")
        pe_oT = sem("pe_oT")
        act_oT = sem("act_oT")
        dve_oT = sem("dve_oT")
        pe_y = sem("pe_y")
        dve_m = sem("dve_m")
        pe_wo = sem("pe_wo")
        dve_u = sem("dve_u")
        pe_h2 = sem("pe_h2")
        act_h2 = sem("act_h2")
        dve_h2 = sem("dve_h2")
        pe_rt = sem("pe_rt")
        act_rt = sem("act_rt")
        dve_sel = sem("dve_sel")
        dve_tabs = sem("dve_tabs")
        dve_ovf = sem("dve_ovf")
        dve_list = sem("dve_list")
        pe_sh = sem("pe_sh")
        act_sh = sem("act_sh")
        dve_sh = sem("dve_sh")
        act_ysh = sem("act_ysh")
        dve_ysh = sem("dve_ysh")
        dve_zx = sem("dve_zx")
        dve_oh = sem("dve_oh")
        pe_info = sem("pe_info")
        dve_info = sem("dve_info")
        dve_idx = sem("dve_idx")
        pe_ht = sem("pe_ht")
        act_ht = sem("act_ht")
        dve_ht = sem("dve_ht")
        pe_gu = sem("pe_gu")
        act_th = sem("act_th")
        dve_g = sem("dve_g")
        dve_act = sem("dve_act")
        pe_at = sem("pe_at")
        dve_at = sem("dve_at")
        pe_dn = sem("pe_dn")
        act_y = sem("act_y")
        dve_y = sem("dve_y")
        dve_idr = sem("dve_idr")
        dve_sum = sem("dve_sum")
        pe_sum = sem("pe_sum")
        act_fss = sem("act_fss")
        act_fsd = sem("act_fsd")
        dve_fv = sem("dve_fv")
        dve_fin = sem("dve_fin")

        block = ctx.enter_context(nc.Block())

        def bview(src, off, dims):
            return bass.AP(tensor=src.tensor, offset=src.offset + off, ap=[list(src.ap[0])] + dims)

        def unit_places(u):
            if u < QK_UNITS:
                dst = qkt[:, u, :]
                g = -1 if u < 8 else (u - 8) % 6 // 2
            else:
                dst = vT[u % VSTAGE]
                g = -1 if u < QK_UNITS + 4 else (u - QK_UNITS - 4) // 2
            if g < 0:
                return dst.rearrange("p (t r c) -> p r t c", t=NT, r=ROWS), \
                    (lambda a: a.rearrange("p (r t c) -> p r t c", t=NT, r=ROWS))
            if g == 0:
                return dst, lambda a: a
            return dst.rearrange("p (r u) -> p u r", r=DIL[g]), lambda a: a.rearrange("p (u r) -> p u r", r=DIL[g])

        def gates_by(step):
            return UNITS + filled(step + 3) // (3 * KD) + 1

        xt = x[0].rearrange("(n p) d -> p n d", p=P)
        NJ = len(JOBS)

        @block.sync
        def _(sp):
            def ada_src(part, k):
                return w_ada[0].rearrange("(p k) n -> p k n", k=KD)[:, k, 2048 * part:2048 * (part + 1)]

            sp.dma_start(c_col[:], c.rearrange("a (p k) -> (a p) k", k=KD)).then_inc(s_small, 16)
            sp.dma_start(bada[:], b_ada[0].rearrange("(s p k) -> p s k", s=6, k=KD)).then_inc(s_small, 16)
            sp.dma_start(gmix[:], g_mix[0].rearrange("(p k) -> p k", k=KD)).then_inc(s_small, 16)
            sp.dma_start(gffn[:], g_ffn[0].rearrange("(p k) -> p k", k=KD)).then_inc(s_small, 16)
            sp.dma_start(x_first, xt).then_inc(s_x, 16)
            for k in range(KD):
                sp.dma_start(ada_first[k], ada_src(0, k)).then_inc(s_ada0[k], 16)
            sp.dma_start(bg_rows[:], b_gate[0].rearrange("(m p) -> m p", p=P)).then_inc(s_bg, 16)

            def w_unit(u):
                if u >= WSLOTS:
                    sp.wait_ge(pe_unit, u - WSLOTS + 1)
                c0 = CHUNKS[u // 2] + P * (u % 2)
                sp.dma_start(w_full[u % WSLOTS].rearrange("p (k f) -> p k f", k=KD),
                             w_in[0].rearrange("(p k) n -> p k n", k=KD)[:, :, c0:c0 + P]).then_inc(s_w[u % WSLOTS], 16)

            def ada_chunk(j):
                if j != 1:
                    sp.wait_ge(dve_ada, KD if j == 0 else KD + j - 1)
                sp.dma_start(ada_ring[j % 2], ada_src(1 + j // KD, j % KD)).then_inc(s_adar[j % 2], 16)

            for u in range(WSLOTS):
                w_unit(u)
            ada_chunk(0)
            ada_chunk(1)
            sp.dma_start(gt1[:], b_ada[0, 2 * D:3 * D].partition_broadcast(P)).then_inc(s_rows, 16)
            sp.dma_start(gt2[:], b_ada[0, 5 * D:6 * D].partition_broadcast(P)).then_inc(s_rows, 16)
            sp.dma_start(ebias[:], e_bias[0].partition_broadcast(P)).then_inc(s_rows, 16)
            for u in range(WSLOTS, UNITS + GATE_UNITS):
                w_unit(u)
                if u == DIL_UNIT + 2:
                    sp.wait_ge(s_dil, 80)
                    sp.wait_ge(pe_pv, LAST_BAND + 1)
                    for i in range(2):
                        d = dil_dram[i].rearrange("(n p) f -> p n f", p=P)
                        sp.dma_start(ogn[1 + i], d[:, :, 0:256]).then_inc(s_ogn, 16)
                        sp.dma_start(nm_z[:, i], d[:, :, 256:264]).then_inc(s_ogn, 16)
                if 2 <= u - 2 < ADA_CHUNKS:
                    ada_chunk(u - 2)
                if u == DIL_UNIT:
                    sp.wait_ge(dve_o, 2 * GH)
                    sp.dma_start(dil_dram[0].rearrange("(p r) f -> p r f", r=4), og[1]).then_inc(s_dil, 16)
                    d2 = dil_dram[1].rearrange("(u t r) f -> r u t f", t=NT, r=4)
                    for r in range(4):
                        sp.dma_start(d2[r], og[2][32 * r:32 * r + 32, :, :]).then_inc(s_dil, 16)
            sp.wait_ge(pe_s, NJ)
            def w_pa_half(i):
                sp.dma_start(wpa[:, :, 512 * i:512 * i + 512], w_pa[0].rearrange("(k p) f -> p k f", p=P)
                             [:, :, 512 * i:512 * i + 512]).then_inc(s_wpa[i], 16)

            w_pa_half(0)
            sp.wait_ge(pe_pv, NJ)
            sp.dma_start(wpb, w_pb[0].rearrange("(k p) f -> p k f", p=P)).then_inc(s_wpb, 16)
            w_pa_half(1)
            sp.wait_ge(pe_unit, UNITS + GATE_UNITS)
            sp.dma_start(wo, w_o[0].rearrange("(k p) f -> p k f", p=P)).then_inc(s_wo, 16)
            sp.dma_start(x2, xt).then_inc(s_xr, 16)

            def matrix(w, e):
                return w[0, e] if isinstance(e, int) else w[0, bass.ds(e, 1)].rearrange("a d f -> (a d) f")

            def w_gate_up(e, k):
                for i, w in enumerate((we_gate, we_up)):
                    sp.dma_start(wgu[k][:, i], matrix(w, e).rearrange("(p k) f -> p k f", k=KD)).then_inc(s_wgu[k], 16)

            def w_down(e, k):
                sp.dma_start(wd[k], matrix(we_down, e).rearrange("(p k) f -> p k f", k=2)).then_inc(s_wd[k], 16)

            def w_expert(e, k, reused):
                if reused is not None:
                    sp.wait_ge(pe_gu, reused)
                w_gate_up(e, k)
                if reused is not None:
                    sp.wait_ge(pe_dn, reused)
                w_down(e, k)

            sp.wait_ge(dve_ob, 1)
            sp.dma_start(wr, w_router[0].rearrange("(p k) e -> p k e", k=KD)).then_inc(s_wr, 16)
            sp.wait_ge(pe_y, KD)
            sp.wait_ge(dve_m, 3 * KD)
            sp.dma_start(wgu[3][:, 0], ws_gate[0].rearrange("(p k) f -> p k f", k=KD)).then_inc(s_wsh, 16)
            sp.dma_start(wgu[3][:, 1], ws_up[0].rearrange("(p k) f -> p k f", k=KD)).then_inc(s_wsh, 16)
            sp.dma_start(wd[3], ws_down[0].rearrange("(k p) f -> p k f", p=P)).then_inc(s_wsh, 16)
            w_expert(0, 0, None)
            for n in range(NT):
                sp.wait_ge(act_xs, NT + n + 1)
                sp.dma_start(xn_dram[n * P:(n + 1) * P, :], xs[:, n, :]).then_inc(s_xn[n // 2], 16)
            sp.wait_ge(pe_wo, 2 * NT)
            sp.wait_ge(dve_u, 4 * NT)
            sp.dma_start(gfin[:], g_final.partition_broadcast(P)).then_inc(s_gfin, 16)
            w_expert(1, 1, None)
            w_expert(2, 2, None)
            sp.wait_ge(pe_sh, 4)
            w_gate_up(3, 3)
            sp.wait_ge(pe_sh, 4 + 2 * NT)
            w_down(3, 3)
            with sp.Fori(1, NE // 4) as i:
                for k in range(4):
                    w_expert(4 * i + k, k, 4 * i + k - 3)
            sp.wait_ge(dve_list, 1)
            for k in range(OVF):
                e = sp.value_load(ovlist[0:1, k:k + 1], min_val=0, max_val=NE - 1)
                w_expert(e, k, NE - 4 + k + 1)
            passes = sp.value_load(ovlist[0:1, 65:66], min_val=0, max_val=16)
            with sp.If(passes > 1):
                with sp.Fori(0, passes - 1) as i:
                    for k in range(OVF):
                        e = sp.value_load(ovlist[0:1, bass.ds(2 * i + 2 + k, 1)], min_val=0, max_val=NE - 1)
                        w_expert(e, k, NE + 2 * i + k + 1)
            for k in range(OVF):
                sp.wait_ge(s_scatter[k], passes * 16 + NE // 4 * 16)
                sp.sem_inc(sp_seq, 1)
                sp.wait_ge(s_wgu[k], (NE // 4 + 1) * 32)
                sp.wait_ge(s_wd[k], (NE // 4 + 1) * 16)
            for k in range(OVF, 4):
                sp.wait_ge(s_scatter[k], NE // 4 * 16)
            for n in range(NT):
                if n >= PBUF:
                    sp.wait_ge(pe_sum, n - PBUF + 1)
                    sp.wait_ge(dve_sum, 4 * (n - PBUF) + 1)
                src = pair_dram[n * P * TOPK:(n + 1) * P * TOPK, :].rearrange("(p q) d -> p q d", q=TOPK)
                for i in (1, 0):
                    sp.dma_start(pairs[n % PBUF][:, :, 512 * i:512 * i + 512],
                                 src[:, :, 512 * i:512 * i + 512]).then_inc(s_pair[i][n % PBUF], 16)
            for n in range(NT):
                sp.wait_ge(dve_fin, n + 1)
                sp.dma_start(out[0, n * P:(n + 1) * P, :], fin[:, n, :]).then_inc(s_out, 16)
            sp.wait_ge(s_out, 16 * NT)

        @block.gpsimd
        def _(pool):
            pool.memset(ident[:], 0.0).then_inc(pool_c, 1)
            pool.memset(flip[:], 0.0).then_inc(pool_c, 1)
            pool.wait_ge(pool_c, 2)
            pool.affine_select(out=ident[:], in_=ident[:], compare_op=ALU.not_equal, fill=1.0, base=0,
                               pattern=[[-1, P]], channel_multiplier=1).then_inc(pool_c, 1)
            pool.affine_select(out=flip[:], in_=flip[:], compare_op=ALU.not_equal, fill=1.0, base=1 - P,
                               pattern=[[1, P]], channel_multiplier=1).then_inc(pool_c, 1)
            pool.iota(part_i[:, 0:1], pattern=[[0, 1]], base=0, channel_multiplier=1).then_inc(pool_c, 1)
            pool.iota(col_i, pattern=[[1, 384]], base=0, channel_multiplier=0).then_inc(pool_c, 1)
            pool.memset(tri[:], 1.0).then_inc(pool_c, 1)
            pool.memset(before[:], 1.0).then_inc(pool_c, 1)
            pool.wait_ge(pool_c, 8)
            pool.affine_select(out=tri[:], in_=tri[:], compare_op=ALU.is_gt, fill=0.0, base=0,
                               pattern=[[1, P]], channel_multiplier=-1).then_inc(pool_c, 1)
            pool.affine_select(out=before[:], in_=before[:], compare_op=ALU.is_gt, fill=0.0, base=0,
                               pattern=[[1, NGRP], [-1, NGRP]], channel_multiplier=0).then_inc(pool_c, 1)
            pool.memset(onesb[:], 1.0).then_inc(pool_c, 1)

            def lo_part(lo, full, hi, ready, n, done):
                pool.wait_ge(ready, n)
                pool.tensor_tensor(lo, full, hi.bitcast(F32), ALU.subtract).then_inc(done, 1)

            for u in range(UNITS):
                if u == WSLOTS:
                    for k in range(0, KD, 2):
                        lo_part(h_lo[:, k, :], h_full[:, k, :], h_hi[:, k, :], act_hT, k // 2 + 1, pool_hlo)
                lo_part(w_lo[u % WSLOTS], w_full[u % WSLOTS], w_hi[u % WSLOTS], act_whi, u + 1, pool_wlo)
            lo_done = UNITS
            done = -1
            pool.wait_ge(dve_tab, 4)
            pool.wait_ge(act_bt, 7)
            pool.wait_ge(pe_col, COLS[2])
            for j, (kind, g, h, t) in enumerate(JOBS):
                while lo_done < min(gates_by(j), UNITS + GATE_UNITS):
                    lo_part(w_lo[lo_done % WSLOTS], w_full[lo_done % WSLOTS], w_hi[lo_done % WSLOTS], act_whi, lo_done + 1, pool_wlo)
                    lo_done += 1
                u = BIAS_OF[j]
                if u == done:
                    continue
                done = u
                if u >= 3:
                    pool.wait_ge(dve_ttr, last_of(BIAS_OF, u - 3) + 1)
                if kind == "na":
                    w = 16 * len(NEAR[t])
                    off = RPAD + 16 * NEAR[t][0] - 16 * t + h * RPBH
                    pool.tensor_tensor(bias[u % 3][:, 0:ROWS * w].rearrange("p (j r c) -> p j r c", r=ROWS, c=16),
                                       bview(bt8, off, [[16, w // 16], [RPBW, ROWS], [1, 16]]),
                                       bview(nmask[:, t, :], 0, [[16, w // 16], [0, ROWS], [1, 16]]),
                                       ALU.add).then_inc(pool_bias, 1)
                else:
                    w = 384 if kind == "band" else P
                    pool.tensor_scalar(bias[u % 3][:, 0:w], dist[g][:, 0:w], -SLOPES[g * GH + h] / SCALE, None,
                                       ALU.mult).then_inc(pool_bias, 1)

            while lo_done < UNITS + GATE_UNITS:
                lo_part(w_lo[lo_done % WSLOTS], w_full[lo_done % WSLOTS], w_hi[lo_done % WSLOTS], act_whi, lo_done + 1, pool_wlo)
                lo_done += 1
            pool.wait_ge(dve_ob, 1)
            pool.iota(slot_id[:, 0, :], pattern=[[1, P]], base=4 * P,
                      channel_multiplier=0, allow_small_or_imprecise_dtypes=True).then_inc(pool_c, 1)
            pool.iota(slot_id[:, 1:4, :].rearrange("p b s -> p (b s)"), pattern=[[1, 3 * P]], base=P,
                      channel_multiplier=0, allow_small_or_imprecise_dtypes=True).then_inc(pool_c, 1)
            pool.iota(slot_id[:, 4, :], pattern=[[1, P]], base=0,
                      channel_multiplier=0, allow_small_or_imprecise_dtypes=True).then_inc(pool_c, 1)
            pool.memset(rhs9[:, :, :, 0, 2], 0.0).then_inc(pool_c, 1)
            for n in range(NT):
                pool.iota(rhs9[:, n, :, 0, 0], pattern=[[0, NE]], base=0, channel_multiplier=1,
                          allow_small_or_imprecise_dtypes=True).then_inc(pool_c, 1)
                pool.iota(rhs9[:, n, :, 1, 0], pattern=[[0, NE]], base=0, channel_multiplier=TOPK,
                          allow_small_or_imprecise_dtypes=True).then_inc(pool_c, 1)
                pool.memset(rhs9[:, n, :, 0, 1], 128.0 * n - 1024.0).then_inc(pool_c, 1)
                pool.memset(rhs9[:, n, :, 1, 1], 1024.0 * n - 8192.0).then_inc(pool_c, 1)

            last_token, last_pair = pool.to_reg(S - 1), pool.to_reg(S * TOPK - 1)

            def gather(n, k):
                pool.wait_ge(dve_idx, n + 1)
                pool.sem_inc(pool_seq, 1)
                pool.indirect_dma_start(xg[k], None, xn_dram,
                                        bass.IndirectOffsetOnAxis(ap=idx_t[:, k, :], axis=0),
                                        bounds_check=last_token, oob_is_err=False).then_inc(s_gather[k], 16)

            def scatter(n, k):
                pool.wait_ge(act_y, n + 1)
                pool.wait_ge(dve_y, n + 1)
                pool.sem_inc(pool_seq, 1)
                pool.indirect_dma_start(pair_dram, bass.IndirectOffsetOnAxis(ap=idx_r[:, k, :], axis=0), ysb[k], None,
                                        bounds_check=last_pair, oob_is_err=False).then_inc(s_scatter[k], 16)

            def body(e, k):
                if not isinstance(e, int) or e + AHEAD < NE + OVF:
                    gather(e + AHEAD, k)
                scatter(e, k)

            for i in range(2):
                pool.wait_ge(s_xn[i], 32)
            for e in range(AHEAD):
                pool.wait_ge(dve_zx, e + 1)
                gather(e, e)
            for e in range(4):
                body(e, e)
            with pool.Fori(1, NE // 4 - 1) as i:
                for k in range(4):
                    body(4 * i + k, k)
            for e in range(NE - 4, NE):
                body(e, e % 4)
            passes = pool.value_load(ovlist[0:1, 65:66], min_val=0, max_val=16)
            with pool.If(passes > 1):
                with pool.Fori(0, passes - 1) as i:
                    for k in range(OVF):
                        scatter(NE + 2 * i + k, k)
                        gather(NE + 2 * i + 2 + k, k)
            with pool.If(passes > 0):
                for k in range(OVF):
                    scatter(NE + 2 * (passes - 1) + k, k)

        @block.scalar
        def _(act):
            act.wait_ge(dve_one, 2)
            act.dma_start(rpb_pad[0:RPAD], zero16[0, :]).then_inc(s_pad, 16)
            act.dma_start(rpb_pad[RPAD + NAH * RPBH:], zero16[0, :]).then_inc(s_pad, 16)
            act.dma_start(rpb_pad[RPAD:RPAD + NAH * RPBH], rpb[0].rearrange("h a b -> (h a b)")).then_inc(s_pad, 16)
            act.wait_ge(s_pad, 48)
            for r in range(ROWS):
                act.dma_start(bt_rev[16 * r:16 * r + 16, :],
                              bass.AP(tensor=rpb_pad.tensor, offset=rpb_pad.offset + RPBW * r,
                                      ap=[[1, 16], [1, BT]])).then_inc(s_btr, 16)
            act.wait_ge(s_small, 64)
            act.activation(c_th[:], c_col[:], ACT.Tanh, scale=0.5).then_inc(act_cth, 1)

            def sum_squares(src, junk, n, done):
                act.activation(junk, src, ACT.Square, accum_out=ss[:, n:n + 1]).then_inc(done, 1)

            act.wait_ge(s_x, 16)
            for n in range(NT):
                sum_squares(x_first[:, n, :], x_junk[n], n, act_ss)
            act.wait_ge(dve_var, 1)
            act.activation(rt[:], var[:], ACT.Sqrt).then_inc(act_sd, 1)
            act.wait_ge(dve_rs, 1)
            for n in range(NT):
                act.activation(x_first[:, n, :], x_first[:, n, :], ACT.Copy,
                               scale=rs[:, n:n + 1]).then_inc(act_xs, 1)

            def hi_part(u):
                act.wait_ge(s_w[u % WSLOTS], 16 * (u // WSLOTS + 1))
                act.copy(w_hi[u % WSLOTS], w_full[u % WSLOTS]).then_inc(act_whi, 1)

            for u in range(WSLOTS):
                hi_part(u)
            act.wait_ge(dve_mod, 1)
            for k in range(0, KD, 2):
                act.wait_ge(pe_xT, k + 1)
                act.activation(h_full[:, k, :], bank[XT_BANK[k]][:, :], ACT.Identity, bias=modc[:, 0, k:k + 1],
                               scale=a1[:, k:k + 1]).then_inc(act_c, 1)
                act.wait_ge(act_c, k // 2 + 1)
                act.copy(h_hi[:, k, :], h_full[:, k, :]).then_inc(act_hT, 1)

            def unit_out(u):
                act.wait_ge(pe_unit, u + 1)
                if u >= QK_UNITS + VSTAGE:
                    act.wait_ge(pe_vT, u - QK_UNITS - VSTAGE + 1)
                dst, of = unit_places(u)
                act.copy(dst, of(ps_proj[0][:, :])).then_inc(act_ev, 1)

            def v_out(f):
                act.wait_ge(pe_vT, f + 1)
                act.copy(vbuf[:, :, P * f:P * f + P],
                         bank[2 + f % 2][:, :].rearrange("p (n f) -> p n f", n=NT)).then_inc(act_vout, 1)

            for u in range(0, UNITS, 2):
                unit_out(u)
                if u == BT_UNIT:
                    for i in range(7):
                        act.wait_ge(pe_bt, i + 1)
                        w = min(512, BT - 512 * i)
                        act.activation(bt8[:, 512 * i:512 * i + w], bank[2 + i % 6][:, 0:w], ACT.Copy,
                                       scale=1.0 / SCALE).then_inc(act_bt, 1)
                if u >= QK_UNITS + 2:
                    v_out(u - QK_UNITS - 2)
                hi_part(u + WSLOTS)
                if u < UNITS - 2:
                    hi_part(u + WSLOTS + 1)
            v_out(V_UNITS - 2)

            def gate_out(m):
                act.wait_ge(pe_unit, UNITS + m + 1)
                if m == 0:
                    act.wait_ge(dve_mod, 3)
                act.activation(gates[m], ps_proj[m % 2][:, :], ACT.Tanh, bias=bg_half[:, m:m + 1],
                               scale=0.5).then_inc(act_gate, 1)

            gate, hi_done = 0, UNITS + 2
            for i, (kind, g, h, t) in enumerate(JOBS):
                while hi_done < min(gates_by(i), UNITS + GATE_UNITS):
                    hi_part(hi_done)
                    hi_done += 1
                act.wait_ge(dve_ttr, i + 1)
                if i >= 2:
                    act.wait_ge(pe_t, i - 1)
                if kind == "group":
                    for q in range(NT):
                        w = slice(P * q, P * q + P)
                        ins = act.activation(prob[i % 2][:, w], sneg[i % 2][:, w], ACT.Exp, scale=-1.0,
                                             bias=og[g][:, q, 256 + h:257 + h],
                                             accum_out=og[g][:, q, 260 + h:261 + h])
                else:
                    w = P * len(NEAR[t])
                    nm = og[0][:, t, 256 + h:257 + h] if kind == "band" else nm_na[:, h, t:t + 1]
                    z = og[0][:, t, 260 + h:261 + h] if kind == "band" else z_na[:, h, t:t + 1]
                    ins = act.activation(prob[i % 2][:, 0:w], sneg[i % 2][:, 0:w], ACT.Exp, scale=-1.0,
                                         bias=nm, accum_out=z)
                ins.then_inc(act_exp, 1)
                if i == COMBINE + 1:
                    act.wait_ge(dve_lse, NG)
                    act.activation(lse[:, 0:3], lse[:, 4:7], ACT.Exp).then_inc(act_lse, 1)
                while gate < GATE_UNITS - 2 and 3 * KD * (gate + 1) <= filled(i):
                    gate_out(gate)
                    gate += 1
            for u in range(hi_done, UNITS + GATE_UNITS):
                hi_part(u)
            while gate < GATE_UNITS:
                gate_out(gate)
                gate += 1
            for k in range(4):
                act.wait_ge(pe_oT, k + 1)
                src = bank[2 + k][:, :].rearrange("p (t r c) -> p t r c", t=NT, r=ROWS)
                dst = oaT[:, k, :].rearrange("p (r t c) -> p t r c", t=NT, r=ROWS)
                act.copy(dst, src).then_inc(act_oT, 1)
            def h2_out(n):
                act.wait_ge(pe_h2, n + 1)
                for k in range(4):
                    ins = act.activation(h2T[:, k, P * n:P * n + P], bank[0][:, P * k:P * k + P], ACT.Identity,
                                         bias=modc[:, 3, k:k + 1], scale=a2[:, k:k + 1])
                ins.then_inc(act_h2, 1)

            for n in range(NT):
                if n:
                    h2_out(n - 1)
                act.wait_ge(dve_u, 4 * n + 4)
                sum_squares(x2[:, n, :], xs[:, n, :], n, act_ss)
                act.wait_ge(dve_var, 2 + n)
                act.activation(rt[:, n:n + 1], var[:, n:n + 1], ACT.Sqrt).then_inc(act_sd, 1)
                act.wait_ge(dve_rs, 2 + n)
                act.wait_ge(act_ss, NT + n + 1)
                act.activation(xs[:, n, :], x2[:, n, :], ACT.Copy, scale=rs[:, n:n + 1]).then_inc(act_xs, 1)
            h2_out(NT - 1)
            act.wait_ge(pe_rt, 1)
            act.activation(score.rearrange("p n e -> p (n e)"), bank[2][:, 0:NT * NE], ACT.Exp,
                           scale=-1.0).then_inc(act_rt, 1)
            for m in range(2):
                act.wait_ge(pe_sh, 2 * m + 1)
                act.activation(sh_tmp[:, m, :], bank[SH_BANK[m][0]][:, :], ACT.Tanh, scale=0.5).then_inc(act_sh, 1)

            def shared_out(u):
                act.wait_ge(pe_sh, 4 + u + 1)
                act.activation(ysh[:, u // 2, 0:512], bank[2 + u % 4][:, :], ACT.Copy, scale=0.5).then_inc(act_ysh, 1)

            def rows_out(n, b):
                act.wait_ge(pe_ht, n + 1)
                for k in range(4):
                    ins = act.activation(hTs[b][:, k, :], bank[0][:, P * k:P * k + P], ACT.Identity,
                                         bias=modc[:, 3, k:k + 1], scale=a2[:, k:k + 1])
                ins.then_inc(act_ht, 1)

            def tanh(n, b):
                act.wait_ge(pe_gu, n + 1)
                act.activation(th[b], bank[2 + b][:, 0:FE], ACT.Tanh, scale=0.5).then_inc(act_th, 1)

            def y_out(n, k, e, scattered):
                act.wait_ge(pe_dn, n + 1)
                if scattered is not None:
                    act.wait_ge(s_scatter[k], scattered)
                w = info[:, e, 2:3] if isinstance(e, int) else info[:, bass.ds(e, 1), 2:3].rearrange("p a b -> p (a b)")
                act.activation(ysb[k][:, 0:512], bank[4][:, :], ACT.Copy, scale=w).then_inc(act_y, 1)

            def body(e, k, i):
                tanh(e, k % 2)
                if not isinstance(e, int) or e + 2 < NE + OVF:
                    rows_out(e + 2, k % 2)
                y_out(e, k, e, None if isinstance(e, int) and e < 4 else 16 * i)

            for b in range(2):
                rows_out(b, b)
                shared_out(4 * b)
                shared_out(4 * b + 2)
            for e in range(4):
                body(e, e, 0)
            with act.Fori(1, NE // 4 - 1) as i:
                for k in range(4):
                    body(4 * i + k, k, i)
            for e in range(NE - 4, NE):
                body(e, e % 4, NE // 4 - 1)
            def overflow_pass(i, more):
                for k in range(OVF):
                    tanh(NE + 2 * i + k, k)
                for k in range(OVF):
                    y_out(NE + 2 * i + k, k, NE + k, i * 16 + NE // 4 * 16)
                if more:
                    for k in range(OVF):
                        rows_out(NE + 2 * i + 2 + k, k)

            passes = act.value_load(ovlist[0:1, 65:66], min_val=0, max_val=16)
            with act.If(passes > 1):
                with act.Fori(0, passes - 1) as i:
                    overflow_pass(i, True)
            with act.If(passes > 0):
                overflow_pass(passes - 1, False)
            for n in range(NT):
                act.wait_ge(dve_sum, 4 * n + 4)
                act.activation(ysh[:, n, :], fin[:, n, :], ACT.Square, accum_out=ss[:, n:n + 1]).then_inc(act_fss, 1)
                act.wait_ge(dve_fv, n + 1)
                act.activation(rt[:, n:n + 1], var[:, n:n + 1], ACT.Sqrt).then_inc(act_fsd, 1)

        @block.vector
        def _(dve):
            steps = [0]

            def link(ins):
                steps[0] += 1
                ins.then_inc(dve_c, 1)
                dve.wait_ge(dve_c, steps[0])

            dve.memset(ones[:], 1.0).then_inc(dve_one, 1)
            dve.memset(zero16[:], 0.0).then_inc(dve_one, 1)

            dve.wait_ge(pool_c, 6)
            link(dve.tensor_copy(col_f, col_i))
            link(dve.tensor_copy(cl[:, 0:1], part_i[:, 0:1]))
            link(dve.tensor_scalar(mtmp, col_f, cl[:, 0:1], -float(P), ALU.subtract, ALU.add))
            link(dve.tensor_scalar(dist[0][:], mtmp, -1.0, None, ALU.mult))
            link(dve.tensor_tensor(dist[0][:], dist[0][:], mtmp, ALU.max))
            link(dve.tensor_scalar(mtmp, dist[0][:], RADIUS + 0.5, BIG, ALU.is_gt, ALU.mult))
            link(dve.tensor_scalar(dist[1][:], dist[0][:, P:2 * P], float(DIL[1]), None, ALU.mult))
            link(dve.tensor_tensor(dist[1][:], dist[1][:], mtmp[:, P:2 * P], ALU.add))
            link(dve.tensor_scalar(dist[2][:], dist[0][:, P:2 * P], float(DIL[2]), None, ALU.mult))
            dve.tensor_tensor(dist[0][:], dist[0][:], mtmp, ALU.add).then_inc(dve_tab, 1)
            link(dve.tensor_single_scalar(part_i[:, 1:2], part_i[:, 0:1], 5, ALU.logical_shift_right))
            link(dve.tensor_copy(cl[:, 1:2], part_i[:, 1:2]))
            link(dve.tensor_single_scalar(col_i[:, 0:P], col_i[:, 0:P], 5, ALU.logical_shift_right))
            link(dve.tensor_copy(mtmp[:, 0:P], col_i[:, 0:P]))
            link(dve.tensor_scalar(mtmp[:, 0:P], mtmp[:, 0:P], cl[:, 1:2], BIG, ALU.not_equal, ALU.mult))
            dve.tensor_tensor(dist[2][:], dist[2][:], mtmp[:, 0:P], ALU.add).then_inc(dve_tab, 1)
            link(dve.tensor_single_scalar(part_i[:, 1:2], part_i[:, 0:1], 15, ALU.bitwise_and))
            link(dve.tensor_copy(cl[:, 1:2], part_i[:, 1:2]))
            for t in range(NT):
                link(dve.tensor_scalar(win[:, t, 0:1], cl[:, 1:2], 16.0 * t - WC // 2, 0.0, ALU.add, ALU.max))
                link(dve.tensor_scalar(win[:, t, 0:1], win[:, t, 0:1], float(GRID - WC), -16.0 * NEAR[t][0],
                                       ALU.min, ALU.add))
                link(dve.tensor_scalar(win[:, t, 1:2], win[:, t, 0:1], float(WC), None, ALU.add))
                link(dve.tensor_scalar(nmask[:, t, :], col_f[:, 0:48], win[:, t, 0:1], None, ALU.is_ge))
                link(dve.tensor_scalar(mtmp[:, 0:48], col_f[:, 0:48], win[:, t, 1:2], None, ALU.is_lt))
                link(dve.tensor_tensor(nmask[:, t, :], nmask[:, t, :], mtmp[:, 0:48], ALU.mult))
                ins = dve.tensor_scalar(nmask[:, t, :], nmask[:, t, :], -1.0, BIG, ALU.add, ALU.mult)
                if t < NT - 1:
                    link(ins)
            ins.then_inc(dve_tab, 2)

            dve.wait_ge(act_cth, 1)
            link(dve.tensor_scalar(c_th[:], c_th[:], 1.0, 0.5, ALU.add, ALU.mult))
            link(dve.tensor_tensor(c_act[:], c_th[:], c_col[:], ALU.mult))

            def variance(n0, n1, done, v):
                dve.tensor_scalar(var[:, n0:n1], ss[:, n0:n1], 1.0 / D, EPS, ALU.mult, ALU.add).then_inc(done, 1)
                dve.wait_ge(done, v)

            def inverse_root(n0, n1, last):
                y = rs[:, n0:n1]
                link(dve.reciprocal(y, rt[:, n0:n1]))
                link(dve.tensor_tensor(rt[:, n0:n1], y, y, ALU.mult))
                link(dve.tensor_tensor(rt[:, n0:n1], rt[:, n0:n1], var[:, n0:n1], ALU.mult))
                link(dve.tensor_scalar(rt[:, n0:n1], rt[:, n0:n1], -0.5, 1.5, ALU.mult, ALU.add))
                ins = dve.tensor_tensor(y, y, rt[:, n0:n1], ALU.mult)
                if last is None:
                    link(ins)
                else:
                    ins.then_inc(last, 1)

            dve.wait_ge(act_ss, NT)
            variance(0, NT, dve_var, 1)
            dve.wait_ge(act_sd, 1)
            inverse_root(0, NT, dve_rs)

            def accumulate(j):
                k = j % KD
                if j < KD:
                    src = ada_first[k]
                    dve.wait_ge(s_ada0[k], 16)
                else:
                    r = j - KD
                    src = ada_ring[r % 2]
                    dve.wait_ge(s_adar[r % 2], 16 * (r // 2 + 1))
                if k == 0:
                    if j:
                        dve.wait_ge(pe_col, COLS[j // KD - 1])
                    dve.tensor_scalar(acc, src, c_act[:, 0:1], None, ALU.mult).then_inc(dve_ada, 1)
                else:
                    dve.wait_ge(dve_ada, j)
                    dve.scalar_tensor_tensor(out=acc, in0=src, scalar=c_act[:, k:k + 1], in1=acc, op0=ALU.mult,
                                             op1=ALU.add).then_inc(dve_ada, 1)

            for j in range(KD):
                accumulate(j)
            dve.wait_ge(s_small, 64)

            def column_sums(banks, s, done):
                for h in range(2):
                    dve.wait_ge(pe_col, done + h + 1)
                    link(dve.tensor_reduce(modc[:, s, 4 * h:4 * h + 4], banks[h][:, :].rearrange("p (k q) -> p k q", k=4),
                                           AX.X, ALU.add))

            column_sums(bank[0:2], 0, 0)
            column_sums(bank[6:8], 1, 2)
            link(dve.tensor_tensor(modc[:, 0:2, :], modc[:, 0:2, :], bada[:, 0:2, :], ALU.add))
            dve.scalar_tensor_tensor(out=a1[:], in0=modc[:, 1, :], scalar=1.0, in1=gmix[:], op0=ALU.add,
                                     op1=ALU.mult).then_inc(dve_mod, 1)
            dve.wait_ge(dve_mod, 1)
            for k in range(1, KD, 2):
                dve.wait_ge(pe_xT, k + 1)
                dve.tensor_scalar(h_full[:, k, :], bank[XT_BANK[k]][:, :], a1[:, k:k + 1], modc[:, 0, k:k + 1],
                                  ALU.mult, ALU.add).then_inc(dve_hfull, 1)
            for k in range(1, KD, 2):
                dve.wait_ge(dve_hfull, k // 2 + 1)
                link(dve.tensor_copy(h_hi[:, k, :], h_full[:, k, :]))
                dve.tensor_tensor(h_lo[:, k, :], h_full[:, k, :], h_hi[:, k, :].bitcast(F32),
                                  ALU.subtract).then_inc(dve_hT, 1)

            def unit_out(u):
                dve.wait_ge(pe_unit, u + 1)
                if u >= QK_UNITS + VSTAGE:
                    dve.wait_ge(pe_vT, u - QK_UNITS - VSTAGE + 1)
                dst, of = unit_places(u)
                dve.tensor_copy(dst, of(ps_proj[1][:, :])).then_inc(dve_ev, 1)

            def v_out(f):
                dve.wait_ge(pe_vT, f + 1)
                dve.tensor_copy(vbuf[:, :, P * f:P * f + P],
                         bank[2 + f % 2][:, :].rearrange("p (n f) -> p n f", n=NT)).then_inc(dve_vout, 1)

            def residual_gate(row, b0, half):
                for i in range(2):
                    o = row[:, 512 * i:512 * i + 512]
                    link(dve.tensor_tensor(o, bank[b0 + i][:, :], o, ALU.add))
                    if half:
                        link(dve.tensor_scalar(o, o, 0.5, None, ALU.mult))

            j = KD
            for u in range(1, UNITS, 2):
                unit_out(u)
                if u >= QK_UNITS + 2:
                    v_out(u - QK_UNITS - 2)
                for _ in range(2):
                    if j < KD + ADA_CHUNKS:
                        accumulate(j)
                        j += 1
                if u == 9:
                    dve.wait_ge(pe_col, COLS[1])
                    dve.wait_ge(s_rows, 48)
                    residual_gate(gt1[:], 2, True)
                    column_sums(bank[4:6], 3, COLS[0])
                    dve.tensor_tensor(modc[:, 3, :], modc[:, 3, :], bada[:, 3, :], ALU.add).then_inc(dve_mod, 1)
                if u == 17:
                    dve.wait_ge(pe_col, COLS[2])
                    residual_gate(gt2[:], 6, False)
                    link(dve.tensor_scalar(bg_half[:], bank[4][:, 16:32], 0.5, None, ALU.mult))
                    column_sums(bank[2:4], 4, COLS[1])
                    link(dve.tensor_tensor(modc[:, 4, :], modc[:, 4, :], bada[:, 4, :], ALU.add))
                    dve.scalar_tensor_tensor(out=a2[:], in0=modc[:, 4, :], scalar=1.0, in1=gffn[:], op0=ALU.add,
                                             op1=ALU.mult).then_inc(dve_mod, 1)
                    dve.wait_ge(dve_mod, 3)

            v_out(V_UNITS - 1)

            def biased_scores(i):
                kind, g, h, t = JOBS[i]
                dve.wait_ge(pe_s, i + 1)
                dve.wait_ge(pool_bias, BIAS_OF[i] + 1)
                if i >= 2:
                    dve.wait_ge(act_exp, i - 1)
                bt = bias[BIAS_OF[i] % 3]
                pieces = []
                if kind == "group":
                    for q in range(NT):
                        pieces.append((slice(P * q, P * q + P), bt[:, 0:P], og[g][:, q, 256 + h:257 + h]))
                else:
                    w = P * len(NEAR[t])
                    if kind == "band":
                        o = P * (NEAR[t][0] - t + 1)
                        pieces.append((slice(0, w), bt[:, o:o + w], og[0][:, t, 256 + h:257 + h]))
                    else:
                        pieces.append((slice(0, w), bt[:, 0:w], nm_na[:, h, t:t + 1]))
                for w, b, nm in pieces:
                    ins = dve.tensor_tensor_reduce(out=sneg[i % 2][:, w], in0=ps_s[i % 2][:, w], in1=b,
                                                   scale=-SCALE, scalar=3e38, op0=ALU.add, op1=ALU.min,
                                                   accum_out=nm)
                ins.then_inc(dve_ttr, 1)

            def transposed_out(i):
                kind, g, h, t = JOBS[i]
                w = 512 if t is None else P * len(NEAR[t])
                dve.wait_ge(pe_t, i + 1)
                if i >= 2:
                    dve.wait_ge(pe_pv, i - 1)
                dve.tensor_copy(pT[i % 2][:, 0:w], ps_t[i % 2][:, 0:w]).then_inc(dve_pt, 1)

            def head_out(i):
                kind, g, h, t = JOBS[i]
                u = HEAD_OF[i]
                if t is not None and t != NT - 1:
                    return
                dve.wait_ge(pe_pv, i + 1)
                src = ps_o[u % 2][:, 0:NT * HD].rearrange("p (n d) -> p n d", n=NT)
                if kind == "na":
                    link(dve.reciprocal(rz_na[:, h, :], z_na[:, h, :]))
                    dve.tensor_tensor(o_na[:, :, HD * h:HD * h + HD], src,
                                      bview(rz_na[:, h, :], 0, [[1, NT], [0, HD]]), ALU.mult).then_inc(dve_o, 1)
                else:
                    dve.tensor_copy(og[g][:, :, HD * h:HD * h + HD], src).then_inc(dve_o, 1)

            nm = [og[0][:, :, 256:260]] + [nm_z[:, i, :, 0:4] for i in range(2)]
            zz = [og[0][:, :, 260:264]] + [nm_z[:, i, :, 4:8] for i in range(2)]

            def weighted(g):
                o = ogn[g].rearrange("p n (h d) -> p n h d", h=GH)
                link(dve.tensor_tensor(o, o, bview(lse[:, g], 0, [[GH, NT], [1, GH], [0, HD]]), ALU.mult))

            def combine(piece):
                if piece == 0:
                    dve.wait_ge(s_ogn, 64)
                    link(dve.tensor_tensor(lse[:, 3], nm[0], nm[1], ALU.min))
                    link(dve.tensor_tensor(lse[:, 3], lse[:, 3], nm[2], ALU.min))
                    for g in range(NG):
                        dve.tensor_tensor(lse[:, 4 + g], lse[:, 3], nm[g], ALU.subtract).then_inc(dve_lse, 1)
                elif piece == 1:
                    dve.wait_ge(act_lse, 1)
                    link(dve.tensor_tensor(lse[:, 7], lse[:, 0], zz[0], ALU.mult))
                    for g in (1, 2):
                        link(dve.tensor_tensor(lse[:, 3 + g], lse[:, g], zz[g], ALU.mult))
                        link(dve.tensor_tensor(lse[:, 7], lse[:, 7], lse[:, 3 + g], ALU.add))
                    link(dve.reciprocal(lse[:, 7], lse[:, 7]))
                    for g in range(NG):
                        link(dve.tensor_tensor(lse[:, g], lse[:, g], lse[:, 7], ALU.mult))
                elif piece <= 4:
                    weighted(piece - 2)
                else:
                    ins = dve.tensor_tensor(ogn[0], ogn[0], ogn[piece - 4], ALU.add)
                    if piece == 6:
                        ins.then_inc(dve_ob, 1)
                    else:
                        link(ins)

            dve.wait_ge(act_bt, 7)
            for i in range(NJ + 2):
                if i < NJ:
                    biased_scores(i)
                if 1 <= i <= NJ:
                    transposed_out(i - 1)
                if i >= 2:
                    head_out(i - 2)
                if COMBINE <= i < COMBINE + 14 and (i - COMBINE) % 2 == 0:
                    combine((i - COMBINE) // 2)

            for k in range(2):
                dve.wait_ge(pe_oT, 4 + k + 1)
                dve.tensor_copy(obT[:, k, :], bank[6 + k][:, :]).then_inc(dve_oT, 1)

            for m in range(KD):
                dve.wait_ge(pe_y, m + 1)
                dve.wait_ge(act_gate, GATE_UNITS)
                t1, t2 = ytmp[2 * (m % 2)], ytmp[2 * (m % 2) + 1]
                dve.scalar_tensor_tensor(out=t1, in0=gates[m], scalar=1.0, in1=ps_proj[m % 2][:, :],
                                         op0=ALU.add, op1=ALU.mult).then_inc(dve_m, 1)
                dve.scalar_tensor_tensor(out=t2, in0=gates[KD + m], scalar=1.0, in1=ps_s[m % 2][:, :],
                                         op0=ALU.add, op1=ALU.mult).then_inc(dve_m, 1)
                dve.wait_ge(dve_m, 3 * m + 2)
                dve.tensor_tensor(merged[:, m, :], t1, t2, ALU.add).then_inc(dve_m, 1)

            dve.wait_ge(s_xr, 16)

            def h2_out(n):
                dve.wait_ge(pe_h2, n + 1)
                for k in range(4, KD):
                    ins = dve.tensor_scalar(h2T[:, k, P * n:P * n + P], bank[1][:, P * (k - 4):P * (k - 3)],
                                            a2[:, k:k + 1], modc[:, 3, k:k + 1], ALU.mult, ALU.add)
                ins.then_inc(dve_h2, 1)

            for n in range(NT):
                for i in range(2):
                    u = 2 * n + i
                    if n and i:
                        h2_out(n - 1)
                    dve.wait_ge(pe_wo, u + 1)
                    cut = slice(512 * i, 512 * i + 512)
                    ut = wo_tmp[:, cut]
                    if u >= 2:
                        dve.wait_ge(dve_u, 2 * u - 2)
                    dve.tensor_tensor(ut, bank[4 + u % 4][:, :], gt1[:, cut], ALU.mult).then_inc(dve_u, 1)
                    dve.wait_ge(dve_u, 2 * u + 1)
                    dve.tensor_tensor(x2[:, n, cut], x2[:, n, cut], ut, ALU.add).then_inc(dve_u, 1)
                dve.wait_ge(act_ss, NT + n + 1)
                variance(n, n + 1, dve_var, 2 + n)
                dve.wait_ge(act_sd, 2 + n)
                inverse_root(n, n + 1, dve_rs)
            h2_out(NT - 1)
            dve.wait_ge(s_xn[0], 32)
            for i in range(2):
                dve.memset(xg[i], 0.0).then_inc(dve_zx, 1)

            dve.wait_ge(act_rt, 1)
            dve.wait_ge(s_rows, 48)
            dve.wait_ge(pool_c, 15 + 4 * NT)
            link(dve.tensor_scalar(score, score, 1.0, None, ALU.add))
            link(dve.reciprocal(score, score))
            link(dve.tensor_tensor(biased, score, bview(ebias[:], 0, [[0, NT], [1, NE]]), ALU.add))
            b8 = biased.rearrange("p n (g e) -> p (n g) e", g=NGRP)
            for i in range(NT * NGRP):
                ins = dve.max(grp8[:, i, :], b8[:, i, :])
            link(ins)
            link(dve.tensor_tensor(grp[:].rearrange("p n g -> p (n g)"), grp8[:, :, 0], grp8[:, :, 1], ALU.add))
            other = bview(grp[:], 0, [[NGRP, NT], [0, NGRP], [1, NGRP]])
            own = bview(grp[:], 0, [[NGRP, NT], [1, NGRP], [0, NGRP]])
            link(dve.tensor_tensor(cmp, other, own, ALU.is_gt))
            link(dve.tensor_tensor(cmq, other, own, ALU.is_equal))
            link(dve.tensor_tensor(cmq, cmq, bview(before[:], 0, [[0, NT], [NGRP, NGRP], [1, NGRP]]),
                                   ALU.mult))
            link(dve.tensor_tensor(cmp, cmp, cmq, ALU.add))
            link(dve.tensor_reduce(gsel[:], cmp, AX.X, ALU.add))
            link(dve.tensor_scalar(gsel[:], gsel[:], TOPG - 0.5, None, ALU.is_lt))
            link(dve.tensor_scalar(gpen[:], gsel[:], -1.0, BIG, ALU.add, ALU.mult))
            spread = [[NGRP, NT], [1, NGRP], [0, NE // NGRP]]
            b4 = biased.rearrange("p n (g e) -> p n g e", g=NGRP)
            link(dve.tensor_tensor(b4, b4, bview(gsel[:], 0, spread), ALU.mult))
            link(dve.tensor_tensor(b4, b4, bview(gpen[:], 0, spread), ALU.add))
            for n in range(NT):
                ins = dve.max(top8[:, n, :], biased[:, n, :])
            link(ins)
            for n in range(NT):
                ins = dve.match_replace(wt[:, n, :], top8[:, n, :], biased[:, n, :], -3e38)
            link(ins)
            link(dve.tensor_scalar(sel, wt, -2e38, None, ALU.is_lt))
            dve.tensor_copy(selb, sel).then_inc(dve_sel, 1)
            link(dve.tensor_tensor(wt, score, sel, ALU.mult))
            link(dve.tensor_reduce(wsum[:], wt, AX.X, ALU.add))
            link(dve.reciprocal(wsum[:], wsum[:]))
            link(dve.tensor_scalar(wsum[:], wsum[:], ROUTED / 2, None, ALU.mult))
            link(dve.tensor_tensor(wt, wt, bview(wsum[:], 0, [[1, NT], [0, NE]]), ALU.mult))
            link(dve.tensor_copy(rhs9[:, :, :, 2, 0], wt))
            link(dve.tensor_tensor(wt, wt, rhs9[:, :, :, 2, 0], ALU.subtract))
            link(dve.tensor_copy(rhs9[:, :, :, 2, 1], wt))
            link(dve.tensor_tensor(wt, wt, rhs9[:, :, :, 2, 1], ALU.subtract))
            link(dve.tensor_copy(rhs9[:, :, :, 2, 2], wt))
            for n in range(NT):
                ins = dve.tensor_tensor_scan(kth[:, n, :], ones[:, 0:NE], sel[:, n, :], 0.0, ALU.mult, ALU.add)
            link(ins)
            link(dve.tensor_scalar(rhs9[:, :, :, 1, 2], kth, -1.0, None, ALU.add))
            dve.wait_ge(pe_rt, 2)
            link(dve.scalar_tensor_tensor(out=posm[:].rearrange("p n e -> p (n e)"), in0=bank[6][:, 0:NT * NE],
                                          scalar=1.0, in1=sel.rearrange("p n e -> p (n e)"), op0=ALU.add,
                                          op1=ALU.mult))
            dve.tensor_scalar(posm[:], posm[:], -1.0, None, ALU.add).then_inc(dve_tabs, 1)
            dve.wait_ge(dve_tabs, 1)

            def overflow():
                link(dve.tensor_copy(cnt_e[:], bank[7][0:NE, 256:257]))
                for b in range(3):
                    link(dve.tensor_scalar(ovf[:, b:b + 1], cnt_e[:], P * (b + 1) + 0.5, None, ALU.is_gt))
                    link(dve.memset(eval_[:, b + 1:b + 2], b + 1.0))
                link(dve.tensor_copy(eval_[:, 0:1], cl[0:NE, 0:1]))
                dve.tensor_copy(ovfb[:], ovf[:]).then_inc(dve_ovf, 1)

            def overflow_places():
                dve.wait_ge(pe_rt, 3)
                link(dve.tensor_copy(ovr[:], bank[7][0:NE, 260:263]))
                for b in range(3):
                    ins = dve.tensor_scalar(ov1h[:, b, :], slot_id[0:NE, 4, 0:32], ovr[:, b:b + 1], ovf[:, b:b + 1],
                                            ALU.is_equal, ALU.mult)
                ins.then_inc(dve_ovf, 1)

            def overflow_list():
                dve.wait_ge(pe_rt, 4)
                link(dve.tensor_copy(ovlist[0:1, 0:65], bank[7][0:1, 264:329]))
                link(dve.tensor_scalar(ovlist[0:1, 65:66], bank[7][0:1, 328:329], OVF - 1.0, None, ALU.add))
                pass_count = ovlist[0:1, 65:66].bitcast(I32)
                dve.tensor_single_scalar(pass_count, pass_count, OVF.bit_length() - 1,
                                         ALU.logical_shift_right).then_inc(dve_list, 1)
                dve.wait_ge(dve_list, 1)

            def shared_activations(m):
                dve.wait_ge(act_sh, m + 1)
                dve.wait_ge(pe_sh, 2 * m + 2)
                link(dve.scalar_tensor_tensor(out=sh_tmp[:, m, :], in0=sh_tmp[:, m, :], scalar=1.0,
                                              in1=bank[SH_BANK[m][0]][:, :], op0=ALU.add, op1=ALU.mult))
                dve.tensor_tensor(sh_act[:, m, :], sh_tmp[:, m, :], bank[SH_BANK[m][1]][:, :],
                                  ALU.mult).then_inc(dve_sh, 1)

            def shared_out(u):
                dve.wait_ge(pe_sh, 4 + u + 1)
                dve.tensor_scalar(ysh[:, u // 2, 512:1024], bank[2 + u % 4][:, :], 0.5, None,
                                  ALU.mult).then_inc(dve_ysh, 1)

            def one_hot(n, k, e, b):
                if b is None:
                    if not isinstance(n, int) or n >= 2:
                        dve.wait_ge(pe_info, n - 1)
                    ids = bview(slot_id, 4 * P, [[0, NT], [1, P]])
                    place = bview(posm[:], e, [[NE, NT], [0, P]]) if isinstance(e, int) else \
                        posm[:, :, bass.ds(e, 1)].to_broadcast([P, NT, P])
                else:
                    ids = slot_id[:, bass.ds(b, 1), :].to_broadcast([P, NT, P])
                    place = posm[:, :, bass.ds(e, 1)].to_broadcast([P, NT, P])
                dve.tensor_tensor(onehot[k % 2], ids, place, ALU.is_equal).then_inc(dve_oh, 1)

            def of_expert(e, c):
                if isinstance(e, int):
                    return info[:, e, c]
                return info[:, bass.ds(e, 1), c].rearrange("p a b -> p (a b)")

            def indices(n, k, e, gathered):
                dve.wait_ge(pe_info, n + 1)
                dve.tensor_reduce(of_expert(e, slice(0, 3)), bank[6][:, 16 * (k % 2):16 * (k % 2) + 9]
                                  .rearrange("p (c a) -> p c a", a=3), AX.X, ALU.add).then_inc(dve_info, 1)
                dve.wait_ge(dve_info, n + 1)
                if gathered is not None:
                    dve.wait_ge(s_gather[k], gathered)
                dve.tensor_scalar(idx_t[:, k, :], of_expert(e, slice(0, 1)), 1024.0, None, ALU.add).then_inc(dve_idx, 1)

            def rows_out(n, b):
                dve.wait_ge(pe_ht, n + 1)
                for k in range(4, KD):
                    ins = dve.tensor_scalar(hTs[b][:, k, :], bank[1][:, P * (k - 4):P * (k - 3)], a2[:, k:k + 1],
                                            modc[:, 3, k:k + 1], ALU.mult, ALU.add)
                ins.then_inc(dve_ht, 1)

            def activations(n, b):
                dve.wait_ge(act_th, n + 1)
                dve.scalar_tensor_tensor(out=gth[b], in0=th[b], scalar=1.0, in1=bank[2 + b][:, 0:FE], op0=ALU.add,
                                         op1=ALU.mult).then_inc(dve_g, 1)
                dve.wait_ge(dve_g, n + 1)
                dve.tensor_tensor(act_t[b], gth[b], bank[2 + b][:, FE:2 * FE], ALU.mult).then_inc(dve_act, 1)

            def act_transposed(n, b):
                dve.wait_ge(pe_at, n + 1)
                dve.tensor_copy(aT[b], bank[7][:, 0:256].rearrange("p (k s) -> p k s", k=2)).then_inc(dve_at, 1)

            def y_out(n, k, e, scattered):
                dve.wait_ge(pe_dn, n + 1)
                if scattered is not None:
                    dve.wait_ge(s_scatter[k], scattered)
                dve.tensor_scalar(idx_r[:, k, :], of_expert(e, slice(1, 2)), 8192.0, None, ALU.add).then_inc(dve_idr, 1)
                dve.tensor_scalar(ysb[k][:, 512:1024], bank[5][:, :], of_expert(e, slice(2, 3)), None,
                                  ALU.mult).then_inc(dve_y, 1)

            def overflow_block(j):
                return (dve.value_load(ovlist[0:1, bass.ds(j, 1)], min_val=0, max_val=NE - 1),
                        dve.value_load(ovlist[0:1, bass.ds(j + 32, 1)], min_val=0, max_val=3))

            def body(e, k, i):
                ahead = not isinstance(e, int) or e + AHEAD < NE + OVF
                if isinstance(e, int) and NE - AHEAD <= e < NE + OVF - AHEAD:
                    j = e + AHEAD - NE
                    one_hot(e + AHEAD, k, dve.value_load(ovlist[0:1, j:j + 1], min_val=0, max_val=NE - 1),
                            dve.value_load(ovlist[0:1, 32 + j:33 + j], min_val=0, max_val=3))
                elif ahead:
                    one_hot(e + AHEAD, k, e + AHEAD, None)
                activations(e, k % 2)
                act_transposed(e, k % 2)
                if not isinstance(e, int) or e + 2 < NE + OVF:
                    rows_out(e + 2, k % 2)
                if ahead:
                    indices(e + AHEAD, k, e + AHEAD, 16 * i + 16)
                y_out(e, k, e, None if isinstance(e, int) and e < 4 else 16 * i)

            for e in range(2):
                one_hot(e, e, e, None)
            indices(0, 0, 0, None)
            shared_activations(0)
            for e in range(2, AHEAD):
                one_hot(e, e, e, None)
                indices(e - 1, e - 1, e - 1, None)
            indices(AHEAD - 1, AHEAD - 1, AHEAD - 1, None)
            shared_activations(1)
            for i in range(2, 4):
                dve.memset(xg[i], 0.0).then_inc(dve_zx, 1)
            rows_out(0, 0)
            overflow()
            shared_out(1)
            shared_out(3)
            overflow_places()
            rows_out(1, 1)
            shared_out(5)
            shared_out(7)
            overflow_list()
            for e in range(4):
                body(e, e, 0)
                if e == 0:
                    dve.wait_ge(act_ysh, NT)
                    dve.wait_ge(dve_ysh, NT)
                link(dve.tensor_tensor(ysh[:, e, :], ysh[:, e, :], gt2[:], ALU.mult))
                link(dve.tensor_tensor(x2[:, e, :], x2[:, e, :], ysh[:, e, :], ALU.add))
            with dve.Fori(1, NE // 4 - 1) as i:
                for k in range(4):
                    body(4 * i + k, k, i)
            for e in range(NE - 4, NE):
                body(e, e % 4, NE // 4 - 1)
            def overflow_pass(i, more):
                if more:
                    ahead = [overflow_block(2 * i + 2 + k) for k in range(OVF)]
                    for k in range(OVF):
                        one_hot(NE + 2 * i + 2 + k, k, *ahead[k])
                activations(NE + 2 * i, 0)
                act_transposed(NE + 2 * i, 0)
                activations(NE + 2 * i + 1, 1)
                for k in range(OVF):
                    if k:
                        act_transposed(NE + 2 * i + k, k)
                    y_out(NE + 2 * i + k, k, NE + k, i * 16 + NE // 4 * 16)
                    if more:
                        dve.wait_ge(dve_y, NE + 2 * i + k + 1)
                        dve.wait_ge(act_y, NE + 2 * i + k + 1)
                        indices(NE + 2 * i + 2 + k, k, NE + k, i * 16 + (NE // 4 + 1) * 16)
                if more:
                    for k in range(OVF):
                        rows_out(NE + 2 * i + 2 + k, k)

            passes = dve.value_load(ovlist[0:1, 65:66], min_val=0, max_val=16)
            with dve.If(passes > 1):
                with dve.Fori(0, passes - 1) as i:
                    overflow_pass(i, True)
            with dve.If(passes > 0):
                overflow_pass(passes - 1, False)

            for n in range(NT):
                f = fin[:, n, :]
                dve.wait_ge(s_pair[0][n % PBUF], 16 * (n // PBUF + 1))
                dve.tensor_reduce(f[:, 0:512], pairs[n % PBUF][:, :, 0:512].rearrange("p q d -> p d q"), AX.X,
                                  ALU.add).then_inc(dve_sum, 1)
                dve.wait_ge(dve_sum, 4 * n + 1)
                dve.tensor_tensor(f[:, 0:512], f[:, 0:512], gt2[:, 0:512], ALU.mult).then_inc(dve_sum, 1)
                dve.wait_ge(pe_sum, n + 1)
                dve.tensor_tensor(f[:, 512:1024], bank[4 + n % 2][:, :], gt2[:, 512:1024], ALU.mult).then_inc(dve_sum, 1)
                dve.wait_ge(dve_sum, 4 * n + 3)
                dve.tensor_tensor(f, f, x2[:, n, :], ALU.add).then_inc(dve_sum, 1)
                dve.wait_ge(act_fss, n + 1)
                variance(n, n + 1, dve_fv, n + 1)
                dve.wait_ge(act_fsd, n + 1)
                inverse_root(n, n + 1, None)
                dve.wait_ge(s_gfin, 16)
                dve.scalar_tensor_tensor(out=f, in0=f, scalar=rs[:, n:n + 1], in1=gfin[:], op0=ALU.mult,
                                         op1=ALU.mult).then_inc(dve_fin, 1)

        @block.tensor
        def _(pe):
            def bias_table():
                pe.wait_ge(s_btr, 16 * ROWS)
                for i in range(7):
                    w = min(512, BT - 512 * i)
                    if i == 0:
                        pe.wait_ge(act_hT, 4)
                        pe.wait_ge(dve_hT, 4)
                    if i == 6:
                        pe.wait_ge(act_bt, 1)
                    pe.matmul(bank[2 + i % 6][:, 0:w], flip[:], bt_rev[:, 512 * i:512 * i + w], start=True,
                              stop=True).then_inc(pe_bt, 1)

            pe.wait_ge(pool_c, 4)

            def x_transposes(k):
                for n in range(NT):
                    src = x_first[:, n, :].rearrange("p (f k) -> p k f", k=KD)[:, k, :]
                    mm = pe.transpose(bank[XT_BANK[k]][:, P * n:P * n + P], src, ident[:])
                mm.then_inc(pe_xT, 1)

            pe.wait_ge(act_xs, NT)
            for k in range(4):
                x_transposes(k)

            def columns(banks, o):
                cols = acc[:, o:o + D].rearrange("p (f k) -> p k f", k=KD)
                for k in range(KD):
                    mm = pe.transpose(banks[k // 4][:, P * (k % 4):P * (k % 4) + P], cols[:, k, :], ident[:])
                    if k % 4 == 3:
                        mm.then_inc(pe_col, 1)

            pe.wait_ge(dve_one, 1)
            pe.wait_ge(dve_ada, KD)
            columns(bank[0:2], 0)
            columns(bank[6:8], D)
            pe.wait_ge(dve_mod, 1)
            for k in range(4, KD):
                x_transposes(k)

            def free_bank(u):
                if u < 2:
                    return
                if u - 2 >= UNITS:
                    pe.wait_ge(act_gate, u - 2 - UNITS + 1)
                elif u % 2:
                    pe.wait_ge(dve_ev, (u - 2) // 2 + 1)
                else:
                    pe.wait_ge(act_ev, (u - 2) // 2 + 1)

            def product(u, i):
                k = i // 3
                w, h = [(w_hi, h_hi), (w_hi, h_lo), (w_lo, h_hi)][i % 3]
                mm = pe.matmul(ps_proj[u % 2][:, :], w[u % WSLOTS][:, P * k:P * k + P],
                               h[:, k, :], start=(i == 0), stop=(i == 3 * KD - 1))
                if i == 3 * KD - 1:
                    mm.then_inc(pe_unit, 1)

            def v_transposes(f):
                u = QK_UNITS + f
                pe.wait_ge(dve_ev if u % 2 else act_ev, u // 2 + 1)
                if f >= 2:
                    pe.wait_ge(dve_vout if f % 2 else act_vout, (f - 2) // 2 + 1)
                for n in range(NT):
                    mm = pe.transpose(bank[2 + f % 2][:, P * n:P * n + P], vT[u % VSTAGE][:, P * n:P * n + P],
                                      ident[:])
                mm.then_inc(pe_vT, 1)

            for u in range(UNITS):
                pe.wait_ge(pool_wlo, u + 1)
                free_bank(u)
                if u == 9:
                    pe.wait_ge(dve_ada, 2 * KD)
                    pe.wait_ge(act_bt, 7)
                    for i in range(2):
                        pe.matmul(bank[2 + i][:, :], ones[:], acc[:, 512 * i:512 * i + 512], start=True, stop=True)
                    columns(bank[4:6], D)
                if u == 17:
                    pe.wait_ge(dve_ada, 3 * KD)
                    pe.wait_ge(dve_mod, 2)
                    pe.wait_ge(s_bg, 16)
                    pe.transpose(bank[4][:, 16:32], bg_rows[:], ident[0:16, 0:16])
                    for k in range(2):
                        pe.matmul(bank[6 + k][:, :], ones[:], acc[:, D + 512 * k:D + 512 * k + 512], start=True,
                                  stop=True)
                    columns(bank[2:4], 0)
                for i in range(3 * KD):
                    if u == 0 and i == 0:
                        pe.wait_ge(dve_hfull, 4)
                    if u == 0 and i % 3 == 0:
                        k = i // 3
                        pe.wait_ge(dve_hT if k % 2 else pool_hlo, k // 2 + 1)
                    product(u, i)
                if u == BT_UNIT:
                    bias_table()
                if u >= QK_UNITS + 1:
                    v_transposes(u - QK_UNITS - 1)
            v_transposes(V_UNITS - 1)
            gate_mm = [0]

            def gate_products(upto):
                while gate_mm[0] < min(upto, 3 * KD * GATE_UNITS):
                    m, i = gate_mm[0] // (3 * KD), gate_mm[0] % (3 * KD)
                    if i == 0:
                        pe.wait_ge(pool_wlo, UNITS + m + 1)
                        free_bank(UNITS + m)
                    product(UNITS + m, i)
                    gate_mm[0] += 1

            def heads(kind, g, h):
                if kind == "na":
                    return qkt[:, h // 2, :], qkt[:, 4 + h // 2, :], HD * (h % 2), HD * h
                n = g * GH + h
                return (qkt[:, 8 + n // 2, :], qkt[:, 14 + n // 2, :], HD * (n % 2), NAH * HD + HD * n)

            def scores(i):
                kind, g, h, t = JOBS[i]
                q, k, p0, _ = heads(kind, g, h)
                q, k = q[p0:p0 + HD, :], k[p0:p0 + HD, :]
                if i >= 2:
                    pe.wait_ge(dve_ttr, i - 1)
                dst = ps_s[i % 2]
                for q_tile in (range(NT) if t is None else [t]):
                    k0, w = (q_tile, 1) if t is None else (NEAR[t][0], len(NEAR[t]))
                    c0 = P * q_tile if t is None else 0
                    mm = pe.matmul(dst[:, c0:c0 + P * w], q[:, P * q_tile:P * q_tile + P],
                                   k[:, P * k0:P * (k0 + w)], start=True, stop=True)
                mm.then_inc(pe_s, 1)

            def transposes(i):
                kind, g, h, t = JOBS[i]
                pe.wait_ge(act_exp, i + 1)
                if i >= 2:
                    pe.wait_ge(dve_pt, i - 1)
                w = NT if t is None else len(NEAR[t])
                for j in range(w):
                    mm = pe.transpose(ps_t[i % 2][:, P * j:P * j + P], prob[i % 2][:, P * j:P * j + P], ident[:])
                mm.then_inc(pe_t, 1)

            def values(i):
                kind, g, h, t = JOBS[i]
                u = HEAD_OF[i]
                f = heads(kind, g, h)[3]
                pe.wait_ge(dve_pt, i + 1)
                if t in (None, 0) and u >= 2:
                    pe.wait_ge(dve_o, u - 1)
                for q in (range(NT) if t is None else [t]):
                    near = [q] if t is None else NEAR[t]
                    for j, kt in enumerate(near):
                        c0 = P * (q if t is None else j)
                        mm = pe.matmul(ps_o[u % 2][:, HD * q:HD * q + HD], pT[i % 2][:, c0:c0 + P],
                                       vbuf[:, kt, f:f + HD], start=(j == 0), stop=(j == len(near) - 1))
                mm.then_inc(pe_pv, 1)

            pe.wait_ge(act_vout, V_UNITS // 2)
            pe.wait_ge(dve_vout, V_UNITS // 2)
            pe.wait_ge(dve_mod, 3)
            for i in range(NJ + 2):
                if i < NJ:
                    scores(i)
                    gate_products(filled(i + 1))
                if 1 <= i <= NJ:
                    transposes(i - 1)
                if i >= 2:
                    values(i - 2)
            gate_products(3 * KD * GATE_UNITS)

            pe.wait_ge(dve_o, N_HEADS)
            for k in range(4):
                for t in range(NT):
                    mm = pe.transpose(bank[2 + k][:, P * t:P * t + P], o_na[:, t, P * k:P * k + P], ident[:])
                mm.then_inc(pe_oT, 1)
            pe.wait_ge(dve_ob, 1)
            for k in range(2):
                for n in range(NT):
                    mm = pe.transpose(bank[6 + k][:, P * n:P * n + P], ogn[0][:, n, P * k:P * k + P], ident[:])
                mm.then_inc(pe_oT, 1)
            pe.wait_ge(act_gate, GATE_UNITS)
            pe.wait_ge(act_oT, 4)
            pe.wait_ge(dve_oT, 2)
            pe.wait_ge(s_wpa[0], 16)
            pe.wait_ge(s_wpb, 16)
            for m in range(KD):
                if m == KD // 2:
                    pe.wait_ge(s_wpa[1], 16)
                if m >= 2:
                    pe.wait_ge(dve_m, 3 * (m - 2) + 2)
                for k in range(4):
                    pe.matmul(ps_proj[m % 2][:, :], wpa[:, k, P * m:P * m + P], oaT[:, k, :], start=(k == 0),
                              stop=(k == 3))
                for k in range(2):
                    mm = pe.matmul(ps_s[m % 2][:, :], wpb[:, k, P * m:P * m + P], obT[:, k, :], start=(k == 0),
                                   stop=(k == 1))
                mm.then_inc(pe_y, 1)
            pe.wait_ge(dve_m, 3 * KD)
            pe.wait_ge(s_wo, 16)
            def h2_transposes(n):
                pe.wait_ge(act_xs, NT + n + 1)
                if n:
                    pe.wait_ge(act_h2, n)
                    pe.wait_ge(dve_h2, n)
                for k in range(KD):
                    src = xs[:, n, :].rearrange("p (f k) -> p k f", k=KD)[:, k, :]
                    mm = pe.transpose(bank[k // 4][:, P * (k % 4):P * (k % 4) + P], src, ident[:])
                mm.then_inc(pe_h2, 1)

            def router(n):
                pe.wait_ge(act_h2, n + 1)
                pe.wait_ge(dve_h2, n + 1)
                if n == 0:
                    pe.wait_ge(s_wr, 16)
                for k in range(KD):
                    mm = pe.matmul(bank[2][:, NE * n:NE * n + NE], h2T[:, k, P * n:P * n + P], wr[:, k, :],
                                   start=(k == 0), stop=(k == KD - 1))
                if n == NT - 1:
                    mm.then_inc(pe_rt, 1)

            for u in range(2 * NT):
                n, i = u // 2, u % 2
                if u >= 4:
                    pe.wait_ge(dve_u, 2 * (u - 4) + 1)
                for k in range(KD):
                    mm = pe.matmul(bank[4 + u % 4][:, :], merged[:, k, P * n:P * n + P],
                                   wo[:, k, 512 * i:512 * i + 512], start=(k == 0), stop=(k == KD - 1))
                mm.then_inc(pe_wo, 1)
                if n and i == 0:
                    h2_transposes(n - 1)
                if n and i == 1:
                    router(n - 1)

            def shared_products(m, a, k0, k1, t0=0, t1=NT):
                for k in range(k0, k1):
                    mm = pe.matmul(bank[SH_BANK[m][a]][:, P * t0:P * t1], wgu[3][:, a, k, P * m:P * m + P],
                                   h2T[:, k, P * t0:P * t1], start=(k == 0), stop=(k == KD - 1))
                if k1 == KD and t1 == NT:
                    mm.then_inc(pe_sh, 1)

            pe.wait_ge(s_wsh, 48)
            shared_products(0, 0, 0, KD, 0, NT - 1)
            h2_transposes(NT - 1)
            router(NT - 1)
            def shared_down(u):
                n, i = u // 2, u % 2
                if u >= 4:
                    pe.wait_ge(dve_ysh if u % 2 else act_ysh, (u - 4) // 2 + 1)
                for m in range(2):
                    mm = pe.matmul(bank[2 + u % 4][:, :], sh_act[:, m, P * n:P * n + P],
                                   wd[3][:, m, 512 * i:512 * i + 512], start=(m == 0), stop=(m == 1))
                mm.then_inc(pe_sh, 1)

            shared_products(0, 0, 0, KD, NT - 1, NT)
            pe.wait_ge(dve_u, 4 * NT)
            shared_products(0, 1, 0, KD)
            pe.wait_ge(dve_sel, 1)
            for n in range(NT):
                for m in range(n + 1):
                    mm = pe.matmul(bank[6][:, NE * n:NE * n + NE], tri[:] if m == n else onesb[:], selb[:, m, :],
                                   start=(m == 0), stop=(m == n))
            for n in range(NT):
                mm = pe.matmul(bank[7][0:NE, 256:257], selb[:, n, :], onesb[:, 0:1], start=(n == 0),
                               stop=(n == NT - 1))
            mm.then_inc(pe_rt, 1)

            def overflow_places():
                pe.wait_ge(dve_ovf, 1)
                pe.matmul(bank[7][0:NE, 260:263], tri[0:NE, 0:NE], ovfb[:], start=True, stop=False,
                          skip_group_check=True)
                pe.matmul(bank[7][0:NE, 261:263], onesb[0:NE, 0:NE], ovfb[:, 0:2], start=False, stop=False,
                          skip_group_check=True)
                pe.matmul(bank[7][0:NE, 262:263], onesb[0:NE, 0:NE], ovfb[:, 0:1], start=False, stop=True,
                          skip_group_check=True).then_inc(pe_rt, 1)

            def overflow_list():
                pe.wait_ge(dve_ovf, 2)
                for b in range(3):
                    pe.matmul(bank[7][0:1, 264:296], eval_[:, 0:1], ov1h[:, b, :], start=(b == 0), stop=(b == 2))
                for b in range(3):
                    pe.matmul(bank[7][0:1, 296:328], eval_[:, b + 1:b + 2], ov1h[:, b, :], start=(b == 0),
                              stop=(b == 2))
                for b in range(3):
                    mm = pe.matmul(bank[7][0:1, 328:329], ones[0:NE, 0:1], ovf[:, b:b + 1], start=(b == 0),
                                   stop=(b == 2))
                mm.then_inc(pe_rt, 1)

            def slots(n, k, e):
                pe.wait_ge(dve_oh, n + 1)
                if not isinstance(n, int) or n >= 1:
                    pe.wait_ge(dve_info, n)
                for t in range(NT):
                    rhs = rhs9[:, t, e, :, :] if isinstance(e, int) else rhs9[:, t, bass.ds(e, 1), :, :]
                    mm = pe.matmul(bank[6][:, 16 * (k % 2):16 * (k % 2) + 9], onehot[k % 2][:, t, :], rhs,
                                   start=(t == 0), stop=(t == NT - 1))
                mm.then_inc(pe_info, 1)

            def rows(n, b, gathered):
                pe.wait_ge(s_gather[b], gathered)
                if not isinstance(n, int) or n >= 1:
                    pe.wait_ge(act_ht, n)
                    pe.wait_ge(dve_ht, n)
                for k in range(KD):
                    src = xg[b].rearrange("p (f k) -> p k f", k=KD)[:, k, :]
                    mm = pe.transpose(bank[k // 4][:, P * (k % 4):P * (k % 4) + P], src, ident[:])
                mm.then_inc(pe_ht, 1)

            def gate_up(n, k, loaded):
                b = k % 2
                pe.wait_ge(act_ht, n + 1)
                pe.wait_ge(dve_ht, n + 1)
                pe.wait_ge(s_wgu[k], loaded)
                if not isinstance(n, int) or n >= 2:
                    pe.wait_ge(dve_act, n - 1)
                for j in range(KD):
                    mm = pe.matmul(bank[2 + b][:, :], hTs[b][:, j, :], wgu[k][:, :, j, :], start=(j == 0),
                                   stop=(j == KD - 1))
                mm.then_inc(pe_gu, 1)

            def act_transposes(n, b):
                pe.wait_ge(dve_act, n + 1)
                for j in range(2):
                    src = act_t[b].rearrange("p (f k) -> p k f", k=2)[:, j, :]
                    mm = pe.transpose(bank[7][:, P * j:P * j + P], src, ident[:])
                mm.then_inc(pe_at, 1)

            def down(n, k, loaded):
                pe.wait_ge(dve_at, n + 1)
                pe.wait_ge(s_wd[k], loaded)
                if not isinstance(n, int) or n >= 1:
                    pe.wait_ge(act_y, n)
                    pe.wait_ge(dve_y, n)
                for i in range(2):
                    for j in range(2):
                        mm = pe.matmul(bank[4 + i][:, :], aT[k % 2][:, j, :], wd[k][:, j, 512 * i:512 * i + 512],
                                       start=(j == 0), stop=(j == 1))
                mm.then_inc(pe_dn, 1)

            def body(e, k, i):
                if not isinstance(e, int) or e + 1 < NE:
                    gate_up(e + 1, (k + 1) % 4, 32 * (i + 1) if k < 3 else 32 * (i + 2))
                act_transposes(e, k % 2)
                if not isinstance(e, int) or e + 2 < NE + OVF:
                    rows(e + 2, (k + 2) % 4, 16 * i + 16 + 16 * (k // 2))
                if isinstance(e, int) and NE - AHEAD <= e < NE + OVF - AHEAD:
                    j = e + AHEAD - NE
                    slots(e + AHEAD, k, pe.value_load(ovlist[0:1, j:j + 1], min_val=0, max_val=NE - 1))
                elif not isinstance(e, int) or e + AHEAD < NE:
                    slots(e + AHEAD, k, e + AHEAD)
                down(e, k, 16 * (i + 1))

            shared_products(1, 0, 0, KD)
            pe.wait_ge(dve_tabs, 1)
            slots(0, 0, 0)
            shared_products(1, 1, 0, KD // 2)
            slots(1, 1, 1)
            shared_products(1, 1, KD // 2, KD)
            for e in range(2, AHEAD):
                slots(e, e, e)
            pe.wait_ge(dve_sh, 2)
            rows(0, 0, 16)
            shared_down(0)
            shared_down(1)
            overflow_places()
            shared_down(2)
            shared_down(3)
            rows(1, 1, 16)
            overflow_list()
            for u in range(4, 2 * NT):
                shared_down(u)
            pe.wait_ge(act_ysh, NT)
            pe.wait_ge(dve_ysh, NT)
            pe.wait_ge(dve_list, 1)
            gate_up(0, 0, 32)
            for e in range(4):
                body(e, e, 0)
            with pe.Fori(1, NE // 4 - 1) as i:
                for k in range(4):
                    body(4 * i + k, k, i)
            for e in range(NE - 4, NE):
                body(e, e % 4, NE // 4 - 1)
            def overflow_pass(i, more):
                for k in range(OVF):
                    gate_up(NE + 2 * i + k, k, i * 32 + (NE // 4 + 1) * 32)
                for k in range(OVF):
                    act_transposes(NE + 2 * i + k, k)
                    down(NE + 2 * i + k, k, i * 16 + (NE // 4 + 1) * 16)
                    if more:
                        slots(NE + 2 * i + 2 + k, k,
                              pe.value_load(ovlist[0:1, bass.ds(2 * i + 2 + k, 1)], min_val=0, max_val=NE - 1))
                if more:
                    for k in range(OVF):
                        rows(NE + 2 * i + 2 + k, k, i * 16 + (NE // 4 + 2) * 16)

            passes = pe.value_load(ovlist[0:1, 65:66], min_val=0, max_val=16)
            with pe.If(passes > 1):
                with pe.Fori(0, passes - 1) as i:
                    overflow_pass(i, True)
            with pe.If(passes > 0):
                overflow_pass(passes - 1, False)
            for n in range(NT):
                pe.wait_ge(s_pair[1][n % PBUF], 16 * (n // PBUF + 1))
                if n >= 2:
                    pe.wait_ge(dve_sum, 4 * (n - 2) + 3)
                for q in range(TOPK):
                    mm = pe.matmul(bank[4 + n % 2][:, :], ident[:], pairs[n % PBUF][:, q, 512:1024], start=(q == 0),
                                   stop=(q == TOPK - 1))
                mm.then_inc(pe_sum, 1)


_INS = ["x", "c", "w_ada", "b_ada", "g_mix", "w_in", "b_gate", "rpb", "w_pa", "w_pb", "w_o", "g_ffn", "w_router",
        "e_bias", "we_gate", "we_up", "we_down", "ws_gate", "ws_up", "ws_down", "g_final"]


def kernel(**inputs):
    import numpy as np
    import concourse.bacc as bacc
    from concourse.bass_utils import run_bass_kernel_spmd

    nc = bacc.Bacc("TRN2", target_bir_lowering=False, num_devices=1)
    arrays, args = {}, []
    for name in _INS:
        a = np.ascontiguousarray(inputs[name])
        arrays[f"in_{name}"] = a
        args.append(nc.dram_tensor(f"in_{name}", a.shape, mybir.dt.from_np(a.dtype), kind="ExternalInput").ap())
    out = nc.dram_tensor("out_0", (1, S, D), F32, kind="ExternalOutput").ap()
    build(nc, *args, out)
    r = run_bass_kernel_spmd(nc, [arrays], core_ids=[0])
    return r.results[0]["out_0"]
```
